# Optimizing a Trainium2 kernel written in Bass

```python
import math
import jax, jax.numpy as jnp
from jax import lax
import numpy as np

D_MODEL = 1024
BATCH = 1
SEQ = 128
DEPTH = 2
DEC_BATCH = 1
DEC_SEQ = 256
PAST_LEN = 128

GRID_W = 64
HA = 4
DHA = 64
A_W = HA * 2 * DHA
POOL_WINDOWS = (2, 4, 8, 16)
POOL_G = 4
POOL_GC = 128
POOL_W = POOL_G * POOL_GC
HC = 8
KVC = 2
REPC = HC // KVC
DHC = 64
WINDOW = 128
C_W = HC * DHC
N_BRANCH = 3
BRANCH_W = 512
QBLK = 128
SPLITS = (A_W, A_W, A_W, POOL_W, C_W, KVC * DHC, KVC * DHC)
IN_W = sum(SPLITS)
ROPE_BASE = 10000.0
ROT_HALF = 32
D_FF = 2816
N_EXP = 8
TOP_K = 2
D_FF_E = 1408
N_DENSE = (DEPTH + 1) // 2
N_MOE = DEPTH // 2
EPS = 1e-6
NEG_INF = -1e30

kernel_name = "hybrid_diffusion_prefix_step"

F32 = jnp.float32

def rmsnorm(x, g):
    xf = x.astype(F32)
    y = xf * lax.rsqrt(jnp.mean(xf * xf, axis=-1, keepdims=True) + EPS)
    return (y * g.astype(F32)).astype(x.dtype)

def adaln_mods(cvec, w, b):
    m = jax.nn.silu(cvec) @ w + b
    return [t[:, None, :] for t in jnp.split(m, 6, axis=-1)]

def split_proj(p):
    B, T, _ = p.shape
    offs = [int(o) for o in np.cumsum(SPLITS)[:-1]]
    qa, ka, va, ub, qc, kc, vc = jnp.split(p, offs, axis=-1)
    return (qa.reshape(B, T, HA, 2, DHA), ka.reshape(B, T, HA, 2, DHA),
            va.reshape(B, T, HA, 2 * DHA), ub,
            qc.reshape(B, T, HC, DHC), kc.reshape(B, T, KVC, DHC), vc.reshape(B, T, KVC, DHC))

def axial_angles(T):
    rows = T // GRID_W
    row = jnp.repeat(jnp.arange(rows, dtype=F32), GRID_W)
    col = jnp.tile(jnp.arange(GRID_W, dtype=F32), rows)
    inv = ROPE_BASE ** (-jnp.arange(0, ROT_HALF, 2, dtype=F32) / ROT_HALF)
    return row[:, None] * inv, col[:, None] * inv

def axial_rope(x, ang_r, ang_c):
    half = ROT_HALF // 2
    bshape = (1, x.shape[1]) + (1,) * (x.ndim - 3) + (half,)

    def rot(seg, ang):
        cos = jnp.cos(ang).reshape(bshape).astype(x.dtype)
        sin = jnp.sin(ang).reshape(bshape).astype(x.dtype)
        a1, a2 = seg[..., :half], seg[..., half:]
        return jnp.concatenate([a1 * cos - a2 * sin, a2 * cos + a1 * sin], axis=-1)

    return jnp.concatenate([rot(x[..., :ROT_HALF], ang_r), rot(x[..., ROT_HALF:], ang_c)], axis=-1)

def diff_lambda(lam_p, l):
    lam_init = 0.8 - 0.6 * math.exp(-0.3 * l)
    lf = lam_p.astype(F32)
    lam = jnp.exp(jnp.sum(lf[0] * lf[1])) - jnp.exp(jnp.sum(lf[2] * lf[3])) + lam_init
    return lam, lam_init

def diff_attention(q, k, v, lam):
    B, Tq = q.shape[:2]
    nblk = Tq // QBLK
    qb = q.reshape(B, nblk, QBLK, HA, 2, DHA).swapaxes(0, 1)

    def block(qi):
        s = jnp.einsum('bqhmd,bkhmd->bhmqk', qi, k).astype(F32) * (DHA ** -0.5)
        p = jax.nn.softmax(s, axis=-1)
        a = p[:, :, 0] - lam * p[:, :, 1]
        return jnp.einsum('bhqk,bkhe->bqhe', a.astype(v.dtype), v)

    o = lax.map(block, qb)
    return o.swapaxes(0, 1).reshape(B, Tq, HA, 2 * DHA)

def sink_softmax_values(s, sink, v):
    sk = jnp.broadcast_to(sink.astype(F32).reshape(1, KVC, REPC, 1, 1), s.shape[:-1] + (1,))
    p = jax.nn.softmax(jnp.concatenate([s, sk], axis=-1), axis=-1)[..., :-1]
    return jnp.einsum('bgrqk,bkgd->bqgrd', p.astype(v.dtype), v)

def gqa_dense_attention(q, k, v, sink):
    B, T = q.shape[:2]
    nblk = T // QBLK
    qb = q.reshape(B, nblk, QBLK, KVC, REPC, DHC).swapaxes(0, 1)

    def block(qi):
        s = jnp.einsum('bqgrd,bkgd->bgrqk', qi, k).astype(F32) * (DHC ** -0.5)
        return sink_softmax_values(s, sink, v)

    o = lax.map(block, qb)
    return o.swapaxes(0, 1).reshape(B, T, C_W)

def window_attention(q, k, v, ck, cv, sink):
    B, T = q.shape[:2]
    L = ck.shape[1]
    nblk = T // QBLK
    span = QBLK + 2 * WINDOW
    kp = jnp.pad(k, ((0, 0), (WINDOW, WINDOW), (0, 0), (0, 0)))
    vp = jnp.pad(v, ((0, 0), (WINDOW, WINDOW), (0, 0), (0, 0)))
    qb = q.reshape(B, nblk, QBLK, KVC, REPC, DHC).swapaxes(0, 1)
    starts = jnp.arange(nblk, dtype=jnp.int32) * QBLK

    def block(args):
        qi, s0 = args
        kw = lax.dynamic_slice_in_dim(kp, s0, span, axis=1)
        vw = lax.dynamic_slice_in_dim(vp, s0, span, axis=1)
        keys = jnp.concatenate([ck, kw], axis=1)
        vals = jnp.concatenate([cv, vw], axis=1)
        s = jnp.einsum('bqgrd,bkgd->bgrqk', qi, keys).astype(F32) * (DHC ** -0.5)
        qpos = s0 + jnp.arange(QBLK)
        kpos = s0 - WINDOW + jnp.arange(span)
        band = ((jnp.abs(qpos[:, None] - kpos[None, :]) <= WINDOW)
                & (kpos >= 0)[None, :] & (kpos < T)[None, :])
        mask = jnp.concatenate([jnp.ones((QBLK, L), dtype=bool), band], axis=1)
        s = jnp.where(mask, s, NEG_INF)
        return sink_softmax_values(s, sink, vals)

    o = lax.map(block, (qb, starts))
    return o.swapaxes(0, 1).reshape(B, T, C_W)

def multiscale_pool(u, w_pool, pscale):
    B, T, _ = u.shape
    uf = u.astype(F32)
    cs = jnp.concatenate([jnp.zeros((B, 1, POOL_W), F32), jnp.cumsum(uf, axis=1)], axis=1)
    t = jnp.arange(T)
    outs = []
    for g, w in enumerate(POOL_WINDOWS):
        lo = jnp.clip(t - w // 2, 0, T)
        hi = jnp.clip(t + w - w // 2, 0, T)
        seg = cs[..., g * POOL_GC:(g + 1) * POOL_GC]
        mean = (jnp.take(seg, hi, axis=1) - jnp.take(seg, lo, axis=1)) / (hi - lo).astype(F32)[None, :, None]
        outs.append(mean - uf[..., g * POOL_GC:(g + 1) * POOL_GC])
    pooled = jnp.stack(outs, axis=2).astype(u.dtype)
    y = jnp.einsum('btgc,gce->btge', pooled, w_pool).reshape(B, T, POOL_W)
    return y * pscale

def merge_branches(h, oA, oB, oC, w_gate_l, w_branch_l, w_out_l):
    B, T, _ = h.shape
    o = jnp.stack([oA, oB, oC], axis=2)
    p = jnp.einsum('btnc,ncd->btnd', o, w_branch_l)
    g = jax.nn.sigmoid((h @ w_gate_l).reshape(B, T, N_BRANCH, D_MODEL))
    return jnp.sum(g * p, axis=2) @ w_out_l

def swiglu(h, wg, wu, wd):
    return (jax.nn.silu(h @ wg) * (h @ wu)) @ wd

def channel_mixer(h, l, w_ff_gate, w_ff_up, w_ff_down, w_router, w_ex_gate, w_ex_up, w_ex_down):
    i = l // 2
    if l % 2 == 0:
        return swiglu(h, w_ff_gate[i], w_ff_up[i], w_ff_down[i])
    logits = (h @ w_router[i]).astype(F32)
    top_v, top_i = lax.top_k(logits, TOP_K)
    top_w = jax.nn.softmax(top_v, axis=-1)
    gates = jnp.sum(jax.nn.one_hot(top_i, N_EXP, dtype=F32) * top_w[..., None], axis=-2).astype(h.dtype)
    y = jnp.zeros_like(h)
    for e in range(N_EXP):
        y = y + gates[..., e:e + 1] * swiglu(h, w_ex_gate[i, e], w_ex_up[i, e], w_ex_down[i, e])
    return y

def setup_inputs(seed: int = 0) -> dict:
    key = jax.random.key(seed)
    ks = iter(jax.random.split(key, 40))

    def nrm(shape, scale=1.0):
        return jax.random.normal(next(ks), shape, F32) * scale

    def gain(shape):
        return 1.0 + nrm(shape, 0.05)

    D = D_MODEL
    return {
        "x_prompt": nrm((BATCH, SEQ, D)),
        "x_sample": nrm((DEC_BATCH, DEC_SEQ, D)),
        "cache_diff_k": nrm((DEC_BATCH, DEPTH, PAST_LEN, HA, 2, DHA)),
        "cache_diff_v": nrm((DEC_BATCH, DEPTH, PAST_LEN, HA, 2 * DHA)),
        "cache_win_k": nrm((DEC_BATCH, DEPTH, PAST_LEN, KVC, DHC)),
        "cache_win_v": nrm((DEC_BATCH, DEPTH, PAST_LEN, KVC, DHC)),
        "c": nrm((DEC_BATCH, D)),
        "c_ctx": nrm((D,)),
        "w_ada": nrm((DEPTH, D, 6 * D), 0.5 * D ** -0.5),
        "b_ada": nrm((DEPTH, 6 * D), 0.01),
        "norm1_g": gain((DEPTH, D)),
        "norm2_g": gain((DEPTH, D)),
        "w_in": nrm((DEPTH, D, IN_W), D ** -0.5),
        "w_gate": nrm((DEPTH, D, N_BRANCH * D), D ** -0.5),
        "lam_p": nrm((DEPTH, 4, DHA), 0.1),
        "subln_g": gain((DEPTH, 2 * DHA)),
        "w_pool": nrm((DEPTH, POOL_G, POOL_GC, POOL_GC), POOL_GC ** -0.5),
        "pool_scale": gain((DEPTH, POOL_W)),
        "sink": nrm((DEPTH, HC), 0.5),
        "w_branch": nrm((DEPTH, N_BRANCH, BRANCH_W, D), BRANCH_W ** -0.5),
        "w_out": nrm((DEPTH, D, D), D ** -0.5),
        "w_ff_gate": nrm((N_DENSE, D, D_FF), D ** -0.5),
        "w_ff_up": nrm((N_DENSE, D, D_FF), D ** -0.5),
        "w_ff_down": nrm((N_DENSE, D_FF, D), D_FF ** -0.5),
        "w_router": nrm((N_MOE, D, N_EXP), D ** -0.5),
        "w_ex_gate": nrm((N_MOE, N_EXP, D, D_FF_E), D ** -0.5),
        "w_ex_up": nrm((N_MOE, N_EXP, D, D_FF_E), D ** -0.5),
        "w_ex_down": nrm((N_MOE, N_EXP, D_FF_E, D), D_FF_E ** -0.5),
        "final_g": gain((D,)),
    }

def reference(x_prompt, x_sample, cache_diff_k, cache_diff_v, cache_win_k, cache_win_v, c, c_ctx,
              w_ada, b_ada, norm1_g, norm2_g, w_in, w_gate, lam_p, subln_g, w_pool, pool_scale,
              sink, w_branch, w_out, w_ff_gate, w_ff_up, w_ff_down, w_router, w_ex_gate,
              w_ex_up, w_ex_down, final_g):
    xp = x_prompt
    Bp, S, _ = xp.shape
    dk_l, dv_l, wk_l, wv_l = [], [], [], []
    for l in range(DEPTH):
        sh1, sc1, g1, sh2, sc2, g2 = adaln_mods(c_ctx[None, :], w_ada[l], b_ada[l])
        h = rmsnorm(xp, norm1_g[l]) * (1.0 + sc1) + sh1
        qa, ka, va, ub, qc, kc, vc = split_proj(h @ w_in[l])
        lam, lam_init = diff_lambda(lam_p[l], l)
        oA = rmsnorm(diff_attention(qa, ka, va, lam), subln_g[l]) * (1.0 - lam_init)
        oA = oA.reshape(Bp, S, A_W)
        oB = multiscale_pool(ub, w_pool[l], pool_scale[l])
        oC = gqa_dense_attention(qc, kc, vc, sink[l])
        xp = xp + g1 * merge_branches(h, oA, oB, oC, w_gate[l], w_branch[l], w_out[l])
        h2 = rmsnorm(xp, norm2_g[l]) * (1.0 + sc2) + sh2
        xp = xp + g2 * channel_mixer(h2, l, w_ff_gate, w_ff_up, w_ff_down, w_router,
                                     w_ex_gate, w_ex_up, w_ex_down)
        dk_l.append(ka)
        dv_l.append(va)
        wk_l.append(kc)
        wv_l.append(vc)
    y_prompt = rmsnorm(xp, final_g)
    new_diff_k = jnp.stack(dk_l, axis=1)
    new_diff_v = jnp.stack(dv_l, axis=1)
    new_win_k = jnp.stack(wk_l, axis=1)
    new_win_v = jnp.stack(wv_l, axis=1)

    xs = x_sample
    Bs, T, _ = xs.shape
    ang_r, ang_c = axial_angles(T)
    for l in range(DEPTH):
        sh1, sc1, g1, sh2, sc2, g2 = adaln_mods(c, w_ada[l], b_ada[l])
        h = rmsnorm(xs, norm1_g[l]) * (1.0 + sc1) + sh1
        qa, ka, va, ub, qc, kc, vc = split_proj(h @ w_in[l])
        qa = axial_rope(qa, ang_r, ang_c)
        ka = axial_rope(ka, ang_r, ang_c)
        qc = axial_rope(qc, ang_r, ang_c)
        kc = axial_rope(kc, ang_r, ang_c)
        lam, lam_init = diff_lambda(lam_p[l], l)
        ka_all = jnp.concatenate([cache_diff_k[:, l], ka], axis=1)
        va_all = jnp.concatenate([cache_diff_v[:, l], va], axis=1)
        oA = rmsnorm(diff_attention(qa, ka_all, va_all, lam), subln_g[l]) * (1.0 - lam_init)
        oA = oA.reshape(Bs, T, A_W)
        oB = multiscale_pool(ub, w_pool[l], pool_scale[l])
        oC = window_attention(qc, kc, vc, cache_win_k[:, l], cache_win_v[:, l], sink[l])
        xs = xs + g1 * merge_branches(h, oA, oB, oC, w_gate[l], w_branch[l], w_out[l])
        h2 = rmsnorm(xs, norm2_g[l]) * (1.0 + sc2) + sh2
        xs = xs + g2 * channel_mixer(h2, l, w_ff_gate, w_ff_up, w_ff_down, w_router,
                                     w_ex_gate, w_ex_up, w_ex_down)
    y_sample = rmsnorm(xs, final_g)

    return (y_prompt, y_sample, new_diff_k, new_diff_v, new_win_k, new_win_v)


_drawn_inputs = setup_inputs


def setup_inputs(seed=0):
    import zlib

    import numpy as np

    out = dict(_drawn_inputs(seed))
    spreads = {}
    factors = {'cache_win_k': 3.122,
     'cache_win_v': 3.073,
     'b_ada': 2.898,
     'subln_g': 4.454,
     'pool_scale': 4.079,
     'sink': 22.681,
     'norm2_g': 2.674}
    for name, (base, spread) in spreads.items():
        noise = np.random.default_rng([zlib.crc32(name.encode()), seed]).standard_normal(out[name].shape)
        drawn = base * np.exp(spread * noise) if base else spread * noise
        out[name] = __import__('jax').numpy.asarray(drawn.astype(out[name].dtype))
    for name, factor in factors.items():
        out[name] = (out[name] * factor).astype(out[name].dtype)
    return out
```

```python
import math
from contextlib import ExitStack

import numpy as np
import concourse.bass as bass
from concourse import mybir

F32 = mybir.dt.float32
F32R = mybir.dt.float32r
ALU = mybir.AluOpType
ACT = mybir.ActivationFunctionType
X = mybir.AxisListType.X

P = 128
D = 1024
KD = D // P
DEPTH = 2
BLK = 3
T = BLK * P
GRID_W = 64
HA, DHA = 4, 64
HC, KVC, DHC = 8, 2, 64
WINDOWS = (2, 4, 8, 16)
EPS = 1e-6
NEG = -1e30
A_COLS = HA * 2 * DHA
IN_W = 3 * A_COLS + 512 + HC * DHC + 2 * KVC * DHC
D_FF = 2816
F_U = 1408
KF = F_U // P
N_EXP = 8
N_HALF = D_FF // F_U

RING = 3
SLOT = 16 * P
N_WIN = IN_W // 256
ORDER = (1, 0, 2)
N_MIX = N_WIN + 3 * 6 + 4
GU = KF
DOWN = ((0, 1), (2, 3), (4, 5), (6, 7), (8,), (9,), (10,))
UNIT = GU + len(DOWN)
assert N_MIX % RING == 0 and UNIT % RING == 0
BASE = (0, N_MIX + N_HALF * UNIT)
STAGED = (0, 1, 2, 3, 8, 9, 10)
WIN_INC = N_WIN + 1
KV_SLOTS = (2, 3, 4, 5, 10)
N_TR = len(STAGED) + 1
N_ADA = 6 * D // P
ADA_RING = 2

R_BADA, R_N1, R_N2, R_PS, R_SUB, R_C, R_CTX, R_FIN, R_END = 0, 48, 56, 64, 68, 69, 77, 85, 93
SH1, SC1, G1, SH2, SC2, G2 = (8 * i for i in range(6))


def shape_constants():
    ident = np.eye(P, dtype=np.float32)
    pool = np.zeros((P, 4, T + 2 * P), np.float32)

    def mean_minus_self(n, w):
        m = np.zeros((n, n), np.float32)
        for t in range(n):
            lo, hi = max(t - w // 2, 0), min(t + w - w // 2, n)
            m[lo:hi, t] = np.float32(1.0) / np.float32(hi - lo)
            m[t, t] -= 1.0
        return m

    for g, w in enumerate(WINDOWS):
        pool[:, g, 0:P] = mean_minus_self(P, w)
        m = mean_minus_self(2 * P, w)
        pool[:, g, P:P + 256] = m[0:P]
        pool[:, g, P + 256:P + 512] = m[P:256]
    q = np.arange(P)
    mask = np.zeros((P, 2, P), np.float32)
    mask[:, 0, :] = np.where(q[None, :] <= q[:, None], 0.0, NEG)
    mask[:, 1, :] = np.where(q[None, :] >= q[:, None], 0.0, NEG)
    inv = 10000.0 ** (-np.arange(0, 32, 2, dtype=np.float32) / np.float32(32))
    t = np.arange(2 * P)
    ang = np.stack([(t // GRID_W)[:, None] * inv, (t % GRID_W)[:, None] * inv], 1).astype(np.float32)
    rope = np.zeros((P, 2, 2, 32), np.float32)
    for b in range(2):
        a = ang[b * P:(b + 1) * P].reshape(P, 32)
        rope[:, b, 0], rope[:, b, 1] = np.cos(a), np.sin(a)
    tri = np.zeros((P, 8, 8), np.float32)
    tri[:] = (np.arange(8)[None, :] < np.arange(8)[:, None])
    return np.concatenate([ident, mask.reshape(P, 256), rope.reshape(P, 128), tri.reshape(P, 64),
                           pool.reshape(P, -1)], 1).astype(np.float32)


C_MASK, C_ROPE, C_TRI, C_POOL = 128, 384, 512, 576
POOL_COLS = 4 * (T + 2 * P)


def prefix_step_kernel(nc, a, outs, const):
    y_prompt, y_sample, new_dk, new_dv, new_wk, new_wv = outs
    ctx = ExitStack()
    with ctx:
        top = [(nc.sbuf_base + 31) // 32 * 32]
        sb_end = nc.sbuf_base + nc.sbuf_bytes_remaining

        def at(name, cols, offset, dt=F32, shape=None):
            return nc.alloc_sbuf_tensor_at(name, [P] + list(shape or [cols]), dt, offset=offset)

        def place(name, shape, dt=F32):
            n = int(np.prod(shape)) * 4
            t = nc.alloc_sbuf_tensor_at(name, [P] + list(shape), dt, offset=top[0])
            top[0] += (n + 31) // 32 * 32
            return t

        def sem(name):
            return ctx.enter_context(nc.semaphore(name))

        raw = place("raw", [RING, SLOT])
        whi = place("whi", [RING, SLOT], F32R)
        wlo = place("wlo", [RING, SLOT], F32R)
        ada = place("ada", [ADA_RING, KD, P])
        xT = place("xT", [KD, T])
        hhi = place("hhi", [KD, T], F32R)
        hlo = place("hlo", [KD, T], F32R)
        scratch_at = top[0]
        macc = place("macc", [KD, T])
        gbuf_at = top[0]
        gbuf = place("gbuf", [4, T])
        oraw_at = top[0]
        oraw = place("oraw", [4, T])
        ohi = place("ohi", [4, T], F32R)
        olo = place("olo", [4, T], F32R)
        rstd = place("rstd", [T])
        cst = place("cst", [C_POOL])
        ones = place("ones", [P])
        epsc = place("epsc", [1])
        wpool = place("wpool", [4, P])
        wrout = place("wrout", [KD, N_EXP])
        cols = place("cols", [DEPTH, R_END])
        silc = place("silc", [2, KD])
        mods = place("mods", [DEPTH, N_ADA, 2])
        amul = place("amul", [DEPTH, 2, KD, 2])
        subg = place("subg", [DEPTH])
        sinkr = place("sinkr", [DEPTH, HC])
        nsink = place("nsink", [DEPTH, HC])
        lamp = place("lamp", [DEPTH, 2])
        neglam = place("neglam", [DEPTH])
        small = place("small", [2, 10])
        rsm = place("rsm", [BLK, 16])
        gates = place("gates", [BLK, N_EXP])
        shared = top[0]
        vtok = place("vtok", [BLK, 640])
        utok = place("utok", [BLK, 512])
        qTA = place("qTA", [4, T])
        kTA = place("kTA", [4, 512])
        qTC = place("qTC", [4, T])
        kTC = place("kTC", [2, 512])
        stage = place("stage", [2, BLK, 256])
        ctxv = place("ctxv", [640])
        assert top[0] <= sb_end, (top[0], sb_end)
        pt = at("pt", 2 * T, stage_off := top[0] - 2560 - 2 * BLK * 256 * 4, shape=[2, T])
        pooled = at("pooled", 4 * T, gbuf_at, shape=[4, T])
        ebuf = at("ebuf", 4 * T, gbuf_at, shape=[2, 2, T])
        osq = at("osq", 4 * T, gbuf_at, shape=[4, T])
        ctxk = at("ctxk", 768, gbuf_at, shape=[768])
        kcd = at("kcd", 768, gbuf_at + 3072, shape=[BLK, 256])
        vrows = at("vrows", 2 * P, gbuf_at, shape=[DEPTH, P])
        lamrow = at("lamrow", 512, gbuf_at + 1024, shape=[DEPTH * 2, 2, DHA])
        lamprod = at("lamprod", 256, gbuf_at + 3072, shape=[DEPTH * 2, DHA])
        xtok = at("xtok", BLK * D, scratch_at, shape=[BLK, D])
        poolm = at("poolm", POOL_COLS, scratch_at, shape=[4, T + 2 * P])
        hidhi = at("hidhi", KF * T, shared, F32R, [KF, T])
        hidlo = at("hidlo", KF * T, shared + KF * T * 4, F32R, [KF, T])
        sil = at("sil", 2 * T, shared + 2 * KF * T * 4, shape=[2, T])
        val = at("val", 2 * T, shared + 2 * KF * T * 4 + 3072, shape=[2, T])
        gbc = at("gbc", N_EXP * T, scratch_at, shape=[N_EXP, T])
        yout = at("yout", BLK * D, shared, shape=[BLK, D])
        rcmp = at("rcmp", 2 * BLK * 64, gbuf_at, shape=[2, BLK, 64])
        rope_t = at("rope_t", 256, oraw_at, shape=[2, 128])
        assert top[0] <= sb_end, (top[0], sb_end)
        assert shared + 2 * KF * T * 4 + 6144 <= sb_end

        ident = cst[:, 0:P]
        mask = cst[:, C_MASK:C_ROPE].rearrange("p (i k) -> p i k", i=2)
        rope = cst[:, C_ROPE:C_TRI].rearrange("p (b c i) -> p b c i", b=2, c=2)
        tri = cst[:, C_TRI:C_POOL]
        ps = ctx.enter_context(nc.psum_tensor("ps", [P, 8, 512], F32))

        def pair(g):
            return ps[:, 2 * g:2 * g + 2, 0:T]

        raw_in = [sem(f"raw_in{j}") for j in range(RING)]
        hi_done, lo_done, mm_done = sem("hi_done"), sem("lo_done"), sem("mm_done")
        ada_in = [sem(f"ada_in{j}") for j in range(ADA_RING)]
        ada_used, ada_read = sem("ada_used"), sem("ada_read")
        mods_ready = sem("mods_ready")
        init_in, ones_set = sem("init_in"), sem("ones_set")
        x_tr, x_ev, v_tr, v_ev, silc_ready = sem("x_tr"), sem("x_ev"), sem("v_tr"), sem("v_ev"), sem("silc_ready")
        sq_done, ssq_done, xn_done, hf_done = sem("sq_done"), sem("ssq_done"), sem("xn_done"), sem("hf_done")
        h_ready, hh_done = sem("h_ready"), sem("hh_done")
        win_evac, rope_done, tr_done, tr_evac = sem("win_evac"), sem("rope_done"), sem("tr_done"), sem("tr_evac")
        layer_in = [sem(f"layer_in{l}") for l in range(DEPTH)]
        poolm_in, kv_out = sem("poolm_in"), sem("kv_out")
        pool_mm, pool_ev, pooly_mm = sem("pool_mm"), sem("pool_ev"), sem("pooly_mm")
        s_done, nmax_done, e_done, p_done = sem("s_done"), sem("nmax_done"), sem("e_done"), sem("p_done")
        tp_done, pt_evac, pv_done, o_evac = sem("tp_done"), sem("pt_evac"), sem("pv_done"), sem("o_evac")
        osq_done, oss_done, on_done = sem("osq_done"), sem("oss_done"), sem("on_done")
        oh_done, o_ready = sem("oh_done"), sem("o_ready")
        gate_evac, merge_done = sem("gate_evac"), sem("merge_done")
        mh_done, merged_ready, out_evac = sem("mh_done"), sem("merged_ready"), sem("out_evac")
        rt_done, gates_ready, gb_done, gbc_ready = sem("rt_done"), sem("gates_ready"), sem("gb_done"), sem("gbc_ready")
        sil_done, hid_done, unit_done = sem("sil_done"), sem("hid_done"), sem("unit_done")
        y_tr, y_ev, y_out = sem("y_tr"), sem("y_ev"), sem("y_out")
        chain_v, chain_u, chain_m = sem("chain_v"), sem("chain_u"), sem("chain_m")
        rms_done, orms_done = sem("rms_done"), sem("orms_done")
        lam_done, lam_sums, chain_p = sem("lam_done"), sem("lam_sums"), sem("chain_p")
        rt_sub, rt_exp, wrout_in = sem("rt_sub"), sem("rt_exp"), sem("wrout_in")

        n_init = 3 + 8 * DEPTH + 2

        def gate_slot(l, o, half, j):
            return BASE[l] + N_WIN + 6 * o + 3 * half + j

        def branch_slot(l, o, half):
            return gate_slot(l, o, half, 2)

        def out_slot(l, j):
            return BASE[l] + N_WIN + 18 + j

        def wide_slots(l):
            return [gate_slot(l, o, half, j) for o in range(3) for half in range(2) for j in range(2)] + [
                out_slot(l, j) for j in range(4)]

        PER_WIDE = N_ADA // len(wide_slots(0))

        def ada_ps(l, j):
            bank = 7 if l == 0 else 2 * (wide_slots(0)[j // PER_WIDE] % 2)
            return ps[:, bank, 384 + 2 * j:386 + 2 * j]

        def raw_wait(eng, n, more=0):
            eng.wait_ge(raw_in[n % RING], more + 32 * (n // RING + 1))

        block = ctx.enter_context(nc.Block())

        @block.sync
        def _(sp):
            def halves(n, dst, src, axis_cols=None):
                if n >= RING:
                    sp.wait_ge(lo_done, n - RING + 1)
                for i in range(2):
                    sp.dma_start(dst[i], src[i]).then_inc(raw_in[n % RING], 16)

            def k_by_cols(n, w, k, c0, width):
                d = raw[:, n % RING, 0:k * width].rearrange("p (k c) -> p k c", k=k)
                s = w.rearrange("(k p) c -> p k c", p=P)[:, :, c0:c0 + width]
                halves(n, [d[:, 0:k // 2], d[:, k // 2:k]], [s[:, 0:k // 2], s[:, k // 2:k]])

            sp.dma_start(cst[:, :], const[:, 0:C_POOL]).then_inc(init_in, 16)
            sp.dma_start(xtok[:, 0, :], a["x_prompt"][0]).then_inc(init_in, 16)
            sp.dma_start(xtok[:, 1:3, :], a["x_sample"][0].rearrange("(b p) d -> p b d", p=P)).then_inc(init_in, 16)
            for l in range(DEPTH):
                for r, src in ((R_BADA, a["b_ada"][l]), (R_N1, a["norm1_g"][l]), (R_N2, a["norm2_g"][l]),
                               (R_PS, a["pool_scale"][l]), (R_SUB, a["subln_g"][l]), (R_C, a["c"][0]),
                               (R_CTX, a["c_ctx"]), (R_FIN, a["final_g"])):
                    rows = src.shape[0] // P
                    sp.dma_start(vrows[r:r + rows, l, :], src.rearrange("(r c) -> r c", c=P)).then_inc(init_in, 16)
            sp.dma_start(lamrow[:, :, :].rearrange("p a b c -> p (a b c)"),
                         a["lam_p"].rearrange("(o l) r d -> o (l r d)", o=1).to_broadcast([P, DEPTH * 4 * DHA])
                         ).then_inc(init_in, 16)
            sp.dma_start(sinkr[:, :, :].rearrange("p l h -> p (l h)"),
                         a["sink"].rearrange("(o l) h -> o (l h)", o=1).to_broadcast([P, DEPTH * HC])
                         ).then_inc(init_in, 16)
            for l in range(DEPTH):
                for s in range(N_WIN):
                    k_by_cols(BASE[l] + s, a["w_in"][l], KD, 256 * s, 256)
                for o, br in enumerate(ORDER):
                    for half in range(2):
                        for j in range(2):
                            k_by_cols(gate_slot(l, o, half, j), a["w_gate"][l], KD,
                                      br * D + 512 * half + 256 * j, 256)
                        k_by_cols(branch_slot(l, o, half), a["w_branch"][l, br], 4, 512 * half, 512)
                for j in range(4):
                    k_by_cols(out_slot(l, j), a["w_out"][l], KD, 256 * j, 256)
                n0 = BASE[l] + N_MIX
                with sp.Fori(0, N_HALF if l == 0 else N_EXP) as u:
                    if l == 0:
                        wg = a["w_ff_gate"][0][:, bass.ds(u * F_U, F_U)]
                        wu = a["w_ff_up"][0][:, bass.ds(u * F_U, F_U)]
                        wd = a["w_ff_down"][0][bass.ds(u * F_U, F_U), :]
                    else:
                        wg, wu, wd = (a[f"w_ex_{x}"][0, bass.ds(u, 1)].rearrange("e k c -> (e k) c")
                                      for x in ("gate", "up", "down"))
                    wg, wu, wd = (w.rearrange("(k p) c -> p k c", p=P) for w in (wg, wu, wd))
                    for s in range(UNIT):
                        j = s % RING
                        sp.wait_ge(lo_done, u * UNIT + (n0 + s - RING + 1))
                        if s < GU:
                            d = raw[:, j, :].rearrange("p (w k c) -> p w k c", w=2, k=KD)
                            pieces = [(d[:, 0], wg[:, :, s * P:(s + 1) * P]), (d[:, 1], wu[:, :, s * P:(s + 1) * P])]
                        else:
                            f = DOWN[s - GU]
                            d = raw[:, j, 0:len(f) * D].rearrange("p (k c) -> p k c", c=D)
                            h = D // 2
                            pieces = [(d[:, :, i * h:(i + 1) * h], wd[:, f[0]:f[-1] + 1, i * h:(i + 1) * h])
                                      for i in range(2)]
                        for dst, src in pieces:
                            sp.dma_start(dst, src).then_inc(raw_in[j], 16)

        @block.gpsimd
        def _(pool):
            pool.memset(epsc[:, :], EPS)
            pool.memset(ones[:, :], 1.0).then_inc(ones_set, 1)

            def ada_loads(l):
                w = a["w_ada"][l].rearrange("(k p) c -> p k c", p=P)
                for j in range(N_ADA):
                    n = l * N_ADA + j
                    if n >= ADA_RING:
                        pool.wait_ge(ada_used, n - ADA_RING + 1)
                    pool.dma_start(ada[:, n % ADA_RING], w[:, :, j * P:(j + 1) * P]).then_inc(ada_in[n % ADA_RING], 16)

            def layer_loads(l):
                if l == 0:
                    pool.wait_ge(v_ev, 2)
                    pool.wait_ge(lam_done, DEPTH)
                else:
                    pool.wait_ge(merge_done, 6 * l)
                ck = a["cache_win_k"][0, l].rearrange("t g d -> t (g d)")
                pool.dma_start(ctxk[:, 0:512], a["cache_diff_k"][0, l].rearrange("t h m d -> t (h m d)")).then_inc(layer_in[l], 16)
                for i in range(2):
                    for g in range(2):
                        pool.dma_start(ctxk[:, 512 + g * 128 + i * 64:512 + g * 128 + i * 64 + 64],
                                       ck[:, g * 64:(g + 1) * 64]).then_inc(layer_in[l], 16)
                pool.dma_start(ctxv[:, 0:512], a["cache_diff_v"][0, l].rearrange("t h e -> t (h e)")).then_inc(layer_in[l], 16)
                pool.dma_start(ctxv[:, 512:640], a["cache_win_v"][0, l].rearrange("t g d -> t (g d)")).then_inc(layer_in[l], 16)
                pool.dma_start(wpool[:, :, :], a["w_pool"][l].rearrange("g c e -> c g e")).then_inc(layer_in[l], 16)
                pool.wait_ge(h_ready, 2 * l + 1)
                pool.dma_start(poolm[:, :, :].rearrange("p g c -> p (g c)"), const[:, C_POOL:C_POOL + POOL_COLS]).then_inc(poolm_in, 16)

            ada_loads(0)
            layer_loads(0)
            pool.dma_start(wrout[:, :, :], a["w_router"][0].rearrange("(k p) e -> p k e", p=P)).then_inc(wrout_in, 16)
            ada_loads(1)
            pool.wait_ge(unit_done, 1 + N_HALF)
            layer_loads(1)

        @block.tensor
        def _(pe):
            def mm3(out, s, m, first, last, **kw):
                pe.matmul(out, s[0], m[0], start=first, stop=False, **kw)
                pe.matmul(out, s[0], m[1], start=False, stop=False, **kw)
                return pe.matmul(out, s[1], m[0], start=False, stop=last, **kw)

            def slot(n, k):
                return [w[:, n % RING, :].rearrange("p (k c) -> p k c", k=k) for w in (whi, wlo)]

            def ada_chunk(l, j):
                n = l * N_ADA + j
                pe.wait_ge(ada_in[n % ADA_RING], 16 * (n // ADA_RING + 1))
                for k in range(KD):
                    mm = pe.matmul(ada_ps(l, j), ada[:, n % ADA_RING, k, :], silc[:, :, k],
                                   start=(k == 0), stop=(k == KD - 1))
                mm.then_inc(ada_used, 1)

            def sum_squares(i):
                pe.wait_ge(sq_done, i + 1)
                for k in range(KD):
                    mm = pe.matmul(ps[:, 6, 0:T], ones[:, :], macc[:, k, :], start=(k == 0), stop=(k == KD - 1))
                mm.then_inc(ssq_done, 1)

            def rot_transposes(l, ti):
                r = N_TR * l + ti
                pe.wait_ge(rope_done, len(STAGED) * l + ti + 1)
                if r >= 1:
                    pe.wait_ge(tr_evac, r)
                for c in range(2):
                    for b in range(BLK):
                        src = kcd[:, b, c * P:(c + 1) * P] if ti == 6 else stage[:, ti % 2, b, c * P:(c + 1) * P]
                        mm = pe.transpose(ps[:, 4 + c, b * P:(b + 1) * P], src, ident)
                mm.then_inc(tr_done, 1)

            def input_projection(l):
                pe.wait_ge(h_ready, 2 * l + 1)
                for s in range(N_WIN):
                    n = BASE[l] + s
                    pe.wait_ge(lo_done, n + 1)
                    g = s % 2
                    if s >= 2:
                        pe.wait_ge(win_evac, WIN_INC * l + s - 1)
                    w = slot(n, KD)
                    out = ps[:, 2 * g:2 * g + 2, :].rearrange("p a c -> p (a c)")
                    for b in range(BLK):
                        for k in range(KD):
                            mm = mm3(out[:, b * 256:(b + 1) * 256], [h[:, k, b * P:(b + 1) * P] for h in (hhi, hlo)],
                                     [x[:, k, :] for x in w], k == 0, k == KD - 1)
                    mm.then_inc(mm_done, 1)
                    if s - 1 in STAGED:
                        rot_transposes(l, STAGED.index(s - 1))
                rot_transposes(l, 6)
                pe.wait_ge(layer_in[l], 16 * 8)
                pe.wait_ge(tr_evac, N_TR * l + 7)
                for c in range(6):
                    mm = pe.transpose(ps[:, 4 + c // 4, (c % 4) * P:(c % 4 + 1) * P], ctxk[:, c * P:(c + 1) * P], ident)
                mm.then_inc(tr_done, 1)

            def pooling(l):
                pe.wait_ge(win_evac, WIN_INC * (l + 1))
                pe.wait_ge(poolm_in, 16 * (l + 1))
                for g in range(4):
                    u = [utok[:, b, g * P:(g + 1) * P] for b in range(BLK)]
                    pe.matmul(ps[:, g, 0:P], u[0], poolm[:, g, 0:P], start=True, stop=True)
                    pe.matmul(ps[:, g, P:T], u[1], poolm[:, g, P:P + 256], start=True, stop=False)
                    mm = pe.matmul(ps[:, g, P:T], u[2], poolm[:, g, P + 256:P + 512], start=False, stop=True)
                mm.then_inc(pool_mm, 1)
                pe.wait_ge(tr_evac, N_TR * (l + 1))
                pe.wait_ge(pool_ev, l + 1)
                for g in range(4):
                    mm = pe.matmul(ps[:, 4 + g, 0:T], wpool[:, g, :], pooled[:, g, :], start=True, stop=True)
                mm.then_inc(pooly_mm, 1)

            def attention(l, kind):
                st0 = 24 * l + 12 * kind
                it0 = 36 * l + 12 * kind
                per = 1 + kind

                def scores(t):
                    h, qb = t // 3, t % 3
                    if t >= 2:
                        pe.wait_ge(e_done, st0 + t - 1)
                    nk, k0 = (P, 0) if qb == 0 else (T, P)
                    q, kk = (qTA, kTA[:, h, k0:k0 + nk]) if kind == 0 else (qTC, kTC[:, h // 2, k0:k0 + nk])
                    for m in range(2):
                        r = slice(64 * m, 64 * m + 64)
                        out, lhs = ps[:, 2 * (t % 2) + m, 0:nk], q[r, h, qb * P:(qb + 1) * P]
                        if kind == 0 or qb == 0:
                            mm = pe.matmul(out, lhs, kk[r], start=True, stop=True)
                            continue
                        o3, k3 = (x.rearrange("p (a c) -> p a c", c=P) for x in (out, kk[r]))
                        far = 2 - qb
                        near = slice(0, 3, 2) if far else slice(1, 3)
                        pe.matmul(o3[:, near, :], lhs, k3[:, near, :], start=True, stop=True)
                        pe.matmul(o3[:, far, :], lhs, k3[:, far, :], start=True, stop=False)
                        mm = pe.matmul(o3[:, far, :], ident, mask[:, qb - 1, :], start=False, stop=True)
                    mm.then_inc(s_done, 1)

                def transposes(i):
                    t, m = i // per, i % per
                    if m == 0:
                        pe.wait_ge(p_done, st0 + t + 1)
                    if it0 + i >= 2:
                        pe.wait_ge(pt_evac, it0 + i - 1)
                    for kb in range(1 if t % 3 == 0 else 3):
                        mm = pe.transpose(ps[:, 4 + (it0 + i) % 2, kb * P:(kb + 1) * P],
                                          ebuf[:, t % 2, m, kb * P:(kb + 1) * P], ident)
                    mm.then_inc(tp_done, 1)

                def values(i):
                    t, m = i // per, i % per
                    h, qb = t // 3, t % 3
                    pe.wait_ge(pt_evac, it0 + i + 1)
                    grp = 8 * l + 4 * kind + h
                    if qb == 0 and m == 0 and grp >= 2:
                        pe.wait_ge(o_evac, grp - 1)
                    c = slice(h * P, (h + 1) * P) if kind == 0 else slice(512 + (h // 2) * 64, 576 + (h // 2) * 64)
                    keys = [vtok[:, 0, c]] if qb == 0 else [vtok[:, 1, c], vtok[:, 2, c], ctxv[:, c]]
                    rows = slice(0, P) if kind == 0 else slice(64 * m, 64 * m + 64)
                    for kb, v in enumerate(keys):
                        mm = pe.matmul(ps[rows, 6 + grp % 2, qb * P:(qb + 1) * P], v,
                                       pt[:, (it0 + i) % 2, kb * P:(kb + 1) * P],
                                       start=(kb == 0), stop=(kb == len(keys) - 1))
                    mm.then_inc(pv_done, 1)

                pe.wait_ge(gate_evac, 12 * l + 4 * (kind + 1))
                scores(0)
                pe.wait_ge(merge_done, 6 * l + 2 * (kind + 1))
                n = 12 * per
                for i in range(n):
                    if i % per == 0 and i // per + 1 < 12:
                        scores(i // per + 1)
                    transposes(i)
                    if i >= 1:
                        values(i - 1)
                values(n - 1)
                if kind == 0:
                    pe.wait_ge(osq_done, l + 1)
                    for h in range(4):
                        mm = pe.matmul(ps[:, h, 0:T], ones[:, :], osq[:, h, :], start=True, stop=True)
                    mm.then_inc(oss_done, 1)

            def wide(l, n, w, x):
                if l == 0:
                    i = wide_slots(0).index(n)
                    for j in range(PER_WIDE * i, PER_WIDE * (i + 1)):
                        ada_chunk(1, j)
                for j in range(2):
                    for k in range(KD):
                        mm = mm3(ps[:, 2 * (n % 2) + j, 0:T], [y[:, k, j * P:(j + 1) * P] for y in w],
                                 [y[:, k, :] for y in x], k == 0, k == KD - 1)
                mm.then_inc(mm_done, 1)

            def branch(l, o):
                for half in range(2):
                    i = 6 * l + 2 * o + half
                    for j in range(2):
                        n = gate_slot(l, o, half, j)
                        pe.wait_ge(lo_done, n + 1)
                        if i and j == 0:
                            pe.wait_ge(gate_evac, 2 * i)
                        if o == 1 and half == 0 and j == 0:
                            pe.wait_ge(on_done, l + 1)
                        wide(l, n, slot(n, KD), (hhi, hlo))
                    n = branch_slot(l, o, half)
                    pe.wait_ge(lo_done, n + 1)
                    pe.wait_ge(o_ready, 3 * l + o + 1)
                    if half:
                        pe.wait_ge(merge_done, i)
                    w = slot(n, 4)
                    for q in range(4):
                        for k in range(4):
                            mm = mm3(ps[:, 4 + q, 0:T], [y[:, k, q * P:(q + 1) * P] for y in w],
                                     [y[:, k, :] for y in (ohi, olo)], k == 0, k == 3)
                    mm.then_inc(mm_done, 1)

            def out_projection(l):
                pe.wait_ge(merged_ready, l + 1)
                pe.wait_ge(gate_evac, 12 * (l + 1))
                for j in range(4):
                    n = out_slot(l, j)
                    pe.wait_ge(lo_done, n + 1)
                    if j >= 2:
                        pe.wait_ge(out_evac, 4 * l + j - 1)
                    wide(l, n, slot(n, KD), (hhi, hlo))

            def router():
                pe.wait_ge(hf_done, 4)
                pe.wait_ge(wrout_in, 16)
                for b in range(BLK):
                    for k in range(KD):
                        mm = pe.matmul(ps[:, 6, b * N_EXP:(b + 1) * N_EXP], macc[:, k, b * P:(b + 1) * P],
                                       wrout[:, k, :], start=(k == 0), stop=(k == KD - 1))
                mm.then_inc(rt_done, 1)
                pe.wait_ge(gates_ready, 1)
                pe.wait_ge(out_evac, 8)
                for e in range(N_EXP):
                    for b in range(BLK):
                        mm = pe.matmul(ps[:, e, b * P:(b + 1) * P], gates[:, b, e:e + 1].to_broadcast([P, P]),
                                       ident, start=True, stop=True)
                mm.then_inc(gb_done, 1)
                pe.wait_ge(gbc_ready, 1)

            def units(l):
                n0 = BASE[l] + N_MIX
                h0 = 0 if l == 0 else N_HALF * GU
                u0 = 1 + (0 if l == 0 else N_HALF)
                pe.wait_ge(h_ready, 2 * l + 2)
                pe.wait_ge(out_evac, 4 * (l + 1))
                with pe.Fori(0, N_HALF if l == 0 else N_EXP) as u:
                    for s in range(GU):
                        pe.wait_ge(lo_done, u * UNIT + (n0 + s + 1))
                        if s == 1:
                            pe.wait_ge(unit_done, u + u0)
                        if s >= 2:
                            pe.wait_ge(hid_done, u * GU + (h0 + s - 1))
                        w = [x[:, s % RING, :].rearrange("p (w k c) -> p w k c", w=2, k=KD) for x in (whi, wlo)]
                        for j in range(2):
                            for k in range(KD):
                                mm = mm3(ps[:, 2 * (s % 2) + j, 0:T], [y[:, j, k, :] for y in w],
                                         [y[:, k, :] for y in (hhi, hlo)], k == 0, k == KD - 1)
                        mm.then_inc(mm_done, 1)
                    for i, f in enumerate(DOWN):
                        s = GU + i
                        pe.wait_ge(lo_done, u * UNIT + (n0 + s + 1))
                        pe.wait_ge(hid_done, u * GU + (h0 + GU))
                        w = [x[:, s % RING, 0:len(f) * D].rearrange("p (k c) -> p k c", c=D) for x in (whi, wlo)]
                        for c, kf in enumerate(f):
                            for m in range(KD):
                                last = kf == KF - 1
                                st = [y[:, c, m * P:(m + 1) * P] for y in w]
                                mm3(ps[:, 2 + m // 2, (m % 2) * 256:(m % 2 + 1) * 256], st,
                                    [y[:, kf, P:T] for y in (hidhi, hidlo)], kf == 0 and m % 2 == 0, last,
                                    skip_group_check=True)
                                mm = mm3(ps[:, 6 + m // 4, (m % 4) * P:(m % 4 + 1) * P], st,
                                         [y[:, kf, 0:P] for y in (hidhi, hidlo)], kf == 0 and m % 4 == 0, last,
                                         skip_group_check=True)
                        mm.then_inc(mm_done, 1)

            pe.wait_ge(init_in, 16 * n_init)
            for k in range(KD):
                for b in range(BLK):
                    mm = pe.transpose(ps[:, k, b * P:(b + 1) * P], xtok[:, b, k * P:(k + 1) * P], ident)
            mm.then_inc(x_tr, 1)
            pe.wait_ge(x_ev, 1)
            for l in range(DEPTH):
                mm = pe.transpose(ps[:, 4, l * P:l * P + R_END], vrows[0:R_END, l, :], ident[0:R_END, 0:R_END])
            mm.then_inc(v_tr, 1)
            pe.wait_ge(silc_ready, 1)
            for j in range(N_ADA):
                ada_chunk(0, j)
            pe.wait_ge(ones_set, 1)
            for l in range(DEPTH):
                sum_squares(2 * l)
                input_projection(l)
                pooling(l)
                branch(l, 0)
                attention(l, 0)
                branch(l, 1)
                attention(l, 1)
                branch(l, 2)
                out_projection(l)
                sum_squares(2 * l + 1)
                if l == 1:
                    router()
                units(l)
            sum_squares(2 * DEPTH)
            pe.wait_ge(chain_m, 16 * 2 * DEPTH + KD)
            for b in range(BLK):
                for k in range(KD):
                    mm = pe.transpose(ps[:, 2 * b + k // 4, (k % 4) * P:(k % 4 + 1) * P],
                                      macc[:, k, b * P:(b + 1) * P], ident)
                mm.then_inc(y_tr, 1)

        @block.scalar
        def _(act):
            copy = ACT.Copy

            def hi(n):
                raw_wait(act, n)
                if n >= RING:
                    act.wait_ge(mm_done, n - RING + 1)
                act.activation(whi[:, n % RING, :], raw[:, n % RING, :], copy).then_inc(hi_done, 1)

            def square(i):
                act.activation(macc[:, :, :], xT[:, :, :], ACT.Square).then_inc(sq_done, 1)
                act.wait_ge(ssq_done, i + 1)
                act.activation(rstd[:, :], ps[:, 6, 0:T], ACT.Sqrt, scale=1.0 / D, bias=epsc[:, 0:1]).then_inc(rms_done, 1)

            def modulate(i):
                act.wait_ge(xn_done, i + 1)
                l, which = i // 2, i % 2
                sh = (SH1, SH2)[which]
                for k in range(KD):
                    for v, t in ((0, slice(P, T)), (1, slice(0, P))):
                        act.activation(macc[:, k, t], macc[:, k, t], ACT.Identity,
                                       scale=amul[:, l, which, k, v:v + 1],
                                       bias=mods[:, l, sh + k, v:v + 1]).then_inc(chain_m, 1)
                act.wait_ge(chain_m, 16 * (i + 1))
                act.activation(hhi[:, :, :], macc[:, :, :], copy).then_inc(hf_done, 1)

            def input_evac(l, s):
                act.wait_ge(mm_done, BASE[l] + s + 1)
                g = s % 2
                src = ps[:, 2 * g:2 * g + 2, :].rearrange("p a c -> p (a c)")[:, 0:BLK * 256].rearrange(
                    "p (b c) -> p b c", b=BLK)
                kv = KV_SLOTS.index(s) if s in KV_SLOTS else None
                if s in STAGED:
                    ti = STAGED.index(s)
                    if ti >= 2:
                        act.wait_ge(tr_done, N_TR * l + ti - 1)
                    if ti == 4:
                        act.wait_ge(kv_out, 16 * (6 * l + 4))
                    if ti == 0 and l:
                        act.wait_ge(kv_out, 16 * 6 * l)
                    act.activation(stage[:, ti % 2], src, copy).then_inc(win_evac, 1)
                    if s == 10:
                        act.activation(vtok[:, :, 512:640], src[:, :, P:256], copy).then_inc(win_evac, 1)
                elif s < 6:
                    act.activation(vtok[:, :, (s - 4) * 256:(s - 3) * 256], src, copy).then_inc(win_evac, 1)
                else:
                    act.activation(utok[:, :, (s - 6) * 256:(s - 5) * 256], src, copy).then_inc(win_evac, 1)
                ev = WIN_INC * l + s + 1 + (s == 10)
                if kv is not None:
                    act.wait_ge(win_evac, ev)
                if s in (2, 3):
                    act.dma_start(new_dk[0, l].rearrange("t h m d -> t (h m d)")[:, (s - 2) * 256:(s - 1) * 256],
                                  stage[:, STAGED.index(s) % 2, 0, :]).then_inc(kv_out, 16)
                if s in (4, 5):
                    act.dma_start(new_dv[0, l].rearrange("t h e -> t (h e)")[:, (s - 4) * 256:(s - 3) * 256],
                                  vtok[:, 0, (s - 4) * 256:(s - 3) * 256]).then_inc(kv_out, 16)
                if s == 10:
                    act.dma_start(new_wk[0, l].rearrange("t g d -> t (g d)"), stage[:, 0, 0, 0:P]).then_inc(kv_out, 16)
                    act.dma_start(new_wv[0, l].rearrange("t g d -> t (g d)"), vtok[:, 0, 512:640]).then_inc(kv_out, 16)

            def turned_evac(l, ti):
                act.wait_ge(tr_done, N_TR * l + ti + 1)
                src = ps[:, 4:6, 0:T]
                if ti < 2:
                    act.activation(qTA[:, 2 * ti:2 * ti + 2, :], src, copy, scale=DHA ** -0.5).then_inc(tr_evac, 1)
                elif ti < 4:
                    act.activation(kTA[:, 2 * ti - 4:2 * ti - 2, 0:T], src, copy).then_inc(tr_evac, 1)
                elif ti < 6:
                    act.activation(qTC[:, 2 * ti - 8:2 * ti - 6, :], src, copy, scale=DHC ** -0.5).then_inc(tr_evac, 1)
                elif ti == 6:
                    act.activation(kTC[:, :, 0:T], src, copy).then_inc(tr_evac, 1)
                else:
                    act.activation(kTA[:, :, T:512], ps[:, 4, :].rearrange("p (h c) -> p h c", h=4), copy)
                    act.activation(kTC[:, :, T:512], ps[:, 5, 0:256].rearrange("p (h c) -> p h c", h=2),
                                   copy).then_inc(tr_evac, 1)

            def pooling(l):
                act.wait_ge(pool_mm, l + 1)
                act.activation(pooled[:, :, :], ps[:, 0:4, 0:T], copy).then_inc(pool_ev, 1)
                act.wait_ge(pooly_mm, l + 1)
                for g in range(4):
                    x = act.activation(oraw[:, g, :], ps[:, 4 + g, 0:T], copy, scale=cols[:, l, R_PS + g:R_PS + g + 1])
                    x.then_inc(chain_p, 1)
                act.wait_ge(chain_p, 4 * (l + 1))
                act.activation(ohi[:, :, :], oraw[:, :, :], copy).then_inc(oh_done, 1)

            def attention(l, kind):
                st0, it0, per = 24 * l + 12 * kind, 36 * l + 12 * kind, 1 + kind

                def exps(t):
                    p, nk = t % 2, (P if t % 3 == 0 else T)
                    act.wait_ge(nmax_done, st0 + t + 1)
                    if t >= 2:
                        act.wait_ge(tp_done, it0 + per * (t - 1))
                    for m in range(2):
                        x = act.activation(ebuf[:, p, m, 0:nk], ps[:, 2 * p + m, 0:nk], ACT.Exp,
                                           bias=small[:, p, m:m + 1], accum_out=small[:, p, 2 + m:3 + m])
                    if kind == 1:
                        x = act.activation(small[:, p, 6:8], small[:, p, 4:6], ACT.Exp)
                    x.then_inc(e_done, 1)

                def pt_copy(i):
                    act.wait_ge(tp_done, it0 + i + 1)
                    n = it0 + i
                    if n >= 2:
                        act.wait_ge(pv_done, n - 1)
                    nk = P if (i // per) % 3 == 0 else T
                    act.activation(pt[:, n % 2, 0:nk], ps[:, 4 + n % 2, 0:nk], copy).then_inc(pt_evac, 1)

                def o_copy(h):
                    act.wait_ge(pv_done, it0 + 3 * per * (h + 1))
                    act.activation(oraw[:, h, :], ps[:, 6 + h % 2, 0:T], copy).then_inc(o_evac, 1)

                if kind == 0:
                    act.wait_ge(kv_out, 16 * 6 * (l + 1))
                    act.wait_ge(o_ready, 3 * l + 1)
                else:
                    act.wait_ge(o_ready, 3 * l + 2)
                exps(0)
                for t in range(12):
                    if t + 1 < 12:
                        exps(t + 1)
                    for m in range(per):
                        pt_copy(per * t + m)
                    if t % 3 == 0 and t >= 3:
                        o_copy(t // 3 - 1)
                o_copy(3)
                act.wait_ge(o_evac, 8 * l + 4 * kind + 4)
                if kind == 0:
                    act.activation(osq[:, :, :], oraw[:, :, :], ACT.Square).then_inc(osq_done, 1)
                    act.wait_ge(oss_done, l + 1)
                    act.activation(osq[:, :, :], ps[:, 0:4, 0:T], ACT.Sqrt, scale=1.0 / P, bias=epsc[:, 0:1]).then_inc(orms_done, 1)
                    act.wait_ge(on_done, l + 1)
                act.wait_ge(mm_done, branch_slot(l, kind, 1) + 1)
                act.activation(ohi[:, :, :], oraw[:, :, :], copy).then_inc(oh_done, 1)

            def gate_out(l, o, half, j):
                n = gate_slot(l, o, half, j)
                act.wait_ge(mm_done, n + 1)
                i = 6 * l + 2 * o + half
                if i:
                    act.wait_ge(merge_done, i)
                act.activation(gbuf[:, 2 * j:2 * j + 2, :], pair(n % 2), ACT.Sigmoid).then_inc(gate_evac, 1)

            def units(l):
                n0 = BASE[l] + N_MIX
                h0 = 0 if l == 0 else N_HALF * GU
                with act.Fori(0, N_HALF if l == 0 else N_EXP) as u:
                    def unit_hi(s):
                        act.wait_ge(raw_in[s % RING], u * (32 * UNIT // RING) + 32 * ((n0 + s) // RING + 1))
                        act.wait_ge(mm_done, u * UNIT + (n0 + s - RING + 1))
                        used = SLOT if s < GU else len(DOWN[s - GU]) * D
                        act.activation(whi[:, s % RING, 0:used], raw[:, s % RING, 0:used], copy).then_inc(hi_done, 1)

                    unit_hi(0)
                    unit_hi(1)
                    for s in range(UNIT):
                        if s + 2 < UNIT:
                            unit_hi(s + 2)
                        if s < GU:
                            act.wait_ge(mm_done, u * UNIT + (n0 + s + 1))
                            if s >= 2:
                                act.wait_ge(hid_done, u * GU + (h0 + s - 1))
                            act.activation(sil[:, s % 2, :], ps[:, 2 * (s % 2), 0:T], ACT.Silu).then_inc(sil_done, 1)

            act.wait_ge(x_tr, 1)
            act.activation(xT[:, :, :], ps[:, :, 0:T], copy).then_inc(x_ev, 1)
            act.wait_ge(v_tr, 1)
            act.activation(cols[:, :, :], ps[:, 4, 0:256].rearrange("p (l c) -> p l c", l=2)[:, :, 0:R_END],
                           copy).then_inc(v_ev, 1)
            act.wait_ge(v_ev, 1)
            act.activation(silc[:, :, :], cols[:, 0, R_C:R_FIN].rearrange("p (v k) -> p v k", v=2),
                           ACT.Silu).then_inc(silc_ready, 1)
            act.wait_ge(lam_sums, 1)
            act.activation(lamp[:, :, :], lamp[:, :, :], ACT.Exp).then_inc(v_ev, 1)
            act.wait_ge(x_ev, 1)
            for l in range(DEPTH):
                b0 = BASE[l]
                if l:
                    act.wait_ge(unit_done, 1 + N_HALF)
                square(2 * l)
                modulate(2 * l)
                hi(b0)
                hi(b0 + 1)
                for s in range(N_WIN):
                    hi(b0 + s + 2)
                    input_evac(l, s)
                    if s - 1 in STAGED:
                        turned_evac(l, STAGED.index(s - 1))
                turned_evac(l, 6)
                turned_evac(l, 7)
                pooling(l)
                for o in range(3):
                    if o:
                        attention(l, o - 1)
                    for half in range(2):
                        for j in range(2):
                            n = gate_slot(l, o, half, j)
                            hi(n + 2)
                            gate_out(l, o, half, j)
                        hi(branch_slot(l, o, half) + 2)
                act.wait_ge(merge_done, 6 * (l + 1))
                act.activation(hhi[:, :, :], macc[:, :, :], copy).then_inc(mh_done, 1)
                for j in range(4):
                    if j < 2:
                        hi(out_slot(l, j + 2))
                act.wait_ge(out_evac, 4 * (l + 1))
                square(2 * l + 1)
                modulate(2 * l + 1)
                if l == 1:
                    act.wait_ge(rt_sub, 1)
                    act.activation(rsm[:, :, 8:16], rsm[:, :, 0:8], ACT.Exp).then_inc(rt_exp, 1)
                    act.wait_ge(gb_done, 1)
                    act.activation(gbc[:, :, :], ps[:, :, 0:T], copy).then_inc(gbc_ready, 1)
                units(l)
            act.wait_ge(unit_done, 1 + N_HALF + N_EXP)
            square(2 * DEPTH)
            act.wait_ge(xn_done, 5)
            for k in range(KD):
                act.activation(macc[:, k, :], macc[:, k, :], copy, scale=cols[:, 0, R_FIN + k:R_FIN + k + 1]
                               ).then_inc(chain_m, 1)
            for b in range(BLK):
                act.wait_ge(y_tr, b + 1)
                act.activation(yout[:, b, :], ps[:, 2 * b:2 * b + 2, :].rearrange("p a c -> p (a c)"), copy
                               ).then_inc(y_ev, 1)
                act.wait_ge(y_ev, b + 1)
                dst = y_prompt[0] if b == 0 else y_sample[0, (b - 1) * P:b * P]
                act.dma_start(dst, yout[:, b, :]).then_inc(y_out, 16)
            act.wait_ge(y_out, 16 * BLK)
            act.wait_ge(kv_out, 16 * 6 * DEPTH)

        @block.vector
        def _(dve):
            count = [0]

            def link(ins):
                count[0] += 1
                ins.then_inc(chain_v, 1)
                dve.wait_ge(chain_v, count[0])

            def lo(n):
                dve.wait_ge(hi_done, n + 1)
                dve.tensor_tensor(wlo[:, n % RING, :], raw[:, n % RING, :], whi[:, n % RING, :].bitcast(F32),
                                  ALU.subtract).then_inc(lo_done, 1)

            def normalise(i):
                dve.wait_ge(rms_done, i + 1)
                link(dve.reciprocal(rstd[:, :], rstd[:, :]))
                dve.tensor_tensor(macc[:, :, :], xT[:, :, :], rstd[:, :].unsqueeze(1).to_broadcast([P, KD, T]),
                                  ALU.mult).then_inc(xn_done, 1)
                if i < 2 * DEPTH:
                    dve.wait_ge(hf_done, i + 1)
                    dve.tensor_tensor(hlo[:, :, :], macc[:, :, :], hhi[:, :, :].bitcast(F32),
                                      ALU.subtract).then_inc(h_ready, 1)

            def modulations(l):
                dve.wait_ge(ada_used, N_ADA * (l + 1))
                run = N_ADA if l == 0 else PER_WIDE
                for j in range(0, N_ADA, run):
                    b = cols[:, l, R_BADA + j:R_BADA + j + run].unsqueeze(2).to_broadcast([P, run, 2])
                    bank = 7 if l == 0 else 2 * (wide_slots(0)[j // PER_WIDE] % 2)
                    src = ps[:, bank, 384 + 2 * j:384 + 2 * (j + run)].rearrange("p (j v) -> p j v", v=2)
                    link(dve.tensor_tensor(mods[:, l, j:j + run, :], src, b, ALU.add))
                for which, (sc, g) in enumerate(((SC1, R_N1), (SC2, R_N2))):
                    link(dve.tensor_scalar(amul[:, l, which], mods[:, l, sc:sc + KD, :], 1.0, None, ALU.add))
                    link(dve.tensor_tensor(amul[:, l, which], amul[:, l, which],
                                           cols[:, l, g:g + KD].unsqueeze(2).to_broadcast([P, KD, 2]), ALU.mult))
                lam_init = 0.8 - 0.6 * math.exp(-0.3 * l)
                link(dve.tensor_scalar(subg[:, l:l + 1], cols[:, l, R_SUB:R_SUB + 1], 1.0 - lam_init, None, ALU.mult))

            def rotate(l, ti):
                s = STAGED[ti]
                dve.wait_ge(win_evac, WIN_INC * l + s + 1 + (s == 10))
                heads = 2 if s == 10 else 4
                for b in range(2):
                    x = stage[:, ti % 2, b + 1, 0:heads * 64].rearrange("p (h s f i) -> p h s f i", h=heads, s=2, f=2)
                    co, si = (rope[:, b, c, :].rearrange("p (s i) -> p s i", s=2).unsqueeze(1)
                              .to_broadcast([P, heads, 2, 16]) for c in range(2))
                    t1, t2 = (rope_t[:, i, 0:heads * 32].rearrange("p (h s i) -> p h s i", h=heads, s=2)
                              for i in range(2))
                    a1, a2 = x[:, :, :, 0, :], x[:, :, :, 1, :]
                    dve.tensor_tensor(t1, a2, si, ALU.mult)
                    link(dve.tensor_tensor(t2, a1, si, ALU.mult))
                    dve.tensor_tensor(a1, a1, co, ALU.mult)
                    link(dve.tensor_tensor(a2, a2, co, ALU.mult))
                    dve.tensor_tensor(a1, a1, t1, ALU.subtract)
                    x = dve.tensor_tensor(a2, a2, t2, ALU.add)
                    if b == 0 or ti == 6:
                        link(x)
                    else:
                        x.then_inc(rope_done, 1)
                        dve.wait_ge(rope_done, len(STAGED) * l + ti + 1)
                if ti == 6:
                    src = stage[:, ti % 2, :, 0:P]
                    for g in range(2):
                        for i in range(2):
                            x = dve.tensor_copy(kcd[:, :, g * P + i * 64:g * P + i * 64 + 64], src[:, :, g * 64:g * 64 + 64])
                            if g == 1 and i == 1:
                                x.then_inc(rope_done, 1)

            def attention(l, kind):
                st0 = 24 * l + 12 * kind

                def maxima(t):
                    p, nk = t % 2, (P if t % 3 == 0 else T)
                    dve.wait_ge(s_done, st0 + t + 1)
                    x = dve.tensor_reduce(small[:, p, 0:2], ps[:, 2 * p:2 * p + 2, 0:nk], X, ALU.max, negate=True)
                    if kind == 1:
                        hp = t // 3
                        link(x)
                        link(dve.tensor_tensor(small[:, p, 0:2], small[:, p, 0:2], nsink[:, l, 2 * hp:2 * hp + 2], ALU.min))
                        x = dve.tensor_tensor(small[:, p, 4:6], small[:, p, 0:2], sinkr[:, l, 2 * hp:2 * hp + 2], ALU.add)
                    x.then_inc(nmax_done, 1)

                def normal(t):
                    p, nk = t % 2, (P if t % 3 == 0 else T)
                    dve.wait_ge(e_done, st0 + t + 1)
                    e = [ebuf[:, p, m, 0:nk] for m in range(2)]
                    if kind == 1:
                        link(dve.tensor_tensor(small[:, p, 2:4], small[:, p, 2:4], small[:, p, 6:8], ALU.add))
                    link(dve.reciprocal(small[:, p, 8:10], small[:, p, 2:4]))
                    if kind == 0:
                        link(dve.tensor_scalar(small[:, p, 9:10], small[:, p, 9:10], neglam[:, l:l + 1], None, ALU.mult))
                        link(dve.tensor_scalar(e[0], e[0], small[:, p, 8:9], None, ALU.mult))
                        dve.scalar_tensor_tensor(e[0], e[1], small[:, p, 9:10], e[0], ALU.mult, ALU.add).then_inc(p_done, 1)
                    else:
                        dve.tensor_scalar(e[0], e[0], small[:, p, 8:9], None, ALU.mult)
                        dve.tensor_scalar(e[1], e[1], small[:, p, 9:10], None, ALU.mult).then_inc(p_done, 1)

                maxima(0)
                for t in range(12):
                    if t + 1 < 12:
                        maxima(t + 1)
                    normal(t)
                if kind == 0:
                    dve.wait_ge(orms_done, l + 1)
                    link(dve.reciprocal(osq[:, :, :], osq[:, :, :]))
                    dve.scalar_tensor_tensor(oraw[:, :, :].rearrange("p a b -> p (a b)"),
                                             oraw[:, :, :].rearrange("p a b -> p (a b)"), subg[:, l:l + 1],
                                             osq[:, :, :].rearrange("p a b -> p (a b)"), ALU.mult, ALU.mult
                                             ).then_inc(on_done, 1)

            def o_low(l, o):
                dve.wait_ge(oh_done, 3 * l + o + 1)
                dve.tensor_tensor(olo[:, :, :], oraw[:, :, :], ohi[:, :, :].bitcast(F32), ALU.subtract).then_inc(o_ready, 1)

            def merge(l, o, half):
                dve.wait_ge(mm_done, branch_slot(l, o, half) + 1)
                dve.wait_ge(gate_evac, 12 * l + 4 * o + 2 * half + 2)
                dst = macc[:, 4 * half:4 * half + 4, :]
                if o == 0:
                    dve.tensor_tensor(dst, gbuf[:, :, :], ps[:, 4:8, 0:T], ALU.mult).then_inc(merge_done, 1)
                else:
                    link(dve.tensor_tensor(gbuf[:, :, :], gbuf[:, :, :], ps[:, 4:8, 0:T], ALU.mult))
                    dve.tensor_tensor(dst, dst, gbuf[:, :, :], ALU.add).then_inc(merge_done, 1)

            def residual(l, n, j):
                dve.wait_ge(mm_done, n + 1)
                for c in range(2):
                    m = 2 * j + c
                    for v, t in ((0, slice(P, T)), (1, slice(0, P))):
                        x = dve.scalar_tensor_tensor(xT[:, m, t], ps[:, 2 * (n % 2) + c, t], mods[:, l, G1 + m, v:v + 1],
                                                     xT[:, m, t], ALU.mult, ALU.add)
                x.then_inc(out_evac, 1)

            def router():
                lg = rsm[:, :, 0:8]
                dve.wait_ge(rt_done, 1)
                link(dve.tensor_copy(lg, ps[:, 6, 0:BLK * 8].rearrange("p (b e) -> p b e", b=BLK)))
                mx = small[:, 0, 0:BLK]
                for b in range(BLK):
                    mine = rsm[:, b, 0:8].unsqueeze(2).to_broadcast([P, 8, 8])
                    other = rsm[:, b, 0:8].unsqueeze(1).to_broadcast([P, 8, 8])
                    gt = rcmp[:, 0, b, :].rearrange("p (e j) -> p e j", e=8)
                    eq = rcmp[:, 1, b, :].rearrange("p (e j) -> p e j", e=8)
                    dve.tensor_tensor(gt, other, mine, ALU.is_gt)
                    link(dve.tensor_tensor(eq, other, mine, ALU.is_equal))
                    link(dve.tensor_tensor(eq, eq, tri.rearrange("p (e j) -> p e j", e=8), ALU.mult))
                    link(dve.tensor_tensor(gt, gt, eq, ALU.add))
                    link(dve.tensor_reduce(gates[:, b, :], gt, X, ALU.add))
                    link(dve.tensor_scalar(gates[:, b, :], gates[:, b, :], 1.5, None, ALU.is_lt))
                link(dve.tensor_reduce(mx, lg, X, ALU.max))
                dve.tensor_tensor(lg, lg, mx.unsqueeze(2).to_broadcast([P, BLK, 8]), ALU.subtract).then_inc(rt_sub, 1)
                dve.wait_ge(rt_exp, 1)
                link(dve.tensor_tensor(gates[:, :, :], gates[:, :, :], rsm[:, :, 8:16], ALU.mult))
                link(dve.tensor_reduce(mx, gates[:, :, :], X, ALU.add))
                link(dve.reciprocal(mx, mx))
                dve.tensor_tensor(gates[:, :, :], gates[:, :, :], mx.unsqueeze(2).to_broadcast([P, BLK, 8]),
                                  ALU.mult).then_inc(gates_ready, 1)

            def units(l):
                n0 = BASE[l] + N_MIX
                h0 = 0 if l == 0 else N_HALF * GU
                per = 2 + (l == 1)
                c0 = 0 if l == 0 else N_HALF * GU * 2
                with dve.Fori(0, N_HALF if l == 0 else N_EXP) as u:
                    def unit_lo(s):
                        used = SLOT if s < GU else len(DOWN[s - GU]) * D
                        dve.wait_ge(hi_done, u * UNIT + (n0 + s + 1))
                        dve.tensor_tensor(wlo[:, s % RING, 0:used], raw[:, s % RING, 0:used],
                                          whi[:, s % RING, 0:used].bitcast(F32), ALU.subtract).then_inc(lo_done, 1)

                    def hop(ins, s, i):
                        ins.then_inc(chain_u, 1)
                        dve.wait_ge(chain_u, u * (GU * per) + (c0 + s * per + i))

                    unit_lo(0)
                    unit_lo(1)
                    for s in range(UNIT):
                        if s + 2 < UNIT:
                            unit_lo(s + 2)
                        if s < GU:
                            dve.wait_ge(sil_done, u * GU + (h0 + s + 1))
                            hop(dve.tensor_tensor(val[:, s % 2, :], sil[:, s % 2, :], ps[:, 2 * (s % 2) + 1, 0:T], ALU.mult), s, 1)
                            if l == 1:
                                hop(dve.tensor_tensor(val[:, s % 2, :], val[:, s % 2, :], gbc[:, bass.ds(u, 1), :].rearrange("p a t -> p (a t)"), ALU.mult), s, 2)
                            hop(dve.tensor_copy(hidhi[:, s, :], val[:, s % 2, :]), s, per)
                            dve.tensor_tensor(hidlo[:, s, :], val[:, s % 2, :], hidhi[:, s, :].bitcast(F32),
                                              ALU.subtract).then_inc(hid_done, 1)
                    dve.wait_ge(mm_done, u * UNIT + (n0 + UNIT))
                    for m in range(KD):
                        for v, t, src in ((0, slice(P, T), ps[:, 2 + m // 2, (m % 2) * 256:(m % 2 + 1) * 256]),
                                          (1, slice(0, P), ps[:, 6 + m // 4, (m % 4) * P:(m % 4 + 1) * P])):
                            x = dve.scalar_tensor_tensor(xT[:, m, t], src, mods[:, l, G2 + m, v:v + 1], xT[:, m, t],
                                                         ALU.mult, ALU.add)
                    x.then_inc(unit_done, 1)

            dve.memset(rope_t[:, :, :], 0.0).then_inc(unit_done, 1)
            dve.wait_ge(init_in, 16 * n_init)
            link(dve.tensor_tensor(lamprod[:, :, :], lamrow[:, :, 0, :], lamrow[:, :, 1, :], ALU.mult))
            link(dve.tensor_reduce(lamp[:, :, :].rearrange("p l i -> p (l i)"), lamprod[:, :, :], X, ALU.add))
            dve.tensor_scalar(nsink[:, :, :], sinkr[:, :, :], -1.0, None, ALU.mult).then_inc(lam_sums, 1)
            dve.wait_ge(v_ev, 2)
            link(dve.tensor_tensor(neglam[:, :], lamp[:, :, 1], lamp[:, :, 0], ALU.subtract))
            for l in range(DEPTH):
                dve.tensor_scalar(neglam[:, l:l + 1], neglam[:, l:l + 1], -(0.8 - 0.6 * math.exp(-0.3 * l)), None,
                                  ALU.add).then_inc(lam_done, 1)
            dve.wait_ge(lam_done, DEPTH)
            modulations(0)
            for l in range(DEPTH):
                b0 = BASE[l]
                normalise(2 * l)
                lo(b0)
                lo(b0 + 1)
                for s in range(N_WIN):
                    lo(b0 + s + 2)
                    if s in STAGED:
                        rotate(l, STAGED.index(s))
                o_low(l, 0)
                for o in range(3):
                    if o:
                        attention(l, o - 1)
                        o_low(l, o)
                    for half in range(2):
                        for j in range(2):
                            lo(gate_slot(l, o, half, j) + 2)
                        lo(branch_slot(l, o, half) + 2)
                        merge(l, o, half)
                dve.wait_ge(mh_done, l + 1)
                dve.tensor_tensor(hlo[:, :, :], macc[:, :, :], hhi[:, :, :].bitcast(F32), ALU.subtract).then_inc(merged_ready, 1)
                for j in range(4):
                    if j < 2:
                        lo(out_slot(l, j + 2))
                    residual(l, out_slot(l, j), j)
                if l == 0:
                    modulations(1)
                normalise(2 * l + 1)
                if l == 1:
                    router()
                units(l)
            normalise(2 * DEPTH)


_INS = ["x_prompt", "x_sample", "cache_diff_k", "cache_diff_v", "cache_win_k", "cache_win_v", "c", "c_ctx",
        "w_ada", "b_ada", "norm1_g", "norm2_g", "w_in", "w_gate", "lam_p", "subln_g", "w_pool", "pool_scale",
        "sink", "w_branch", "w_out", "w_ff_gate", "w_ff_up", "w_ff_down", "w_router", "w_ex_gate", "w_ex_up",
        "w_ex_down", "final_g"]
_OUTS = [(1, 128, 1024), (1, 256, 1024), (1, 2, 128, 4, 2, 64), (1, 2, 128, 4, 128), (1, 2, 128, 2, 64),
         (1, 2, 128, 2, 64)]


def kernel(**inputs):
    import concourse.bacc as _bacc
    from concourse.bass_utils import run_bass_kernel_spmd as _run

    nc = _bacc.Bacc("TRN2", target_bir_lowering=False, num_devices=1)
    arrays, args = {}, {}
    for name in _INS:
        x = np.ascontiguousarray(inputs[name])
        arrays[f"in_{name}_dram"] = x
        args[name] = nc.dram_tensor(f"in_{name}_dram", x.shape, mybir.dt.from_np(x.dtype), kind="ExternalInput").ap()
    const = shape_constants()
    arrays["shape_constants_dram"] = const
    cap = nc.dram_tensor("shape_constants_dram", const.shape, F32, kind="ExternalInput").ap()
    outs = [nc.dram_tensor(f"out_{i}_dram", s, F32, kind="ExternalOutput").ap() for i, s in enumerate(_OUTS)]
    prefix_step_kernel(nc, args, outs, cap)
    r = _run(nc, [arrays], core_ids=[0])
    return tuple(r.results[0][f"out_{i}_dram"] for i in range(len(_OUTS)))
```

```python
import math
from contextlib import ExitStack

import numpy as np
import concourse.bass as bass
from concourse import mybir

F32 = mybir.dt.float32
F32R = mybir.dt.float32r
ALU = mybir.AluOpType
ACT = mybir.ActivationFunctionType
X = mybir.AxisListType.X

P = 128
D = 1024
KD = D // P
DEPTH = 2
BLK = 3
T = BLK * P
GRID_W = 64
HA, DHA = 4, 64
HC, KVC, DHC = 8, 2, 64
WINDOWS = (2, 4, 8, 16)
EPS = 1e-6
NEG = -1e30
A_COLS = HA * 2 * DHA
IN_W = 3 * A_COLS + 512 + HC * DHC + 2 * KVC * DHC
D_FF = 2816
F_U = 1408
KF = F_U // P
N_EXP = 8
N_HALF = D_FF // F_U
CAP = 160
MAX_ROUNDS = -(-T // CAP)
CW = KD * CAP

RING = 3
SLOT = 16 * P
N_WIN = IN_W // 256
ORDER = (1, 0, 2)
N_MIX = N_WIN + 3 * 6 + 4
GU = KF
DOWN = ((0, 1), (2, 3), (4, 5), (6, 7), (8,), (9,), (10,))
UNIT = GU + len(DOWN)
assert N_MIX % RING == 0 and UNIT % RING == 0
BASE = (0, N_MIX + N_HALF * UNIT)
STAGED = (0, 1, 2, 3, 8, 9, 10)
WIN_INC = N_WIN + 1
KV_SLOTS = (2, 3, 4, 5, 10)
N_TR = len(STAGED) + 1
N_ADA = 6 * D // P
ADA_RING = 2

R_BADA, R_N1, R_N2, R_PS, R_SUB, R_C, R_CTX, R_FIN, R_END = 0, 48, 56, 64, 68, 69, 77, 85, 93
SH1, SC1, G1, SH2, SC2, G2 = (8 * i for i in range(6))


def shape_constants():
    ident = np.eye(P, dtype=np.float32)
    pool = np.zeros((P, 4, T + 2 * P), np.float32)

    def mean_minus_self(n, w):
        m = np.zeros((n, n), np.float32)
        for t in range(n):
            lo, hi = max(t - w // 2, 0), min(t + w - w // 2, n)
            m[lo:hi, t] = np.float32(1.0) / np.float32(hi - lo)
            m[t, t] -= 1.0
        return m

    for g, w in enumerate(WINDOWS):
        pool[:, g, 0:P] = mean_minus_self(P, w)
        m = mean_minus_self(2 * P, w)
        pool[:, g, P:P + 256] = m[0:P]
        pool[:, g, P + 256:P + 512] = m[P:256]
    q = np.arange(P)
    mask = np.zeros((P, 2, P), np.float32)
    mask[:, 0, :] = np.where(q[None, :] <= q[:, None], 0.0, NEG)
    mask[:, 1, :] = np.where(q[None, :] >= q[:, None], 0.0, NEG)
    inv = 10000.0 ** (-np.arange(0, 32, 2, dtype=np.float32) / np.float32(32))
    t = np.arange(2 * P)
    ang = np.stack([(t // GRID_W)[:, None] * inv, (t % GRID_W)[:, None] * inv], 1).astype(np.float32)
    rope = np.zeros((P, 2, 2, 32), np.float32)
    for b in range(2):
        a = ang[b * P:(b + 1) * P].reshape(P, 32)
        rope[:, b, 0], rope[:, b, 1] = np.cos(a), np.sin(a)
    tri = np.zeros((P, 8, 8), np.float32)
    tri[:] = (np.arange(8)[None, :] < np.arange(8)[:, None])
    before = (q[:, None] < q[None, :]).astype(np.float32)
    slots = np.broadcast_to(np.arange(CAP, dtype=np.float32), (P, CAP))
    slot_of_row = np.stack([q, q + P], 1).astype(np.float32)
    return np.concatenate([ident, mask.reshape(P, 256), rope.reshape(P, 128), tri.reshape(P, 64),
                           pool.reshape(P, -1), before, slots, slot_of_row], 1).astype(np.float32)


C_MASK, C_ROPE, C_TRI, C_POOL = 128, 384, 512, 576
POOL_COLS = 4 * (T + 2 * P)
C_SLOT = C_POOL + POOL_COLS
SLOT_COLS = P + CAP + 2


def prefix_step_kernel(nc, a, outs, const):
    y_prompt, y_sample, new_dk, new_dv, new_wk, new_wv = outs
    ctx = ExitStack()
    with ctx:
        top = [(nc.sbuf_base + 31) // 32 * 32]
        sb_end = nc.sbuf_base + nc.sbuf_bytes_remaining

        def at(name, cols, offset, dt=F32, shape=None):
            return nc.alloc_sbuf_tensor_at(name, [P] + list(shape or [cols]), dt, offset=offset)

        def place(name, shape, dt=F32):
            n = int(np.prod(shape)) * 4
            t = nc.alloc_sbuf_tensor_at(name, [P] + list(shape), dt, offset=top[0])
            top[0] += (n + 31) // 32 * 32
            return t

        def sem(name):
            return ctx.enter_context(nc.semaphore(name))

        raw = place("raw", [RING, SLOT])
        whi = place("whi", [RING, SLOT], F32R)
        wlo = place("wlo", [RING, SLOT], F32R)
        ada_at = top[0]
        ada = place("ada", [ADA_RING, KD, P])
        xT = place("xT", [KD, T])
        hhi = place("hhi", [KD, T], F32R)
        hlo = place("hlo", [KD, T], F32R)
        scratch_at = top[0]
        macc = place("macc", [KD, T])
        gbuf_at = top[0]
        gbuf = place("gbuf", [4, T])
        oraw_at = top[0]
        oraw = place("oraw", [4, T])
        ohi_at = top[0]
        ohi = place("ohi", [4, T], F32R)
        olo_at = top[0]
        olo = place("olo", [4, T], F32R)
        rstd = place("rstd", [T])
        cst = place("cst", [C_POOL])
        ones = place("ones", [P])
        epsc = place("epsc", [1])
        wpool = place("wpool", [4, P])
        wrout = place("wrout", [KD, N_EXP])
        cols = place("cols", [DEPTH, R_END])
        silc = place("silc", [2, KD])
        mods = place("mods", [DEPTH, N_ADA, 2])
        amul = place("amul", [DEPTH, 2, KD, 2])
        subg = place("subg", [DEPTH])
        sinkr = place("sinkr", [DEPTH, HC])
        nsink = place("nsink", [DEPTH, HC])
        lamp = place("lamp", [DEPTH, 2])
        neglam = place("neglam", [DEPTH])
        small = place("small", [2, 10])
        rsm = place("rsm", [BLK, 16])
        gates = place("gates", [BLK, N_EXP])
        posx = place("posx", [BLK, N_EXP + 1])
        gwx = place("gwx", [BLK, N_EXP + 1])
        gws = place("gws", [2, 2])
        rounds = nc.alloc_sbuf_tensor_at("rounds", [P, 1], mybir.dt.int32, offset=top[0])
        top[0] += 32
        shared = top[0]
        vtok = place("vtok", [BLK, 640])
        utok = place("utok", [BLK, 512])
        qTA = place("qTA", [4, T])
        kTA = place("kTA", [4, 512])
        qTC = place("qTC", [4, T])
        kTC = place("kTC", [2, 512])
        stage = place("stage", [2, BLK, 256])
        ctxv = place("ctxv", [640])
        assert top[0] <= sb_end, (top[0], sb_end)
        pt = at("pt", 2 * T, stage_off := top[0] - 2560 - 2 * BLK * 256 * 4, shape=[2, T])
        pooled = at("pooled", 4 * T, gbuf_at, shape=[4, T])
        ebuf = at("ebuf", 4 * T, gbuf_at, shape=[2, 2, T])
        osq = at("osq", 4 * T, gbuf_at, shape=[4, T])
        ctxk = at("ctxk", 768, gbuf_at, shape=[768])
        kcd = at("kcd", 768, gbuf_at + 3072, shape=[BLK, 256])
        vrows = at("vrows", 2 * P, gbuf_at, shape=[DEPTH, P])
        lamrow = at("lamrow", 512, gbuf_at + 1024, shape=[DEPTH * 2, 2, DHA])
        lamprod = at("lamprod", 256, gbuf_at + 3072, shape=[DEPTH * 2, DHA])
        xtok = at("xtok", BLK * D, scratch_at, shape=[BLK, D])
        poolm = at("poolm", POOL_COLS, scratch_at, shape=[4, T + 2 * P])
        hidhi = at("hidhi", KF * T, shared, F32R, [KF, T])
        hidlo = at("hidlo", KF * T, shared + KF * T * 4, F32R, [KF, T])
        sil = at("sil", 2 * T, shared + 2 * KF * T * 4, shape=[2, T])
        val = at("val", 2 * T, shared + 2 * KF * T * 4 + 3072, shape=[2, T])
        prow = at("prow", N_EXP * T, scratch_at, shape=[N_EXP, T])
        gat = at("gat", BLK * CAP + 96, ohi_at, F32R)
        sct = at("sct", 2 * T, ohi_at + 2304, F32R, [2, T])
        xgh = at("xgh", CW, olo_at, F32R)
        ysb = at("ysb", CW + 96, oraw_at)
        yhi = at("yhi", 2 * D, ada_at, F32R, [2, D])
        ehh = at("ehh", KF * CAP, shared, F32R, [KF, CAP])
        ehl = at("ehl", KF * CAP, shared + 4 * KF * CAP, F32R, [KF, CAP])
        xgl = at("xgl", CW, shared + 8 * KF * CAP, F32R)
        ylo = at("ylo", 2 * D, shared + 8 * KF * CAP + 4 * CW, F32R, [2, D])
        esil = at("esil", 2 * CAP, gbuf_at + 1536, shape=[2, CAP])
        evalu = at("evalu", 2 * CAP, gbuf_at + 1536 + 8 * CAP, shape=[2, CAP])
        slotc = at("slotc", SLOT_COLS, gbuf_at + 1536 + 16 * CAP)
        assert 1536 + 16 * CAP + 4 * SLOT_COLS <= 4 * 4 * T and 2304 + 8 * T <= 4 * 4 * T
        htok = [x[:, :, :].rearrange("p k t -> p (k t)").rearrange("p (b d) -> p b d", b=BLK) for x in (hhi, hlo)]
        yout = at("yout", BLK * D, shared, shape=[BLK, D])
        rcmp = at("rcmp", 2 * BLK * 64, gbuf_at, shape=[2, BLK, 64])
        rope_t = at("rope_t", 256, oraw_at, shape=[2, 128])
        assert top[0] <= sb_end, (top[0], sb_end)
        assert shared + 2 * KF * T * 4 + 6144 <= sb_end

        ident = cst[:, 0:P]
        mask = cst[:, C_MASK:C_ROPE].rearrange("p (i k) -> p i k", i=2)
        rope = cst[:, C_ROPE:C_TRI].rearrange("p (b c i) -> p b c i", b=2, c=2)
        tri = cst[:, C_TRI:C_POOL]
        ps = ctx.enter_context(nc.psum_tensor("ps", [P, 8, 512], F32))

        def pair(g):
            return ps[:, 2 * g:2 * g + 2, 0:T]

        raw_in = [sem(f"raw_in{j}") for j in range(RING)]
        hi_done, lo_done, mm_done = sem("hi_done"), sem("lo_done"), sem("mm_done")
        ada_in = [sem(f"ada_in{j}") for j in range(ADA_RING)]
        ada_used, ada_read = sem("ada_used"), sem("ada_read")
        mods_ready = sem("mods_ready")
        init_in, ones_set = sem("init_in"), sem("ones_set")
        x_tr, x_ev, v_tr, v_ev, silc_ready = sem("x_tr"), sem("x_ev"), sem("v_tr"), sem("v_ev"), sem("silc_ready")
        sq_done, ssq_done, xn_done, hf_done = sem("sq_done"), sem("ssq_done"), sem("xn_done"), sem("hf_done")
        h_ready, hh_done = sem("h_ready"), sem("hh_done")
        win_evac, rope_done, tr_done, tr_evac = sem("win_evac"), sem("rope_done"), sem("tr_done"), sem("tr_evac")
        layer_in = [sem(f"layer_in{l}") for l in range(DEPTH)]
        poolm_in, kv_out = sem("poolm_in"), sem("kv_out")
        pool_mm, pool_ev, pooly_mm = sem("pool_mm"), sem("pool_ev"), sem("pooly_mm")
        s_done, nmax_done, e_done, p_done = sem("s_done"), sem("nmax_done"), sem("e_done"), sem("p_done")
        tp_done, pt_evac, pv_done, o_evac = sem("tp_done"), sem("pt_evac"), sem("pv_done"), sem("o_evac")
        osq_done, oss_done, on_done = sem("osq_done"), sem("oss_done"), sem("on_done")
        oh_done, o_ready = sem("oh_done"), sem("o_ready")
        gate_evac, merge_done = sem("gate_evac"), sem("merge_done")
        mh_done, merged_ready, out_evac = sem("mh_done"), sem("merged_ready"), sem("out_evac")
        rt_done, gates_ready, sel_ready = sem("rt_done"), sem("gates_ready"), sem("sel_ready")
        h2_tr, h2_hi, h2_lo, slotc_in, pos_mm = sem("h2_tr"), sem("h2_hi"), sem("h2_lo"), sem("slotc_in"), sem("pos_mm")
        pos_ready, prow_mm, prow_ready, exp_init = sem("pos_ready"), sem("prow_mm"), sem("prow_ready"), sem("exp_init")
        gat_ready, gather_done, xgh_done, xg_ready = sem("gat_ready"), sem("gather_done"), sem("xgh_done"), sem("xg_ready")
        esil_done, ehid_done, ysb_done, gws_moved = sem("esil_done"), sem("ehid_done"), sem("ysb_done"), sem("gws_moved")
        yt_done, yh_done, yl_done = sem("yt_done"), sem("yh_done"), sem("yl_done")
        sc_done, sc_evac, sct_ready, round_done = sem("sc_done"), sem("sc_evac"), sem("sct_ready"), sem("round_done")
        chain_e = sem("chain_e")
        sil_done, hid_done, unit_done = sem("sil_done"), sem("hid_done"), sem("unit_done")
        y_tr, y_ev, y_out = sem("y_tr"), sem("y_ev"), sem("y_out")
        chain_v, chain_u, chain_m = sem("chain_v"), sem("chain_u"), sem("chain_m")
        rms_done, orms_done = sem("rms_done"), sem("orms_done")
        lam_done, lam_sums, chain_p = sem("lam_done"), sem("lam_sums"), sem("chain_p")
        rt_sub, rt_exp, wrout_in = sem("rt_sub"), sem("rt_exp"), sem("wrout_in")

        n_init = 3 + 8 * DEPTH + 2

        def gate_slot(l, o, half, j):
            return BASE[l] + N_WIN + 6 * o + 3 * half + j

        def branch_slot(l, o, half):
            return gate_slot(l, o, half, 2)

        def out_slot(l, j):
            return BASE[l] + N_WIN + 18 + j

        GATES = [gate_slot(0, o, half, j) for o in range(3) for half in range(2) for j in range(2)]
        PER_GATE = N_ADA // len(GATES)

        def ada_bank(l, j):
            if l == 0:
                return 7
            return 2 * (GATES[j // PER_GATE] % 2) + (j % PER_GATE < PER_GATE // 2)

        def ada_ps(l, j, n=1):
            return ps[:, ada_bank(l, j), 384 + 2 * j:384 + 2 * (j + n)]

        def raw_wait(eng, n, more=0):
            eng.wait_ge(raw_in[n % RING], more + 32 * (n // RING + 1))

        block = ctx.enter_context(nc.Block())

        @block.sync
        def _(sp):
            def halves(n, dst, src, axis_cols=None):
                if n >= RING:
                    sp.wait_ge(lo_done, n - RING + 1)
                for i in range(2):
                    sp.dma_start(dst[i], src[i]).then_inc(raw_in[n % RING], 16)

            def k_by_cols(n, w, k, c0, width):
                d = raw[:, n % RING, 0:k * width].rearrange("p (k c) -> p k c", k=k)
                s = w.rearrange("(k p) c -> p k c", p=P)[:, :, c0:c0 + width]
                halves(n, [d[:, 0:k // 2], d[:, k // 2:k]], [s[:, 0:k // 2], s[:, k // 2:k]])
                if n - 2 in GATES:
                    modulation(1, PER_GATE * GATES.index(n - 2), PER_GATE)

            def unit_slot(w, s):
                j = s % RING
                if s < GU:
                    d = raw[:, j, :].rearrange("p (w k c) -> p w k c", w=2, k=KD)
                    pieces = [(d[:, i], w[i][:, :, s * P:(s + 1) * P]) for i in range(2)]
                else:
                    f = DOWN[s - GU]
                    d = raw[:, j, 0:len(f) * D].rearrange("p (k c) -> p k c", c=D)
                    h = D // 2
                    pieces = [(d[:, :, i * h:(i + 1) * h], w[2][:, f[0]:f[-1] + 1, i * h:(i + 1) * h])
                              for i in range(2)]
                for dst, src in pieces:
                    sp.dma_start(dst, src).then_inc(raw_in[j], 16)

            def modulation(l, first, count):
                w = a["w_ada"][l].rearrange("(k p) c -> p k c", p=P)
                for j in range(first, first + count):
                    n = l * N_ADA + j
                    if n >= ADA_RING:
                        sp.wait_ge(ada_used, n - ADA_RING + 1)
                    sp.dma_start(ada[:, n % ADA_RING], w[:, :, j * P:(j + 1) * P]).then_inc(ada_in[n % ADA_RING], 16)

            sp.dma_start(cst[:, :], const[:, 0:C_POOL]).then_inc(init_in, 16)
            sp.dma_start(xtok[:, 0, :], a["x_prompt"][0]).then_inc(init_in, 16)
            sp.dma_start(xtok[:, 1:3, :], a["x_sample"][0].rearrange("(b p) d -> p b d", p=P)).then_inc(init_in, 16)
            for l in range(DEPTH):
                for r, src in ((R_BADA, a["b_ada"][l]), (R_N1, a["norm1_g"][l]), (R_N2, a["norm2_g"][l]),
                               (R_PS, a["pool_scale"][l]), (R_SUB, a["subln_g"][l]), (R_C, a["c"][0]),
                               (R_CTX, a["c_ctx"]), (R_FIN, a["final_g"])):
                    rows = src.shape[0] // P
                    sp.dma_start(vrows[r:r + rows, l, :], src.rearrange("(r c) -> r c", c=P)).then_inc(init_in, 16)
            sp.dma_start(lamrow[:, :, :].rearrange("p a b c -> p (a b c)"),
                         a["lam_p"].rearrange("(o l) r d -> o (l r d)", o=1).to_broadcast([P, DEPTH * 4 * DHA])
                         ).then_inc(init_in, 16)
            sp.dma_start(sinkr[:, :, :].rearrange("p l h -> p (l h)"),
                         a["sink"].rearrange("(o l) h -> o (l h)", o=1).to_broadcast([P, DEPTH * HC])
                         ).then_inc(init_in, 16)
            modulation(0, 0, N_ADA)
            for l in range(DEPTH):
                for s in range(N_WIN):
                    k_by_cols(BASE[l] + s, a["w_in"][l], KD, 256 * s, 256)
                for o, br in enumerate(ORDER):
                    for half in range(2):
                        for j in range(2):
                            k_by_cols(gate_slot(l, o, half, j), a["w_gate"][l], KD,
                                      br * D + 512 * half + 256 * j, 256)
                        k_by_cols(branch_slot(l, o, half), a["w_branch"][l, br], 4, 512 * half, 512)
                for j in range(4):
                    k_by_cols(out_slot(l, j), a["w_out"][l], KD, 256 * j, 256)
                if l == 0:
                    n0 = BASE[l] + N_MIX
                    with sp.Fori(0, N_HALF) as u:
                        w = [x.rearrange("(k p) c -> p k c", p=P) for x in (
                            a["w_ff_gate"][0][:, bass.ds(u * F_U, F_U)], a["w_ff_up"][0][:, bass.ds(u * F_U, F_U)],
                            a["w_ff_down"][0][bass.ds(u * F_U, F_U), :])]
                        for s in range(UNIT):
                            sp.wait_ge(lo_done, u * UNIT + (n0 + s - RING + 1))
                            unit_slot(w, s)
            n0 = BASE[1] + N_MIX

            def expert(e):
                return [a[f"w_ex_{x}"][0, e].rearrange("(k p) c -> p k c", p=P) if isinstance(e, int) else
                        a[f"w_ex_{x}"][0, bass.ds(e, 1)].rearrange("e (k p) c -> p (e k) c", p=P)
                        for x in ("gate", "up", "down")]

            for s in range(RING):
                sp.wait_ge(lo_done, n0 + s - RING + 1)
                unit_slot(expert(0), s)
            sp.wait_ge(pos_ready, 1)
            n_rounds = sp.value_load(rounds[0:1, 0:1], min_val=1, max_val=MAX_ROUNDS)
            with sp.Fori(0, n_rounds) as r:
                with sp.Fori(0, N_EXP) as e:
                    w, after = expert(e), expert(sp.snap((e + 1) % N_EXP, min_val=0, max_val=N_EXP - 1))
                    for s in range(UNIT):
                        ahead = s == GU - RING - 1
                        if s != GU - RING:
                            sp.wait_ge(lo_done, r * (N_EXP * UNIT) + e * UNIT + (n0 + s + ahead + 1))
                        unit_slot(w if s + RING < UNIT else after, (s + RING) % UNIT)
        @block.gpsimd
        def _(pool):
            pool.memset(epsc[:, :], EPS)
            pool.memset(ones[:, :], 1.0).then_inc(ones_set, 1)

            def layer_loads(l):
                if l == 0:
                    pool.wait_ge(v_ev, 2)
                    pool.wait_ge(lam_done, DEPTH)
                else:
                    pool.wait_ge(merge_done, 6 * l)
                ck = a["cache_win_k"][0, l].rearrange("t g d -> t (g d)")
                pool.dma_start(ctxk[:, 0:512], a["cache_diff_k"][0, l].rearrange("t h m d -> t (h m d)")).then_inc(layer_in[l], 16)
                for i in range(2):
                    for g in range(2):
                        pool.dma_start(ctxk[:, 512 + g * 128 + i * 64:512 + g * 128 + i * 64 + 64],
                                       ck[:, g * 64:(g + 1) * 64]).then_inc(layer_in[l], 16)
                pool.dma_start(ctxv[:, 0:512], a["cache_diff_v"][0, l].rearrange("t h e -> t (h e)")).then_inc(layer_in[l], 16)
                pool.dma_start(ctxv[:, 512:640], a["cache_win_v"][0, l].rearrange("t g d -> t (g d)")).then_inc(layer_in[l], 16)
                pool.dma_start(wpool[:, :, :], a["w_pool"][l].rearrange("g c e -> c g e")).then_inc(layer_in[l], 16)
                pool.wait_ge(h_ready, 2 * l + 1)
                pool.dma_start(poolm[:, :, :].rearrange("p g c -> p (g c)"), const[:, C_POOL:C_POOL + POOL_COLS]).then_inc(poolm_in, 16)

            layer_loads(0)
            pool.dma_start(wrout[:, :, :], a["w_router"][0].rearrange("(k p) e -> p k e", p=P)).then_inc(wrout_in, 16)
            pool.wait_ge(unit_done, 1 + N_HALF)
            layer_loads(1)
            pool.wait_ge(merge_done, 6 * DEPTH)
            pool.dma_start(slotc[:, :], const[:, C_SLOT:C_SLOT + SLOT_COLS]).then_inc(slotc_in, 16)

        @block.tensor
        def _(pe):
            def mm3(out, s, m, first, last, **kw):
                pe.matmul(out, s[0], m[0], start=first, stop=False, **kw)
                pe.matmul(out, s[0], m[1], start=False, stop=False, **kw)
                return pe.matmul(out, s[1], m[0], start=False, stop=last, **kw)

            def slot(n, k):
                return [w[:, n % RING, :].rearrange("p (k c) -> p k c", k=k) for w in (whi, wlo)]

            def ada_chunk(l, j):
                n = l * N_ADA + j
                pe.wait_ge(ada_in[n % ADA_RING], 16 * (n // ADA_RING + 1))
                for k in range(KD):
                    mm = pe.matmul(ada_ps(l, j), ada[:, n % ADA_RING, k, :], silc[:, :, k],
                                   start=(k == 0), stop=(k == KD - 1))
                mm.then_inc(ada_used, 1)

            def sum_squares(i):
                pe.wait_ge(sq_done, i + 1)
                for k in range(KD):
                    mm = pe.matmul(ps[:, 6, 0:T], ones[:, :], macc[:, k, :], start=(k == 0), stop=(k == KD - 1))
                mm.then_inc(ssq_done, 1)

            def rot_transposes(l, ti):
                r = N_TR * l + ti
                pe.wait_ge(rope_done, len(STAGED) * l + ti + 1)
                if r >= 1:
                    pe.wait_ge(tr_evac, r)
                for c in range(2):
                    for b in range(BLK):
                        src = kcd[:, b, c * P:(c + 1) * P] if ti == 6 else stage[:, ti % 2, b, c * P:(c + 1) * P]
                        mm = pe.transpose(ps[:, 4 + c, b * P:(b + 1) * P], src, ident)
                mm.then_inc(tr_done, 1)

            def input_projection(l):
                pe.wait_ge(h_ready, 2 * l + 1)
                for s in range(N_WIN):
                    n = BASE[l] + s
                    pe.wait_ge(lo_done, n + 1)
                    g = s % 2
                    if s >= 2:
                        pe.wait_ge(win_evac, WIN_INC * l + s - 1)
                    w = slot(n, KD)
                    out = ps[:, 2 * g:2 * g + 2, :].rearrange("p a c -> p (a c)")
                    for b in range(BLK):
                        for k in range(KD):
                            mm = mm3(out[:, b * 256:(b + 1) * 256], [h[:, k, b * P:(b + 1) * P] for h in (hhi, hlo)],
                                     [x[:, k, :] for x in w], k == 0, k == KD - 1)
                    mm.then_inc(mm_done, 1)
                    if s - 1 in STAGED:
                        rot_transposes(l, STAGED.index(s - 1))
                rot_transposes(l, 6)
                pe.wait_ge(layer_in[l], 16 * 8)
                pe.wait_ge(tr_evac, N_TR * l + 7)
                for c in range(6):
                    mm = pe.transpose(ps[:, 4 + c // 4, (c % 4) * P:(c % 4 + 1) * P], ctxk[:, c * P:(c + 1) * P], ident)
                mm.then_inc(tr_done, 1)

            def pooling(l):
                pe.wait_ge(win_evac, WIN_INC * (l + 1))
                pe.wait_ge(poolm_in, 16 * (l + 1))
                for g in range(4):
                    u = [utok[:, b, g * P:(g + 1) * P] for b in range(BLK)]
                    pe.matmul(ps[:, g, 0:P], u[0], poolm[:, g, 0:P], start=True, stop=True)
                    pe.matmul(ps[:, g, P:T], u[1], poolm[:, g, P:P + 256], start=True, stop=False)
                    mm = pe.matmul(ps[:, g, P:T], u[2], poolm[:, g, P + 256:P + 512], start=False, stop=True)
                mm.then_inc(pool_mm, 1)
                pe.wait_ge(tr_evac, N_TR * (l + 1))
                pe.wait_ge(pool_ev, l + 1)
                for g in range(4):
                    mm = pe.matmul(ps[:, 4 + g, 0:T], wpool[:, g, :], pooled[:, g, :], start=True, stop=True)
                mm.then_inc(pooly_mm, 1)

            def attention(l, kind):
                st0 = 24 * l + 12 * kind
                it0 = 36 * l + 12 * kind
                per = 1 + kind

                def scores(t):
                    h, qb = t // 3, t % 3
                    if t >= 2:
                        pe.wait_ge(e_done, st0 + t - 1)
                    nk, k0 = (P, 0) if qb == 0 else (T, P)
                    q, kk = (qTA, kTA[:, h, k0:k0 + nk]) if kind == 0 else (qTC, kTC[:, h // 2, k0:k0 + nk])
                    for m in range(2):
                        r = slice(64 * m, 64 * m + 64)
                        out, lhs = ps[:, 2 * (t % 2) + m, 0:nk], q[r, h, qb * P:(qb + 1) * P]
                        if kind == 0 or qb == 0:
                            mm = pe.matmul(out, lhs, kk[r], start=True, stop=True)
                            continue
                        o3, k3 = (x.rearrange("p (a c) -> p a c", c=P) for x in (out, kk[r]))
                        far = 2 - qb
                        near = slice(0, 3, 2) if far else slice(1, 3)
                        pe.matmul(o3[:, near, :], lhs, k3[:, near, :], start=True, stop=True)
                        pe.matmul(o3[:, far, :], lhs, k3[:, far, :], start=True, stop=False)
                        mm = pe.matmul(o3[:, far, :], ident, mask[:, qb - 1, :], start=False, stop=True)
                    mm.then_inc(s_done, 1)

                def transposes(i):
                    t, m = i // per, i % per
                    if m == 0:
                        pe.wait_ge(p_done, st0 + t + 1)
                    if it0 + i >= 2:
                        pe.wait_ge(pt_evac, it0 + i - 1)
                    for kb in range(1 if t % 3 == 0 else 3):
                        mm = pe.transpose(ps[:, 4 + (it0 + i) % 2, kb * P:(kb + 1) * P],
                                          ebuf[:, t % 2, m, kb * P:(kb + 1) * P], ident)
                    mm.then_inc(tp_done, 1)

                def values(i):
                    t, m = i // per, i % per
                    h, qb = t // 3, t % 3
                    pe.wait_ge(pt_evac, it0 + i + 1)
                    grp = 8 * l + 4 * kind + h
                    if qb == 0 and m == 0 and grp >= 2:
                        pe.wait_ge(o_evac, grp - 1)
                    c = slice(h * P, (h + 1) * P) if kind == 0 else slice(512 + (h // 2) * 64, 576 + (h // 2) * 64)
                    keys = [vtok[:, 0, c]] if qb == 0 else [vtok[:, 1, c], vtok[:, 2, c], ctxv[:, c]]
                    rows = slice(0, P) if kind == 0 else slice(64 * m, 64 * m + 64)
                    for kb, v in enumerate(keys):
                        mm = pe.matmul(ps[rows, 6 + grp % 2, qb * P:(qb + 1) * P], v,
                                       pt[:, (it0 + i) % 2, kb * P:(kb + 1) * P],
                                       start=(kb == 0), stop=(kb == len(keys) - 1))
                    mm.then_inc(pv_done, 1)

                pe.wait_ge(gate_evac, 12 * l + 4 * (kind + 1))
                scores(0)
                pe.wait_ge(merge_done, 6 * l + 2 * (kind + 1))
                n = 12 * per
                for i in range(n):
                    if i % per == 0 and i // per + 1 < 12:
                        scores(i // per + 1)
                    transposes(i)
                    if i >= 1:
                        values(i - 1)
                values(n - 1)
                if kind == 0:
                    pe.wait_ge(osq_done, l + 1)
                    for h in range(4):
                        mm = pe.matmul(ps[:, h, 0:T], ones[:, :], osq[:, h, :], start=True, stop=True)
                    mm.then_inc(oss_done, 1)

            def wide(l, n, w, x):
                for j in range(2):
                    for k in range(KD):
                        if n in GATES and k in (1, 5):
                            ada_chunk(1, PER_GATE * GATES.index(n) + 2 * j + (k == 5))
                        mm = mm3(ps[:, 2 * (n % 2) + j, 0:T], [y[:, k, j * P:(j + 1) * P] for y in w],
                                 [y[:, k, :] for y in x], k == 0, k == KD - 1)
                mm.then_inc(mm_done, 1)

            def branch(l, o):
                for half in range(2):
                    i = 6 * l + 2 * o + half
                    for j in range(2):
                        n = gate_slot(l, o, half, j)
                        pe.wait_ge(lo_done, n + 1)
                        if i and j == 0:
                            pe.wait_ge(gate_evac, 2 * i)
                        if o == 1 and half == 0 and j == 0:
                            pe.wait_ge(on_done, l + 1)
                        wide(l, n, slot(n, KD), (hhi, hlo))
                    n = branch_slot(l, o, half)
                    pe.wait_ge(lo_done, n + 1)
                    pe.wait_ge(o_ready, 3 * l + o + 1)
                    if half:
                        pe.wait_ge(merge_done, i)
                    w = slot(n, 4)
                    for q in range(4):
                        for k in range(4):
                            mm = mm3(ps[:, 4 + q, 0:T], [y[:, k, q * P:(q + 1) * P] for y in w],
                                     [y[:, k, :] for y in (ohi, olo)], k == 0, k == 3)
                    mm.then_inc(mm_done, 1)

            def out_projection(l):
                pe.wait_ge(merged_ready, l + 1)
                pe.wait_ge(gate_evac, 12 * (l + 1))
                for j in range(4):
                    n = out_slot(l, j)
                    pe.wait_ge(lo_done, n + 1)
                    if j >= 2:
                        pe.wait_ge(out_evac, 4 * l + j - 1)
                    wide(l, n, slot(n, KD), (hhi, hlo))

            def router():
                pe.wait_ge(chain_m, 16 * 4)
                pe.wait_ge(wrout_in, 16)
                for b in range(BLK):
                    for k in range(KD):
                        mm = pe.matmul(ps[:, 6, b * N_EXP:(b + 1) * N_EXP], macc[:, k, b * P:(b + 1) * P],
                                       wrout[:, k, :], start=(k == 0), stop=(k == KD - 1))
                mm.then_inc(rt_done, 1)
                for b in range(BLK):
                    for k in range(KD):
                        mm = pe.transpose(ps[:, 2 * b + k // 4, (k % 4) * P:(k % 4 + 1) * P],
                                          macc[:, k, b * P:(b + 1) * P], ident)
                mm.then_inc(h2_tr, 1)
                pe.wait_ge(sel_ready, 1)
                pe.wait_ge(slotc_in, 16)
                for b in range(BLK):
                    for c in range(b):
                        pe.matmul(ps[:, 6, b * N_EXP:(b + 1) * N_EXP], ones[:, :], rsm[:, c, 0:8],
                                  start=(c == 0), stop=False)
                    pe.matmul(ps[:, 6, b * N_EXP:(b + 1) * N_EXP], slotc[:, 0:P], rsm[:, b, 0:8], start=(b == 0), stop=True)
                for b in range(BLK):
                    mm = pe.matmul(ps[:, 6, 24:32], ones[:, :], rsm[:, b, 0:8], start=(b == 0), stop=(b == BLK - 1))
                mm.then_inc(pos_mm, 1)
                pe.wait_ge(pos_ready, 1)
                pe.wait_ge(h2_lo, 1)
                for e in range(N_EXP):
                    for b in range(BLK):
                        mm = pe.matmul(ps[:, e, b * P:(b + 1) * P], posx[:, b, e:e + 1].to_broadcast([P, P]),
                                       ident, start=True, stop=True)
                mm.then_inc(prow_mm, 1)
                pe.wait_ge(prow_ready, 1)

            def gather(weights):
                for m in range(KD):
                    for i, h in enumerate(htok):
                        for b in range(BLK):
                            mm = pe.matmul(ps[:, 2 + m // 3, (m % 3) * CAP:(m % 3 + 1) * CAP], h[:, b, m * P:(m + 1) * P],
                                           gat[:, b * CAP:(b + 1) * CAP], start=(i + b == 0), stop=(i + b == BLK))
                for c in range(2):
                    for b in range(BLK):
                        mm = pe.matmul(ps[:, 4, 2 * CAP + c:2 * CAP + c + 1],
                                       gat[:, b * CAP + c * P:b * CAP + c * P + P].bitcast(F32), weights(b),
                                       start=(b == 0), stop=(b == BLK - 1))
                mm.then_inc(gather_done, 1)

            def y_transposes(part, q4):
                tail, half = part // 2, part % 2
                for i in range(4):
                    m = 4 * half + i
                    mm = pe.transpose(ps[:, (2, 3, 4, 2)[part], i * P:(i + 1) * P],
                                      ysb[:, m * CAP + tail * P:m * CAP + tail * P + P], ident)
                mm.then_inc(yt_done, 1)

            def scatter(m):
                for i, (y, c) in enumerate(((yhi, 0), (ylo, 0), (yhi, 1), (ylo, 1))):
                    mm = pe.matmul(ps[:, 2 + m % 3, 0:T], y[:, c, m * P:(m + 1) * P], sct[:, c, :],
                                   start=(i == 0), stop=(i == 3))
                mm.then_inc(sc_done, 1)

            def scatter_steps(s, q):
                if s == 1:
                    pe.wait_ge(ysb_done, q + 1)
                    y_transposes(0, q)
                    y_transposes(1, q)
                if s == 2:
                    y_transposes(2, q)
                if s == 3:
                    pe.wait_ge(yl_done, 4 * q + 1)
                    y_transposes(3, q)
                if 4 <= s < 8:
                    if s == 4:
                        pe.wait_ge(yl_done, 4 * q + 4)
                        pe.wait_ge(sct_ready, q + 1)
                    for m in (2 * s - 8, 2 * s - 7):
                        if m >= 3:
                            pe.wait_ge(sc_evac, 8 * q + (m - 2))
                        scatter(m)

            def experts():
                n0 = BASE[1] + N_MIX
                n_rounds = pe.value_load(rounds[0:1, 0:1], min_val=1, max_val=MAX_ROUNDS)
                pe.wait_ge(gat_ready, 1)
                pe.wait_ge(gates_ready, 1)
                gather(lambda b: gwx[:, b, 0:1])
                with pe.Fori(0, n_rounds) as r:
                    with pe.Fori(0, N_EXP) as e:
                        q = r * N_EXP + e
                        pe.wait_ge(xg_ready, q + 1)
                        for s in range(GU):
                            pe.wait_ge(lo_done, q * UNIT + (n0 + s + 1))
                            if s >= 2:
                                pe.wait_ge(ehid_done, q * GU + (s - 1))
                            w = [x[:, s % RING, :].rearrange("p (w k c) -> p w k c", w=2, k=KD) for x in (whi, wlo)]
                            for j in range(2):
                                for k in range(KD):
                                    mm = mm3(ps[:, s % 2, j * CAP:(j + 1) * CAP], [y[:, j, k, :] for y in w],
                                             [y[:, k * CAP:(k + 1) * CAP] for y in (xgh, xgl)], k == 0, k == KD - 1)
                            mm.then_inc(mm_done, 1)
                            scatter_steps(s, q)
                        pe.wait_ge(sc_evac, 8 * q + 8)
                        pe.wait_ge(gat_ready, q + 2)
                        gather(lambda b: gwx[:, b, bass.ds(e + 1, 1)])
                        for i, f in enumerate(DOWN):
                            s = GU + i
                            pe.wait_ge(lo_done, q * UNIT + (n0 + s + 1))
                            pe.wait_ge(ehid_done, q * GU + GU)
                            w = [x[:, s % RING, 0:len(f) * D].rearrange("p (k c) -> p k c", c=D) for x in (whi, wlo)]
                            for c, kf in enumerate(f):
                                for m in range(KD):
                                    mm = mm3(ps[:, 5 + m // 3, (m % 3) * CAP:(m % 3 + 1) * CAP],
                                             [y[:, c, m * P:(m + 1) * P] for y in w],
                                             [y[:, kf, :] for y in (ehh, ehl)], kf == 0 and m % 3 == 0, kf == KF - 1,
                                             skip_group_check=True)
                            mm.then_inc(mm_done, 1)
                for s in range(1, 8):
                    scatter_steps(s, n_rounds * N_EXP)

            def units(l):
                n0 = BASE[l] + N_MIX
                h0, u0 = 0, 1
                pe.wait_ge(h_ready, 2 * l + 2)
                pe.wait_ge(out_evac, 4 * (l + 1))
                with pe.Fori(0, N_HALF if l == 0 else N_EXP) as u:
                    for s in range(GU):
                        pe.wait_ge(lo_done, u * UNIT + (n0 + s + 1))
                        if s == 1:
                            pe.wait_ge(unit_done, u + u0)
                        if s >= 2:
                            pe.wait_ge(hid_done, u * GU + (h0 + s - 1))
                        w = [x[:, s % RING, :].rearrange("p (w k c) -> p w k c", w=2, k=KD) for x in (whi, wlo)]
                        for j in range(2):
                            for k in range(KD):
                                mm = mm3(ps[:, 2 * (s % 2) + j, 0:T], [y[:, j, k, :] for y in w],
                                         [y[:, k, :] for y in (hhi, hlo)], k == 0, k == KD - 1)
                        mm.then_inc(mm_done, 1)
                    for i, f in enumerate(DOWN):
                        s = GU + i
                        pe.wait_ge(lo_done, u * UNIT + (n0 + s + 1))
                        pe.wait_ge(hid_done, u * GU + (h0 + GU))
                        w = [x[:, s % RING, 0:len(f) * D].rearrange("p (k c) -> p k c", c=D) for x in (whi, wlo)]
                        for c, kf in enumerate(f):
                            for m in range(KD):
                                last = kf == KF - 1
                                st = [y[:, c, m * P:(m + 1) * P] for y in w]
                                mm3(ps[:, 2 + m // 2, (m % 2) * 256:(m % 2 + 1) * 256], st,
                                    [y[:, kf, P:T] for y in (hidhi, hidlo)], kf == 0 and m % 2 == 0, last,
                                    skip_group_check=True)
                                mm = mm3(ps[:, 6 + m // 4, (m % 4) * P:(m % 4 + 1) * P], st,
                                         [y[:, kf, 0:P] for y in (hidhi, hidlo)], kf == 0 and m % 4 == 0, last,
                                         skip_group_check=True)
                        mm.then_inc(mm_done, 1)

            pe.wait_ge(init_in, 16 * n_init)
            for k in range(KD):
                for b in range(BLK):
                    mm = pe.transpose(ps[:, k, b * P:(b + 1) * P], xtok[:, b, k * P:(k + 1) * P], ident)
            mm.then_inc(x_tr, 1)
            pe.wait_ge(x_ev, 1)
            for l in range(DEPTH):
                mm = pe.transpose(ps[:, 4, l * P:l * P + R_END], vrows[0:R_END, l, :], ident[0:R_END, 0:R_END])
            mm.then_inc(v_tr, 1)
            pe.wait_ge(silc_ready, 1)
            for j in range(N_ADA):
                ada_chunk(0, j)
            pe.wait_ge(ones_set, 1)
            for l in range(DEPTH):
                sum_squares(2 * l)
                input_projection(l)
                pooling(l)
                branch(l, 0)
                attention(l, 0)
                branch(l, 1)
                attention(l, 1)
                branch(l, 2)
                out_projection(l)
                sum_squares(2 * l + 1)
                if l == 0:
                    units(l)
                else:
                    router()
                    experts()
            sum_squares(2 * DEPTH)
            pe.wait_ge(chain_m, 16 * 2 * DEPTH + KD)
            for b in range(BLK):
                for k in range(KD):
                    mm = pe.transpose(ps[:, 2 * b + k // 4, (k % 4) * P:(k % 4 + 1) * P],
                                      macc[:, k, b * P:(b + 1) * P], ident)
                mm.then_inc(y_tr, 1)

        @block.scalar
        def _(act):
            copy = ACT.Copy

            def hi(n):
                raw_wait(act, n)
                if n >= RING:
                    act.wait_ge(mm_done, n - RING + 1)
                act.activation(whi[:, n % RING, :], raw[:, n % RING, :], copy).then_inc(hi_done, 1)

            def square(i):
                act.activation(macc[:, :, :], xT[:, :, :], ACT.Square).then_inc(sq_done, 1)
                act.wait_ge(ssq_done, i + 1)
                act.activation(rstd[:, :], ps[:, 6, 0:T], ACT.Sqrt, scale=1.0 / D, bias=epsc[:, 0:1]).then_inc(rms_done, 1)

            def modulate(i):
                act.wait_ge(xn_done, i + 1)
                l, which = i // 2, i % 2
                sh = (SH1, SH2)[which]
                for k in range(KD):
                    for v, t in ((0, slice(P, T)), (1, slice(0, P))):
                        act.activation(macc[:, k, t], macc[:, k, t], ACT.Identity,
                                       scale=amul[:, l, which, k, v:v + 1],
                                       bias=mods[:, l, sh + k, v:v + 1]).then_inc(chain_m, 1)
                act.wait_ge(chain_m, 16 * (i + 1))
                if i == 3:
                    return
                act.activation(hhi[:, :, :], macc[:, :, :], copy).then_inc(hf_done, 1)

            def input_evac(l, s):
                act.wait_ge(mm_done, BASE[l] + s + 1)
                g = s % 2
                src = ps[:, 2 * g:2 * g + 2, :].rearrange("p a c -> p (a c)")[:, 0:BLK * 256].rearrange(
                    "p (b c) -> p b c", b=BLK)
                kv = KV_SLOTS.index(s) if s in KV_SLOTS else None
                if s in STAGED:
                    ti = STAGED.index(s)
                    if ti >= 2:
                        act.wait_ge(tr_done, N_TR * l + ti - 1)
                    if ti == 4:
                        act.wait_ge(kv_out, 16 * (6 * l + 4))
                    if ti == 0 and l:
                        act.wait_ge(kv_out, 16 * 6 * l)
                    act.activation(stage[:, ti % 2], src, copy).then_inc(win_evac, 1)
                    if s == 10:
                        act.activation(vtok[:, :, 512:640], src[:, :, P:256], copy).then_inc(win_evac, 1)
                elif s < 6:
                    act.activation(vtok[:, :, (s - 4) * 256:(s - 3) * 256], src, copy).then_inc(win_evac, 1)
                else:
                    act.activation(utok[:, :, (s - 6) * 256:(s - 5) * 256], src, copy).then_inc(win_evac, 1)
                ev = WIN_INC * l + s + 1 + (s == 10)
                if kv is not None:
                    act.wait_ge(win_evac, ev)
                if s in (2, 3):
                    act.dma_start(new_dk[0, l].rearrange("t h m d -> t (h m d)")[:, (s - 2) * 256:(s - 1) * 256],
                                  stage[:, STAGED.index(s) % 2, 0, :]).then_inc(kv_out, 16)
                if s in (4, 5):
                    act.dma_start(new_dv[0, l].rearrange("t h e -> t (h e)")[:, (s - 4) * 256:(s - 3) * 256],
                                  vtok[:, 0, (s - 4) * 256:(s - 3) * 256]).then_inc(kv_out, 16)
                if s == 10:
                    act.dma_start(new_wk[0, l].rearrange("t g d -> t (g d)"), stage[:, 0, 0, 0:P]).then_inc(kv_out, 16)
                    act.dma_start(new_wv[0, l].rearrange("t g d -> t (g d)"), vtok[:, 0, 512:640]).then_inc(kv_out, 16)

            def turned_evac(l, ti):
                act.wait_ge(tr_done, N_TR * l + ti + 1)
                src = ps[:, 4:6, 0:T]
                if ti < 2:
                    act.activation(qTA[:, 2 * ti:2 * ti + 2, :], src, copy, scale=DHA ** -0.5).then_inc(tr_evac, 1)
                elif ti < 4:
                    act.activation(kTA[:, 2 * ti - 4:2 * ti - 2, 0:T], src, copy).then_inc(tr_evac, 1)
                elif ti < 6:
                    act.activation(qTC[:, 2 * ti - 8:2 * ti - 6, :], src, copy, scale=DHC ** -0.5).then_inc(tr_evac, 1)
                elif ti == 6:
                    act.activation(kTC[:, :, 0:T], src, copy).then_inc(tr_evac, 1)
                else:
                    act.activation(kTA[:, :, T:512], ps[:, 4, :].rearrange("p (h c) -> p h c", h=4), copy)
                    act.activation(kTC[:, :, T:512], ps[:, 5, 0:256].rearrange("p (h c) -> p h c", h=2),
                                   copy).then_inc(tr_evac, 1)

            def pooling(l):
                act.wait_ge(pool_mm, l + 1)
                act.activation(pooled[:, :, :], ps[:, 0:4, 0:T], copy).then_inc(pool_ev, 1)
                act.wait_ge(pooly_mm, l + 1)
                for g in range(4):
                    x = act.activation(oraw[:, g, :], ps[:, 4 + g, 0:T], copy, scale=cols[:, l, R_PS + g:R_PS + g + 1])
                    x.then_inc(chain_p, 1)
                act.wait_ge(chain_p, 4 * (l + 1))
                act.activation(ohi[:, :, :], oraw[:, :, :], copy).then_inc(oh_done, 1)

            def attention(l, kind):
                st0, it0, per = 24 * l + 12 * kind, 36 * l + 12 * kind, 1 + kind

                def exps(t):
                    p, nk = t % 2, (P if t % 3 == 0 else T)
                    act.wait_ge(nmax_done, st0 + t + 1)
                    if t >= 2:
                        act.wait_ge(tp_done, it0 + per * (t - 1))
                    for m in range(2):
                        x = act.activation(ebuf[:, p, m, 0:nk], ps[:, 2 * p + m, 0:nk], ACT.Exp,
                                           bias=small[:, p, m:m + 1], accum_out=small[:, p, 2 + m:3 + m])
                    if kind == 1:
                        x = act.activation(small[:, p, 6:8], small[:, p, 4:6], ACT.Exp)
                    x.then_inc(e_done, 1)

                def pt_copy(i):
                    act.wait_ge(tp_done, it0 + i + 1)
                    n = it0 + i
                    if n >= 2:
                        act.wait_ge(pv_done, n - 1)
                    nk = P if (i // per) % 3 == 0 else T
                    act.activation(pt[:, n % 2, 0:nk], ps[:, 4 + n % 2, 0:nk], copy).then_inc(pt_evac, 1)

                def o_copy(h):
                    act.wait_ge(pv_done, it0 + 3 * per * (h + 1))
                    act.activation(oraw[:, h, :], ps[:, 6 + h % 2, 0:T], copy).then_inc(o_evac, 1)

                if kind == 0:
                    act.wait_ge(kv_out, 16 * 6 * (l + 1))
                    act.wait_ge(o_ready, 3 * l + 1)
                else:
                    act.wait_ge(o_ready, 3 * l + 2)
                exps(0)
                for t in range(12):
                    if t + 1 < 12:
                        exps(t + 1)
                    for m in range(per):
                        pt_copy(per * t + m)
                    if t % 3 == 0 and t >= 3:
                        o_copy(t // 3 - 1)
                o_copy(3)
                act.wait_ge(o_evac, 8 * l + 4 * kind + 4)
                if kind == 0:
                    act.activation(osq[:, :, :], oraw[:, :, :], ACT.Square).then_inc(osq_done, 1)
                    act.wait_ge(oss_done, l + 1)
                    act.activation(osq[:, :, :], ps[:, 0:4, 0:T], ACT.Sqrt, scale=1.0 / P, bias=epsc[:, 0:1]).then_inc(orms_done, 1)
                    act.wait_ge(on_done, l + 1)
                act.wait_ge(mm_done, branch_slot(l, kind, 1) + 1)
                act.activation(ohi[:, :, :], oraw[:, :, :], copy).then_inc(oh_done, 1)

            def gate_out(l, o, half, j):
                n = gate_slot(l, o, half, j)
                act.wait_ge(mm_done, n + 1)
                i = 6 * l + 2 * o + half
                if i:
                    act.wait_ge(merge_done, i)
                if l == 0:
                    for c in range(PER_GATE * (2 * i + j), PER_GATE * (2 * i + j + 1), 2):
                        act.activation(mods[:, 1, c:c + 2, :].rearrange("p j v -> p (j v)"), ada_ps(1, c, 2), copy
                                       ).then_inc(ada_read, 1)
                act.activation(gbuf[:, 2 * j:2 * j + 2, :], pair(n % 2), ACT.Sigmoid).then_inc(gate_evac, 1)

            def units(l):
                n0 = BASE[l] + N_MIX
                h0 = 0 if l == 0 else N_HALF * GU
                with act.Fori(0, N_HALF if l == 0 else N_EXP) as u:
                    def unit_hi(s):
                        act.wait_ge(raw_in[s % RING], u * (32 * UNIT // RING) + 32 * ((n0 + s) // RING + 1))
                        act.wait_ge(mm_done, u * UNIT + (n0 + s - RING + 1))
                        used = len(DOWN[s - GU]) * D if GU <= s < UNIT else SLOT
                        act.activation(whi[:, s % RING, 0:used], raw[:, s % RING, 0:used], copy).then_inc(hi_done, 1)

                    for s in range(UNIT):
                        unit_hi(s + 2)
                        if s < GU:
                            act.wait_ge(mm_done, u * UNIT + (n0 + s + 1))
                            if s >= 2:
                                act.wait_ge(hid_done, u * GU + (h0 + s - 1))
                            act.activation(sil[:, s % 2, :], ps[:, 2 * (s % 2), 0:T], ACT.Silu).then_inc(sil_done, 1)

            def y_high(part):
                rows = slice(0, P if part < 2 else CAP - P)
                act.activation(yhi[rows, part // 2, (part % 2) * 512:(part % 2 + 1) * 512],
                               ps[rows, (2, 3, 4, 2)[part], :], copy, scale=gws[rows, 0, part // 2:part // 2 + 1]
                               ).then_inc(yh_done, 1)

            def y_steps(s, q):
                for part in {1: (0, 1), 2: (2,), 3: (3,)}.get(s, ()):
                    act.wait_ge(yt_done, 4 * q + (part + 1))
                    y_high(part)

            def gathered(q, first=False):
                act.wait_ge(gather_done, q + 2) if not first else act.wait_ge(gather_done, 1)
                act.activation(gws[:, 0, :], gws[:, 1, :], copy).then_inc(gws_moved, 1)
                act.activation(xgh[:, 0:6 * CAP].rearrange("p (a c) -> p a c", a=2), ps[:, 2:4, 0:3 * CAP], copy)
                act.activation(xgh[:, 6 * CAP:CW], ps[:, 4, 0:2 * CAP], copy)
                act.wait_ge(gws_moved, q + 2) if not first else act.wait_ge(gws_moved, 1)
                act.activation(gws[:, 1, :], ps[:, 4, 2 * CAP:2 * CAP + 2], copy).then_inc(xgh_done, 1)

            def experts():
                n0 = BASE[1] + N_MIX
                act.wait_ge(pos_ready, 1)
                n_rounds = act.value_load(rounds[0:1, 0:1], min_val=1, max_val=MAX_ROUNDS)
                act.wait_ge(exp_init, 1)
                gathered(0, first=True)
                with act.Fori(0, n_rounds) as r:
                    with act.Fori(0, N_EXP) as e:
                        q = r * N_EXP + e
                        for s in range(UNIT):
                            n = s + 2
                            act.wait_ge(raw_in[n % RING], q * (32 * UNIT // RING) + 32 * ((n0 + n) // RING + 1))
                            act.wait_ge(mm_done, q * UNIT + (n0 + n - RING + 1))
                            used = len(DOWN[n - GU]) * D if GU <= n < UNIT else SLOT
                            act.activation(whi[:, n % RING, 0:used], raw[:, n % RING, 0:used], copy).then_inc(hi_done, 1)
                            if s < GU:
                                act.wait_ge(mm_done, q * UNIT + (n0 + s + 1))
                                if s >= 2:
                                    act.wait_ge(ehid_done, q * GU + (s - 1))
                                act.activation(esil[:, s % 2, :], ps[:, s % 2, 0:CAP], ACT.Silu).then_inc(esil_done, 1)
                            y_steps(s, q)
                            if s == GU:
                                gathered(q)
                        act.wait_ge(mm_done, q * UNIT + (n0 + UNIT))
                        act.activation(ysb[:, 0:6 * CAP].rearrange("p (a c) -> p a c", a=2), ps[:, 5:7, 0:3 * CAP], copy)
                        act.activation(ysb[:, 6 * CAP:CW], ps[:, 7, 0:2 * CAP], copy).then_inc(ysb_done, 1)
                for s in range(1, 4):
                    y_steps(s, n_rounds * N_EXP)
                act.wait_ge(raw_in[2], n_rounds * (N_EXP * UNIT // RING * 32) + 32 * (n0 // RING + 1))
                act.wait_ge(sc_evac, n_rounds * (8 * N_EXP) + 8)

            act.wait_ge(x_tr, 1)
            act.activation(xT[:, :, :], ps[:, :, 0:T], copy).then_inc(x_ev, 1)
            act.wait_ge(v_tr, 1)
            act.activation(cols[:, :, :], ps[:, 4, 0:256].rearrange("p (l c) -> p l c", l=2)[:, :, 0:R_END],
                           copy).then_inc(v_ev, 1)
            act.wait_ge(v_ev, 1)
            act.activation(silc[:, :, :], cols[:, 0, R_C:R_FIN].rearrange("p (v k) -> p v k", v=2),
                           ACT.Silu).then_inc(silc_ready, 1)
            act.wait_ge(ada_used, N_ADA)
            act.activation(mods[:, 0].rearrange("p j v -> p (j v)"), ada_ps(0, 0, N_ADA), copy).then_inc(ada_read, 1)
            act.wait_ge(lam_sums, 1)
            act.activation(lamp[:, :, :], lamp[:, :, :], ACT.Exp).then_inc(v_ev, 1)
            act.wait_ge(x_ev, 1)
            for l in range(DEPTH):
                b0 = BASE[l]
                if l:
                    act.wait_ge(unit_done, 1 + N_HALF)
                square(2 * l)
                modulate(2 * l)
                if l == 0:
                    hi(b0)
                    hi(b0 + 1)
                for s in range(N_WIN):
                    hi(b0 + s + 2)
                    input_evac(l, s)
                    if s - 1 in STAGED:
                        turned_evac(l, STAGED.index(s - 1))
                turned_evac(l, 6)
                turned_evac(l, 7)
                pooling(l)
                for o in range(3):
                    if o:
                        attention(l, o - 1)
                    for half in range(2):
                        for j in range(2):
                            n = gate_slot(l, o, half, j)
                            hi(n + 2)
                            gate_out(l, o, half, j)
                        hi(branch_slot(l, o, half) + 2)
                act.wait_ge(merge_done, 6 * (l + 1))
                act.activation(hhi[:, :, :], macc[:, :, :], copy).then_inc(mh_done, 1)
                for j in range(4):
                    hi(out_slot(l, j + 2))
                act.wait_ge(out_evac, 4 * (l + 1))
                square(2 * l + 1)
                modulate(2 * l + 1)
                if l == 0:
                    units(l)
                else:
                    act.wait_ge(h2_tr, 1)
                    act.activation(htok[0].rearrange("p b d -> p (b d)"), ps[:, 0:6, :].rearrange("p a c -> p (a c)"), copy
                                   ).then_inc(h2_hi, 1)
                    act.wait_ge(rt_sub, 1)
                    act.activation(rsm[:, :, 8:16], rsm[:, :, 8:16], ACT.Exp).then_inc(rt_exp, 1)
                    act.wait_ge(prow_mm, 1)
                    act.activation(prow[:, :, :], ps[:, :, 0:T], copy).then_inc(prow_ready, 1)
                    experts()
            square(2 * DEPTH)
            act.wait_ge(xn_done, 5)
            for k in range(KD):
                act.activation(macc[:, k, :], macc[:, k, :], copy, scale=cols[:, 0, R_FIN + k:R_FIN + k + 1]
                               ).then_inc(chain_m, 1)
            for b in range(BLK):
                act.wait_ge(y_tr, b + 1)
                act.activation(yout[:, b, :], ps[:, 2 * b:2 * b + 2, :].rearrange("p a c -> p (a c)"), copy
                               ).then_inc(y_ev, 1)
                act.wait_ge(y_ev, b + 1)
                dst = y_prompt[0] if b == 0 else y_sample[0, (b - 1) * P:b * P]
                act.dma_start(dst, yout[:, b, :]).then_inc(y_out, 16)
            act.wait_ge(y_out, 16 * BLK)
            act.wait_ge(kv_out, 16 * 6 * DEPTH)

        @block.vector
        def _(dve):
            count = [0]

            def link(ins):
                count[0] += 1
                ins.then_inc(chain_v, 1)
                dve.wait_ge(chain_v, count[0])

            def lo(n):
                dve.wait_ge(hi_done, n + 1)
                dve.tensor_tensor(wlo[:, n % RING, :], raw[:, n % RING, :], whi[:, n % RING, :].bitcast(F32),
                                  ALU.subtract).then_inc(lo_done, 1)

            def normalise(i):
                dve.wait_ge(rms_done, i + 1)
                link(dve.reciprocal(rstd[:, :], rstd[:, :]))
                dve.tensor_tensor(macc[:, :, :], xT[:, :, :], rstd[:, :].unsqueeze(1).to_broadcast([P, KD, T]),
                                  ALU.mult).then_inc(xn_done, 1)
                if i < 3:
                    dve.wait_ge(hf_done, i + 1)
                    dve.tensor_tensor(hlo[:, :, :], macc[:, :, :], hhi[:, :, :].bitcast(F32),
                                      ALU.subtract).then_inc(h_ready, 1)

            def modulations(l):
                dve.wait_ge(ada_read, 1 + l * N_ADA // 2)
                b = cols[:, l, R_BADA:R_BADA + N_ADA].unsqueeze(2).to_broadcast([P, N_ADA, 2])
                link(dve.tensor_tensor(mods[:, l], mods[:, l], b, ALU.add))
                for which, (sc, g) in enumerate(((SC1, R_N1), (SC2, R_N2))):
                    link(dve.tensor_scalar(amul[:, l, which], mods[:, l, sc:sc + KD, :], 1.0, None, ALU.add))
                    link(dve.tensor_tensor(amul[:, l, which], amul[:, l, which],
                                           cols[:, l, g:g + KD].unsqueeze(2).to_broadcast([P, KD, 2]), ALU.mult))
                lam_init = 0.8 - 0.6 * math.exp(-0.3 * l)
                link(dve.tensor_scalar(subg[:, l:l + 1], cols[:, l, R_SUB:R_SUB + 1], 1.0 - lam_init, None, ALU.mult))

            def rotate(l, ti):
                s = STAGED[ti]
                dve.wait_ge(win_evac, WIN_INC * l + s + 1 + (s == 10))
                heads = 2 if s == 10 else 4
                for b in range(2):
                    x = stage[:, ti % 2, b + 1, 0:heads * 64].rearrange("p (h s f i) -> p h s f i", h=heads, s=2, f=2)
                    co, si = (rope[:, b, c, :].rearrange("p (s i) -> p s i", s=2).unsqueeze(1)
                              .to_broadcast([P, heads, 2, 16]) for c in range(2))
                    t1, t2 = (rope_t[:, i, 0:heads * 32].rearrange("p (h s i) -> p h s i", h=heads, s=2)
                              for i in range(2))
                    a1, a2 = x[:, :, :, 0, :], x[:, :, :, 1, :]
                    dve.tensor_tensor(t1, a2, si, ALU.mult)
                    link(dve.tensor_tensor(t2, a1, si, ALU.mult))
                    dve.tensor_tensor(a1, a1, co, ALU.mult)
                    link(dve.tensor_tensor(a2, a2, co, ALU.mult))
                    dve.tensor_tensor(a1, a1, t1, ALU.subtract)
                    x = dve.tensor_tensor(a2, a2, t2, ALU.add)
                    if b == 0 or ti == 6:
                        link(x)
                    else:
                        x.then_inc(rope_done, 1)
                        dve.wait_ge(rope_done, len(STAGED) * l + ti + 1)
                if ti == 6:
                    src = stage[:, ti % 2, :, 0:P]
                    for g in range(2):
                        for i in range(2):
                            x = dve.tensor_copy(kcd[:, :, g * P + i * 64:g * P + i * 64 + 64], src[:, :, g * 64:g * 64 + 64])
                            if g == 1 and i == 1:
                                x.then_inc(rope_done, 1)

            def attention(l, kind):
                st0 = 24 * l + 12 * kind

                def maxima(t):
                    p, nk = t % 2, (P if t % 3 == 0 else T)
                    dve.wait_ge(s_done, st0 + t + 1)
                    x = dve.tensor_reduce(small[:, p, 0:2], ps[:, 2 * p:2 * p + 2, 0:nk], X, ALU.max, negate=True)
                    if kind == 1:
                        hp = t // 3
                        link(x)
                        link(dve.tensor_tensor(small[:, p, 0:2], small[:, p, 0:2], nsink[:, l, 2 * hp:2 * hp + 2], ALU.min))
                        x = dve.tensor_tensor(small[:, p, 4:6], small[:, p, 0:2], sinkr[:, l, 2 * hp:2 * hp + 2], ALU.add)
                    x.then_inc(nmax_done, 1)

                def normal(t):
                    p, nk = t % 2, (P if t % 3 == 0 else T)
                    dve.wait_ge(e_done, st0 + t + 1)
                    e = [ebuf[:, p, m, 0:nk] for m in range(2)]
                    if kind == 1:
                        link(dve.tensor_tensor(small[:, p, 2:4], small[:, p, 2:4], small[:, p, 6:8], ALU.add))
                    link(dve.reciprocal(small[:, p, 8:10], small[:, p, 2:4]))
                    if kind == 0:
                        link(dve.tensor_scalar(small[:, p, 9:10], small[:, p, 9:10], neglam[:, l:l + 1], None, ALU.mult))
                        link(dve.tensor_scalar(e[0], e[0], small[:, p, 8:9], None, ALU.mult))
                        dve.scalar_tensor_tensor(e[0], e[1], small[:, p, 9:10], e[0], ALU.mult, ALU.add).then_inc(p_done, 1)
                    else:
                        dve.tensor_scalar(e[0], e[0], small[:, p, 8:9], None, ALU.mult)
                        dve.tensor_scalar(e[1], e[1], small[:, p, 9:10], None, ALU.mult).then_inc(p_done, 1)

                maxima(0)
                for t in range(12):
                    if t + 1 < 12:
                        maxima(t + 1)
                    normal(t)
                if kind == 0:
                    dve.wait_ge(orms_done, l + 1)
                    link(dve.reciprocal(osq[:, :, :], osq[:, :, :]))
                    dve.scalar_tensor_tensor(oraw[:, :, :].rearrange("p a b -> p (a b)"),
                                             oraw[:, :, :].rearrange("p a b -> p (a b)"), subg[:, l:l + 1],
                                             osq[:, :, :].rearrange("p a b -> p (a b)"), ALU.mult, ALU.mult
                                             ).then_inc(on_done, 1)

            def o_low(l, o):
                dve.wait_ge(oh_done, 3 * l + o + 1)
                dve.tensor_tensor(olo[:, :, :], oraw[:, :, :], ohi[:, :, :].bitcast(F32), ALU.subtract).then_inc(o_ready, 1)

            def merge(l, o, half):
                dve.wait_ge(mm_done, branch_slot(l, o, half) + 1)
                dve.wait_ge(gate_evac, 12 * l + 4 * o + 2 * half + 2)
                dst = macc[:, 4 * half:4 * half + 4, :]
                if o == 0:
                    dve.tensor_tensor(dst, gbuf[:, :, :], ps[:, 4:8, 0:T], ALU.mult).then_inc(merge_done, 1)
                else:
                    link(dve.tensor_tensor(gbuf[:, :, :], gbuf[:, :, :], ps[:, 4:8, 0:T], ALU.mult))
                    dve.tensor_tensor(dst, dst, gbuf[:, :, :], ALU.add).then_inc(merge_done, 1)

            def residual(l, n, j):
                dve.wait_ge(mm_done, n + 1)
                for c in range(2):
                    m = 2 * j + c
                    for v, t in ((0, slice(P, T)), (1, slice(0, P))):
                        x = dve.scalar_tensor_tensor(xT[:, m, t], ps[:, 2 * (n % 2) + c, t], mods[:, l, G1 + m, v:v + 1],
                                                     xT[:, m, t], ALU.mult, ALU.add)
                x.then_inc(out_evac, 1)

            def router():
                dve.memset(ysb[:, :], 0.0)
                dve.memset(gws[:, :, :], 0.0)
                dve.memset(gat[:, :].bitcast(F32), 0.0)
                dve.memset(yhi[:, :, :].bitcast(F32), 0.0)
                dve.memset(ylo[:, :, :].bitcast(F32), 0.0)
                link(dve.memset(sct[:, :, :].bitcast(F32), 0.0))
                dve.tensor_copy(gws[:, 0, :], gws[:, 1, :]).then_inc(exp_init, 1)
                dve.wait_ge(rt_done, 1)
                lg, ex, sel = rsm[:, :, 8:16], rsm[:, :, 8:16], rsm[:, :, 0:8]
                link(dve.tensor_copy(lg, ps[:, 6, 0:BLK * 8].rearrange("p (b e) -> p b e", b=BLK)))
                mx = small[:, 0, 0:BLK]
                for b in range(BLK):
                    mine = lg[:, b, :].unsqueeze(2).to_broadcast([P, 8, 8])
                    other = lg[:, b, :].unsqueeze(1).to_broadcast([P, 8, 8])
                    gt = rcmp[:, 0, b, :].rearrange("p (e j) -> p e j", e=8)
                    eq = rcmp[:, 1, b, :].rearrange("p (e j) -> p e j", e=8)
                    dve.tensor_tensor(gt, other, mine, ALU.is_gt)
                    link(dve.tensor_tensor(eq, other, mine, ALU.is_equal))
                    link(dve.tensor_tensor(eq, eq, tri.rearrange("p (e j) -> p e j", e=8), ALU.mult))
                    link(dve.tensor_tensor(gt, gt, eq, ALU.add))
                    link(dve.tensor_reduce(sel[:, b, :], gt, X, ALU.add))
                dve.tensor_scalar(sel, sel, 1.5, None, ALU.is_lt).then_inc(sel_ready, 1)
                link(dve.tensor_reduce(mx, lg, X, ALU.max))
                dve.tensor_tensor(lg, lg, mx.unsqueeze(2).to_broadcast([P, BLK, 8]), ALU.subtract).then_inc(rt_sub, 1)
                dve.wait_ge(h2_hi, 1)
                dve.tensor_tensor(htok[1].rearrange("p b d -> p (b d)"), ps[:, 0:6, :].rearrange("p a c -> p (a c)"),
                                  htok[0].rearrange("p b d -> p (b d)").bitcast(F32), ALU.subtract).then_inc(h2_lo, 1)
                dve.wait_ge(pos_mm, 1)
                pos = ps[:, 6, 0:BLK * 8].rearrange("p (b e) -> p b e", b=BLK)
                dve.tensor_reduce(small[:, 1, 0:1], ps[:, 6, 24:32], X, ALU.max)
                link(dve.scalar_tensor_tensor(posx[:, :, 0:8], pos, 1.0, sel, ALU.add, ALU.mult))
                link(dve.tensor_scalar(posx[:, :, 0:8], posx[:, :, 0:8], -1.0, None, ALU.add))
                dve.tensor_scalar(posx[:, :, 8:9], posx[:, :, 0:1], -float(CAP), None, ALU.add)
                for i in range(1, MAX_ROUNDS):
                    dve.tensor_scalar(small[:, 1, 1 + i:2 + i], small[:, 1, 0:1], float(i * CAP), None, ALU.is_gt)
                link(dve.memset(small[:, 1, 1:2], 1.0))
                link(dve.tensor_reduce(small[:, 1, 8:9], small[:, 1, 1:1 + MAX_ROUNDS], X, ALU.add))
                dve.tensor_copy(rounds[:, :], small[:, 1, 8:9]).then_inc(pos_ready, 1)
                dve.wait_ge(pos_ready, 1)
                gather_matrix(lambda b: posx[:, b, 0:1])
                dve.wait_ge(rt_exp, 1)
                g8 = gwx[:, :, 0:8]
                link(dve.tensor_tensor(g8, ex, sel, ALU.mult))
                link(dve.tensor_reduce(mx, g8, X, ALU.add))
                link(dve.reciprocal(mx, mx))
                link(dve.tensor_tensor(g8, g8, mx.unsqueeze(2).to_broadcast([P, BLK, 8]), ALU.mult))
                dve.tensor_copy(gwx[:, :, 8:9], gwx[:, :, 0:1]).then_inc(gates_ready, 1)

            def gather_matrix(pos):
                for b in range(BLK):
                    x = dve.tensor_scalar(gat[:, b * CAP:(b + 1) * CAP], slotc[:, P:P + CAP], pos(b), None, ALU.is_equal)
                x.then_inc(gat_ready, 1)

            def y_low(s, q):
                for part in {1: (0, 1), 2: (2,), 3: (3,)}.get(s, ()):
                    rows = slice(0, P if part < 2 else CAP - P)
                    c = slice((part % 2) * 512, (part % 2 + 1) * 512)
                    dve.wait_ge(yh_done, 4 * q + (part + 1))
                    dve.scalar_tensor_tensor(ylo[rows, part // 2, c], ps[rows, (2, 3, 4, 2)[part], :],
                                             gws[rows, 0, part // 2:part // 2 + 1],
                                             yhi[rows, part // 2, c].bitcast(F32), ALU.mult, ALU.subtract
                                             ).then_inc(yl_done, 1)

            def scattered(s, q):
                if 4 <= s < 8:
                    for m in (2 * s - 8, 2 * s - 7):
                        dve.wait_ge(sc_done, 8 * q + (m + 1))
                        for v, t in ((0, slice(P, T)), (1, slice(0, P))):
                            x = dve.scalar_tensor_tensor(xT[:, m, t], ps[:, 2 + m % 3, t], mods[:, 1, G2 + m, v:v + 1],
                                                         xT[:, m, t], ALU.mult, ALU.add)
                        x.then_inc(sc_evac, 1)

            def gathered_low(wait):
                wait()
                dve.tensor_tensor(xgl[:, 0:6 * CAP].rearrange("p (a c) -> p a c", a=2), ps[:, 2:4, 0:3 * CAP],
                                  xgh[:, 0:6 * CAP].rearrange("p (a c) -> p a c", a=2).bitcast(F32), ALU.subtract)
                dve.tensor_tensor(xgl[:, 6 * CAP:CW], ps[:, 4, 0:2 * CAP], xgh[:, 6 * CAP:CW].bitcast(F32),
                                  ALU.subtract).then_inc(xg_ready, 1)

            def experts():
                n0 = BASE[1] + N_MIX
                n_rounds = dve.value_load(rounds[0:1, 0:1], min_val=1, max_val=MAX_ROUNDS)
                dve.memset(small[:, 0, 0:1], 0.0).then_inc(ysb_done, 1)
                dve.memset(small[:, 0, 1:2], 0.0).then_inc(sct_ready, 1)
                gathered_low(lambda: dve.wait_ge(xgh_done, 1))
                with dve.Fori(0, n_rounds) as r:
                    with dve.Fori(0, N_EXP) as e:
                        q = r * N_EXP + e
                        dve.wait_ge(gather_done, q + 1)
                        gather_matrix(lambda b: posx[:, b, bass.ds(e + 1, 1)])
                        for s in range(UNIT):
                            n = s + 2
                            used = len(DOWN[n - GU]) * D if GU <= n < UNIT else SLOT
                            dve.wait_ge(hi_done, q * UNIT + (n0 + n + 1))
                            dve.tensor_tensor(wlo[:, n % RING, 0:used], raw[:, n % RING, 0:used],
                                              whi[:, n % RING, 0:used].bitcast(F32), ALU.subtract).then_inc(lo_done, 1)
                            if s < GU:
                                dve.wait_ge(esil_done, q * GU + (s + 1))
                                dve.tensor_tensor(evalu[:, s % 2, :], esil[:, s % 2, :], ps[:, s % 2, CAP:2 * CAP],
                                                  ALU.mult).then_inc(chain_e, 1)
                                dve.wait_ge(chain_e, q * (2 * GU) + (2 * s + 1))
                                dve.tensor_copy(ehh[:, s, :], evalu[:, s % 2, :]).then_inc(chain_e, 1)
                                dve.wait_ge(chain_e, q * (2 * GU) + (2 * s + 2))
                                dve.tensor_tensor(ehl[:, s, :], evalu[:, s % 2, :], ehh[:, s, :].bitcast(F32),
                                                  ALU.subtract).then_inc(ehid_done, 1)
                            y_low(s, q)
                            scattered(s, q)
                            if s == 8:
                                for c in range(2):
                                    x = dve.tensor_scalar(sct[:, c, :], prow[:, bass.ds(e, 1), :].rearrange("p a t -> p (a t)"),
                                                          slotc[:, P + CAP + c:P + CAP + c + 1], None, ALU.is_equal)
                                x.then_inc(sct_ready, 1)
                            if s == GU:
                                gathered_low(lambda: dve.wait_ge(xgh_done, q + 2))
                    dve.wait_ge(gat_ready, r * N_EXP + (N_EXP + 1))
                    dve.wait_ge(sct_ready, r * N_EXP + (N_EXP + 1))
                    dve.tensor_scalar(posx[:, :, :], posx[:, :, :], -float(CAP), None, ALU.add)
                    dve.tensor_scalar(slotc[:, P + CAP:P + CAP + 2], slotc[:, P + CAP:P + CAP + 2], float(CAP), None,
                                      ALU.add).then_inc(round_done, 1)
                    dve.wait_ge(round_done, r + 1)
                for s in range(1, 8):
                    y_low(s, n_rounds * N_EXP)
                    scattered(s, n_rounds * N_EXP)

            def units(l):
                n0 = BASE[l] + N_MIX
                h0 = 0 if l == 0 else N_HALF * GU
                per = 2 + (l == 1)
                c0 = 0 if l == 0 else N_HALF * GU * 2
                with dve.Fori(0, N_HALF if l == 0 else N_EXP) as u:
                    def unit_lo(s):
                        used = len(DOWN[s - GU]) * D if GU <= s < UNIT else SLOT
                        dve.wait_ge(hi_done, u * UNIT + (n0 + s + 1))
                        dve.tensor_tensor(wlo[:, s % RING, 0:used], raw[:, s % RING, 0:used],
                                          whi[:, s % RING, 0:used].bitcast(F32), ALU.subtract).then_inc(lo_done, 1)

                    def hop(ins, s, i):
                        ins.then_inc(chain_u, 1)
                        dve.wait_ge(chain_u, u * (GU * per) + (c0 + s * per + i))

                    for s in range(UNIT):
                        unit_lo(s + 2)
                        if s < GU:
                            dve.wait_ge(sil_done, u * GU + (h0 + s + 1))
                            hop(dve.tensor_tensor(val[:, s % 2, :], sil[:, s % 2, :], ps[:, 2 * (s % 2) + 1, 0:T], ALU.mult), s, 1)
                            if l == 1:
                                hop(dve.tensor_tensor(val[:, s % 2, :], val[:, s % 2, :], gbc[:, bass.ds(u, 1), :].rearrange("p a t -> p (a t)"), ALU.mult), s, 2)
                            hop(dve.tensor_copy(hidhi[:, s, :], val[:, s % 2, :]), s, per)
                            dve.tensor_tensor(hidlo[:, s, :], val[:, s % 2, :], hidhi[:, s, :].bitcast(F32),
                                              ALU.subtract).then_inc(hid_done, 1)
                    dve.wait_ge(mm_done, u * UNIT + (n0 + UNIT))
                    for m in range(KD):
                        for v, t, src in ((0, slice(P, T), ps[:, 2 + m // 2, (m % 2) * 256:(m % 2 + 1) * 256]),
                                          (1, slice(0, P), ps[:, 6 + m // 4, (m % 4) * P:(m % 4 + 1) * P])):
                            x = dve.scalar_tensor_tensor(xT[:, m, t], src, mods[:, l, G2 + m, v:v + 1], xT[:, m, t],
                                                         ALU.mult, ALU.add)
                    x.then_inc(unit_done, 1)

            dve.memset(rope_t[:, :, :], 0.0).then_inc(unit_done, 1)
            dve.wait_ge(init_in, 16 * n_init)
            link(dve.tensor_tensor(lamprod[:, :, :], lamrow[:, :, 0, :], lamrow[:, :, 1, :], ALU.mult))
            link(dve.tensor_reduce(lamp[:, :, :].rearrange("p l i -> p (l i)"), lamprod[:, :, :], X, ALU.add))
            dve.tensor_scalar(nsink[:, :, :], sinkr[:, :, :], -1.0, None, ALU.mult).then_inc(lam_sums, 1)
            dve.wait_ge(v_ev, 2)
            link(dve.tensor_tensor(neglam[:, :], lamp[:, :, 1], lamp[:, :, 0], ALU.subtract))
            for l in range(DEPTH):
                dve.tensor_scalar(neglam[:, l:l + 1], neglam[:, l:l + 1], -(0.8 - 0.6 * math.exp(-0.3 * l)), None,
                                  ALU.add).then_inc(lam_done, 1)
            dve.wait_ge(lam_done, DEPTH)
            modulations(0)
            for l in range(DEPTH):
                b0 = BASE[l]
                normalise(2 * l)
                if l == 0:
                    lo(b0)
                    lo(b0 + 1)
                for s in range(N_WIN):
                    lo(b0 + s + 2)
                    if s in STAGED:
                        rotate(l, STAGED.index(s))
                o_low(l, 0)
                for o in range(3):
                    if o:
                        attention(l, o - 1)
                        o_low(l, o)
                    for half in range(2):
                        for j in range(2):
                            lo(gate_slot(l, o, half, j) + 2)
                        lo(branch_slot(l, o, half) + 2)
                        merge(l, o, half)
                dve.wait_ge(mh_done, l + 1)
                dve.tensor_tensor(hlo[:, :, :], macc[:, :, :], hhi[:, :, :].bitcast(F32), ALU.subtract).then_inc(merged_ready, 1)
                for j in range(4):
                    lo(out_slot(l, j + 2))
                    residual(l, out_slot(l, j), j)
                if l == 0:
                    modulations(1)
                normalise(2 * l + 1)
                if l == 0:
                    units(l)
                else:
                    router()
                    experts()
            normalise(2 * DEPTH)


_INS = ["x_prompt", "x_sample", "cache_diff_k", "cache_diff_v", "cache_win_k", "cache_win_v", "c", "c_ctx",
        "w_ada", "b_ada", "norm1_g", "norm2_g", "w_in", "w_gate", "lam_p", "subln_g", "w_pool", "pool_scale",
        "sink", "w_branch", "w_out", "w_ff_gate", "w_ff_up", "w_ff_down", "w_router", "w_ex_gate", "w_ex_up",
        "w_ex_down", "final_g"]
_OUTS = [(1, 128, 1024), (1, 256, 1024), (1, 2, 128, 4, 2, 64), (1, 2, 128, 4, 128), (1, 2, 128, 2, 64),
         (1, 2, 128, 2, 64)]


def kernel(**inputs):
    import concourse.bacc as _bacc
    from concourse.bass_utils import run_bass_kernel_spmd as _run

    nc = _bacc.Bacc("TRN2", target_bir_lowering=False, num_devices=1)
    arrays, args = {}, {}
    for name in _INS:
        x = np.ascontiguousarray(inputs[name])
        arrays[f"in_{name}_dram"] = x
        args[name] = nc.dram_tensor(f"in_{name}_dram", x.shape, mybir.dt.from_np(x.dtype), kind="ExternalInput").ap()
    const = shape_constants()
    arrays["shape_constants_dram"] = const
    cap = nc.dram_tensor("shape_constants_dram", const.shape, F32, kind="ExternalInput").ap()
    outs = [nc.dram_tensor(f"out_{i}_dram", s, F32, kind="ExternalOutput").ap() for i, s in enumerate(_OUTS)]
    prefix_step_kernel(nc, args, outs, cap)
    r = _run(nc, [arrays], core_ids=[0])
    return tuple(r.results[0][f"out_{i}_dram"] for i in range(len(_OUTS)))
```

```python
import math
from contextlib import ExitStack

import numpy as np
import concourse.bass as bass
from concourse import mybir

F32 = mybir.dt.float32
F32R = mybir.dt.float32r
ALU = mybir.AluOpType
ACT = mybir.ActivationFunctionType
X = mybir.AxisListType.X

P = 128
D = 1024
KD = D // P
DEPTH = 2
BLK = 3
T = BLK * P
GRID_W = 64
HA, DHA = 4, 64
HC, KVC, DHC = 8, 2, 64
WINDOWS = (2, 4, 8, 16)
EPS = 1e-6
NEG = -1e30
A_COLS = HA * 2 * DHA
IN_W = 3 * A_COLS + 512 + HC * DHC + 2 * KVC * DHC
D_FF = 2816
F_U = 1408
KF = F_U // P
N_EXP = 8
N_HALF = D_FF // F_U
MAX_TASKS = N_EXP + (2 * T - 1) // (P + 1)

RING = 3
SLOT = 16 * P
N_WIN = IN_W // 256
ORDER = (1, 0, 2)
N_MIX = N_WIN + 3 * 6 + 4
GU = KF
DOWN = ((0, 1), (2,), (3, 4), (5,), (6, 7), (8,), (9, 10))
UNIT = GU + len(DOWN)
SCATTER = (2, 4, 6, 7)
assert N_MIX % RING == 0 and UNIT % RING == 0
N_ADA = 6 * D // P
ADA_SLOTS = (9, 12, 12, 8, 7)
ADA_AT = [sum(ADA_SLOTS[:i]) for i in range(6)]
assert ADA_AT[-1] == DEPTH * N_ADA // 2 and (ADA_SLOTS[0] + sum(ADA_SLOTS[1:3])) % RING == 0 == sum(ADA_SLOTS[3:]) % RING
UNITS_AT = [ADA_AT[3] + N_MIX, ADA_AT[5] + 2 * N_MIX + N_HALF * UNIT]
BASE = (ADA_AT[1], UNITS_AT[0] + N_HALF * UNIT)
STAGED = (0, 1, 2, 3, 8, 9, 10)
WIN_INC = N_WIN + 1
KV_SLOTS = (2, 3, 4, 5, 10)
N_TR = len(STAGED) + 1

R_BADA, R_N1, R_N2, R_PS, R_SUB, R_C, R_CTX, R_FIN, R_END = 0, 48, 56, 64, 68, 69, 77, 85, 93
SH1, SC1, G1, SH2, SC2, G2 = (8 * i for i in range(6))


def shape_constants():
    ident = np.eye(P, dtype=np.float32)
    pool = np.zeros((P, 4, T + 2 * P), np.float32)

    def mean_minus_self(n, w):
        m = np.zeros((n, n), np.float32)
        for t in range(n):
            lo, hi = max(t - w // 2, 0), min(t + w - w // 2, n)
            m[lo:hi, t] = np.float32(1.0) / np.float32(hi - lo)
            m[t, t] -= 1.0
        return m

    for g, w in enumerate(WINDOWS):
        pool[:, g, 0:P] = mean_minus_self(P, w)
        m = mean_minus_self(2 * P, w)
        pool[:, g, P:P + 256] = m[0:P]
        pool[:, g, P + 256:P + 512] = m[P:256]
    q = np.arange(P)
    mask = np.zeros((P, 2, P), np.float32)
    mask[:, 0, :] = np.where(q[None, :] <= q[:, None], 0.0, NEG)
    mask[:, 1, :] = np.where(q[None, :] >= q[:, None], 0.0, NEG)
    inv = 10000.0 ** (-np.arange(0, 32, 2, dtype=np.float32) / np.float32(32))
    t = np.arange(2 * P)
    ang = np.stack([(t // GRID_W)[:, None] * inv, (t % GRID_W)[:, None] * inv], 1).astype(np.float32)
    rope = np.zeros((P, 2, 2, 32), np.float32)
    for b in range(2):
        a = ang[b * P:(b + 1) * P].reshape(P, 32)
        rope[:, b, 0], rope[:, b, 1] = np.cos(a), np.sin(a)
    tri = np.zeros((P, 8, 8), np.float32)
    tri[:] = (np.arange(8)[None, :] < np.arange(8)[:, None])
    before = (q[:, None] < q[None, :]).astype(np.float32)
    slots = np.broadcast_to(np.arange(P, dtype=np.float32), (P, P))
    return np.concatenate([ident, mask.reshape(P, 256), rope.reshape(P, 128), tri.reshape(P, 64),
                           pool.reshape(P, -1), before, slots], 1).astype(np.float32)


C_MASK, C_ROPE, C_TRI, C_POOL = 128, 384, 512, 576
POOL_COLS = 4 * (T + 2 * P)
C_SLOT = C_POOL + POOL_COLS
SLOT_COLS = 2 * P


def prefix_step_kernel(nc, a, outs, const):
    y_prompt, y_sample, new_dk, new_dv, new_wk, new_wv = outs
    ctx = ExitStack()
    with ctx:
        top = [(nc.sbuf_base + 31) // 32 * 32]
        sb_end = nc.sbuf_base + nc.sbuf_bytes_remaining

        def at(name, cols, offset, dt=F32, shape=None):
            return nc.alloc_sbuf_tensor_at(name, [P] + list(shape or [cols]), dt, offset=offset)

        def place(name, shape, dt=F32):
            n = int(np.prod(shape)) * 4
            t = nc.alloc_sbuf_tensor_at(name, [P] + list(shape), dt, offset=top[0])
            top[0] += (n + 31) // 32 * 32
            return t

        def sem(name):
            return ctx.enter_context(nc.semaphore(name))

        raw = place("raw", [RING, SLOT])
        whi = place("whi", [RING, SLOT], F32R)
        wlo = place("wlo", [RING, SLOT], F32R)
        yhi = place("yhi", [D], F32R)
        xT = place("xT", [KD, T])
        hhi = place("hhi", [KD, T], F32R)
        hlo = place("hlo", [KD, T], F32R)
        scratch_at = top[0]
        macc = place("macc", [KD, T])
        gbuf_at = top[0]
        gbuf = place("gbuf", [4, T])
        oraw_at = top[0]
        oraw = place("oraw", [4, T])
        ohi_at = top[0]
        ohi = place("ohi", [4, T], F32R)
        olo_at = top[0]
        olo = place("olo", [4, T], F32R)
        rstd = place("rstd", [T])
        cst = place("cst", [C_POOL])
        ones = place("ones", [P])
        epsc = place("epsc", [1])
        wpool = place("wpool", [4, P])
        wrout = place("wrout", [KD, N_EXP])
        cols = place("cols", [DEPTH, R_END])
        silc = place("silc", [2, KD])
        sil4 = place("sil4", [KD, 4], F32R)
        adarow = place("adarow", [256])
        mods4 = place("mods4", [DEPTH, N_ADA, 4])
        mods = place("mods", [DEPTH, N_ADA, 2])
        amul = place("amul", [DEPTH, 2, KD, 2])
        subg = place("subg", [DEPTH])
        sinkr = place("sinkr", [DEPTH, HC])
        nsink = place("nsink", [DEPTH, HC])
        lamp = place("lamp", [DEPTH, 2])
        neglam = place("neglam", [DEPTH])
        small = place("small", [2, 10])
        rsm = place("rsm", [BLK, 16])
        posq = place("posq", [BLK, MAX_TASKS + 1])
        gwq = place("gwq", [BLK, MAX_TASKS + 1])
        posx = place("posx", [BLK, N_EXP])
        gwe = place("gwe", [BLK, N_EXP])
        gws = place("gws", [1])
        tasks = place("tasks", [MAX_TASKS + 2], mybir.dt.int32)
        shared = top[0]
        vtok = place("vtok", [BLK, 640])
        utok = place("utok", [BLK, 512])
        qTA = place("qTA", [4, T])
        kTA = place("kTA", [4, 512])
        qTC = place("qTC", [4, T])
        kTC = place("kTC", [2, 512])
        stage = place("stage", [2, BLK, 256])
        ctxv = place("ctxv", [640])
        assert top[0] <= sb_end, (top[0], sb_end)
        pt = at("pt", 2 * T, stage_off := top[0] - 2560 - 2 * BLK * 256 * 4, shape=[2, T])
        pooled = at("pooled", 4 * T, gbuf_at, shape=[4, T])
        ebuf = at("ebuf", 4 * T, gbuf_at, shape=[2, 2, T])
        osq = at("osq", 4 * T, gbuf_at, shape=[4, T])
        ctxk = at("ctxk", 768, gbuf_at, shape=[768])
        kcd = at("kcd", 768, gbuf_at + 3072, shape=[BLK, 256])
        vrows = at("vrows", 2 * P, gbuf_at, shape=[DEPTH, P])
        lamrow = at("lamrow", 512, gbuf_at + 1024, shape=[DEPTH * 2, 2, DHA])
        lamprod = at("lamprod", 256, gbuf_at + 3072, shape=[DEPTH * 2, DHA])
        xtok = at("xtok", BLK * D, scratch_at, shape=[BLK, D])
        poolm = at("poolm", POOL_COLS, scratch_at, shape=[4, T + 2 * P])
        hidhi = at("hidhi", KF * T, shared, F32R, [KF, T])
        hidlo = at("hidlo", KF * T, shared + KF * T * 4, F32R, [KF, T])
        sil = at("sil", 2 * T, shared + 2 * KF * T * 4, shape=[2, T])
        val = at("val", 2 * T, shared + 2 * KF * T * 4 + 3072, shape=[2, T])
        gat = at("gat", T, ohi_at, F32R, [BLK, P])
        gas = at("gas", T, ohi_at + 4 * T, shape=[BLK, P])
        sct = at("sct", T, ohi_at + 8 * T, F32R)
        xgh = at("xgh", D, olo_at, F32R, [KD, P])
        ehh = at("ehh", KF * P, shared, F32R, [KF, P])
        ehl = at("ehl", KF * P, shared + 4 * KF * P, F32R, [KF, P])
        xgl = at("xgl", D, shared + 8 * KF * P, F32R, [KD, P])
        ylo = at("ylo", D, shared + 8 * KF * P + 4 * D, F32R)
        esil = at("esil", 2 * P, gbuf_at + 1536, shape=[2, P])
        evalu = at("evalu", 2 * P, gbuf_at + 1536 + 8 * P, shape=[2, P])
        slotc = at("slotc", SLOT_COLS, gbuf_at + 1536 + 16 * P)
        NQ = MAX_TASKS + 1
        owner = at("owner", NQ * N_EXP, gbuf_at + 1536, shape=[NQ, N_EXP])
        by_task = at("by_task", BLK * NQ * N_EXP, gbuf_at + 1536 + 4 * NQ * N_EXP, shape=[BLK, NQ, N_EXP])
        tk = at("tk", 6 * NQ, oraw_at, shape=[6, NQ])
        assert 4 * (BLK + 1) * NQ * N_EXP <= 16 * P and 1536 + 16 * P + 4 * SLOT_COLS <= 4 * 4 * T
        htok = [x[:, :, :].rearrange("p k t -> p (k t)").rearrange("p (b d) -> p b d", b=BLK) for x in (hhi, hlo)]
        ssum = at("ssum", 2 * T, olo_at, shape=[2, T])
        yout = at("yout", BLK * D, shared, shape=[BLK, D])
        rcmp = at("rcmp", 2 * BLK * 64, gbuf_at, shape=[2, BLK, 64])
        rope_t = at("rope_t", 256, oraw_at, shape=[2, 128])
        assert top[0] <= sb_end, (top[0], sb_end)
        assert shared + 2 * KF * T * 4 + 6144 <= sb_end

        ident = cst[:, 0:P]
        mask = cst[:, C_MASK:C_ROPE].rearrange("p (i k) -> p i k", i=2)
        rope = cst[:, C_ROPE:C_TRI].rearrange("p (b c i) -> p b c i", b=2, c=2)
        tri = cst[:, C_TRI:C_POOL]
        ps = ctx.enter_context(nc.psum_tensor("ps", [P, 8, 512], F32))

        def pair(g):
            return ps[:, 2 * g:2 * g + 2, 0:T]

        raw_in = [sem(f"raw_in{j}") for j in range(RING)]
        hi_done, lo_done, mm_done = sem("hi_done"), sem("lo_done"), sem("mm_done")
        ada_row, ada_turned, ada_read = sem("ada_row"), sem("ada_turned"), sem("ada_read")
        init_in, ones_set = sem("init_in"), sem("ones_set")
        x_tr, x_ev, v_tr, v_ev = sem("x_tr"), sem("x_ev"), sem("v_tr"), sem("v_ev")
        silc_done, silh_done, silc_ready = sem("silc_done"), sem("silh_done"), sem("silc_ready")
        sqs_done, mod_done = sem("sqs_done"), sem("mod_done")
        sq_done, ssq_done, xn_done, hf_done = sem("sq_done"), sem("ssq_done"), sem("xn_done"), sem("hf_done")
        h_ready = sem("h_ready")
        win_evac, rope_done, tr_done, tr_evac = sem("win_evac"), sem("rope_done"), sem("tr_done"), sem("tr_evac")
        layer_in = [sem(f"layer_in{l}") for l in range(DEPTH)]
        poolm_in, kv_out = sem("poolm_in"), sem("kv_out")
        pool_mm, pool_ev, pooly_mm = sem("pool_mm"), sem("pool_ev"), sem("pooly_mm")
        s_done, nmax_done, e_done, p_done = sem("s_done"), sem("nmax_done"), sem("e_done"), sem("p_done")
        tp_done, pt_evac, pv_done, o_evac = sem("tp_done"), sem("pt_evac"), sem("pv_done"), sem("o_evac")
        osq_done, oss_done, on_done = sem("osq_done"), sem("oss_done"), sem("on_done")
        oh_done, o_ready = sem("oh_done"), sem("o_ready")
        gate_evac, merge_done = sem("gate_evac"), sem("merge_done")
        mh_done, merged_ready, out_evac = sem("mh_done"), sem("merged_ready"), sem("out_evac")
        rt_done, gates_ready, sel_ready = sem("rt_done"), sem("gates_ready"), sem("sel_ready")
        h2_tr, h2_hi, h2_lo, slotc_in, pos_mm = sem("h2_tr"), sem("h2_hi"), sem("h2_lo"), sem("slotc_in"), sem("pos_mm")
        pos_ready, exp_init = sem("pos_ready"), sem("exp_init")
        gat_ready, gather_done, xgh_done, xg_ready = sem("gat_ready"), sem("gather_done"), sem("xgh_done"), sem("xg_ready")
        esil_done, val_done, ht_done, ehh_done = sem("esil_done"), sem("val_done"), sem("ht_done"), sem("ehh_done")
        ehid_done, yh_done, yl_done = sem("ehid_done"), sem("yh_done"), sem("yl_done")
        gas_ready, st_done, sct_ready = sem("gas_ready"), sem("st_done"), sem("sct_ready")
        sc_done, sc_evac = sem("sc_done"), sem("sc_evac")
        sil_done, hid_done, unit_done = sem("sil_done"), sem("hid_done"), sem("unit_done")
        y_tr, y_ev, y_out = sem("y_tr"), sem("y_ev"), sem("y_out")
        chain_v, chain_u, chain_m = sem("chain_v"), sem("chain_u"), sem("chain_m")
        rms_done, orms_done = sem("rms_done"), sem("orms_done")
        lam_done, lam_sums, chain_p = sem("lam_done"), sem("lam_sums"), sem("chain_p")
        rt_sub, rt_exp, wrout_in = sem("rt_sub"), sem("rt_exp"), sem("wrout_in")

        n_init = 3 + 8 * DEPTH + 2

        def gate_slot(l, o, half, j):
            return BASE[l] + N_WIN + 6 * o + 3 * half + j + sum(ADA_SLOTS[2 * l + 1:2 * l + 1 + min(o, 2)])

        def branch_slot(l, o, half):
            return gate_slot(l, o, half, 2)

        def out_slot(l, j):
            return gate_slot(l, 3, 0, 0) + j

        def ada_slot(phase, i):
            if phase == 0:
                return i
            l, kind = (phase - 1) // 2, (phase - 1) % 2
            return gate_slot(l, kind + 1, 0, 0) - ADA_SLOTS[phase] + i

        def raw_wait(eng, n, more=0):
            eng.wait_ge(raw_in[n % RING], more + 32 * (n // RING + 1))

        block = ctx.enter_context(nc.Block())

        @block.sync
        def _(sp):
            def halves(n, dst, src, axis_cols=None):
                if n >= RING:
                    sp.wait_ge(lo_done, n - RING + 1)
                for i in range(2):
                    sp.dma_start(dst[i], src[i]).then_inc(raw_in[n % RING], 16)

            def k_by_cols(n, w, k, c0, width):
                d = raw[:, n % RING, 0:k * width].rearrange("p (k c) -> p k c", k=k)
                s = w.rearrange("(k p) c -> p k c", p=P)[:, :, c0:c0 + width]
                halves(n, [d[:, 0:k // 2], d[:, k // 2:k]], [s[:, 0:k // 2], s[:, k // 2:k]])

            def unit_slot(w, s):
                j = s % RING
                if s < GU:
                    d = raw[:, j, :].rearrange("p (w k c) -> p w k c", w=2, k=KD)
                    pieces = [(d[:, i], w[i][:, :, s * P:(s + 1) * P]) for i in range(2)]
                else:
                    f = DOWN[s - GU]
                    d = raw[:, j, 0:len(f) * D].rearrange("p (k c) -> p k c", c=D)
                    h = D // 2
                    pieces = [(d[:, :, i * h:(i + 1) * h], w[2][:, f[0]:f[-1] + 1, i * h:(i + 1) * h])
                              for i in range(2)]
                for dst, src in pieces:
                    sp.dma_start(dst, src).then_inc(raw_in[j], 16)

            def modulation(phase):
                for i in range(ADA_SLOTS[phase]):
                    l, c = divmod(ADA_AT[phase] + i, N_ADA // 2)
                    k_by_cols(ada_slot(phase, i), a["w_ada"][l], KD, 256 * c, 256)

            sp.dma_start(cst[:, :], const[:, 0:C_POOL]).then_inc(init_in, 16)
            sp.dma_start(xtok[:, 0, :], a["x_prompt"][0]).then_inc(init_in, 16)
            sp.dma_start(xtok[:, 1:3, :], a["x_sample"][0].rearrange("(b p) d -> p b d", p=P)).then_inc(init_in, 16)
            for l in range(DEPTH):
                for r, src in ((R_BADA, a["b_ada"][l]), (R_N1, a["norm1_g"][l]), (R_N2, a["norm2_g"][l]),
                               (R_PS, a["pool_scale"][l]), (R_SUB, a["subln_g"][l]), (R_C, a["c"][0]),
                               (R_CTX, a["c_ctx"]), (R_FIN, a["final_g"])):
                    rows = src.shape[0] // P
                    sp.dma_start(vrows[r:r + rows, l, :], src.rearrange("(r c) -> r c", c=P)).then_inc(init_in, 16)
            sp.dma_start(lamrow[:, :, :].rearrange("p a b c -> p (a b c)"),
                         a["lam_p"].rearrange("(o l) r d -> o (l r d)", o=1).to_broadcast([P, DEPTH * 4 * DHA])
                         ).then_inc(init_in, 16)
            sp.dma_start(sinkr[:, :, :].rearrange("p l h -> p (l h)"),
                         a["sink"].rearrange("(o l) h -> o (l h)", o=1).to_broadcast([P, DEPTH * HC])
                         ).then_inc(init_in, 16)
            modulation(0)
            for l in range(DEPTH):
                for s in range(N_WIN):
                    k_by_cols(BASE[l] + s, a["w_in"][l], KD, 256 * s, 256)
                for o, br in enumerate(ORDER):
                    if o:
                        modulation(2 * l + o)
                    for half in range(2):
                        for j in range(2):
                            k_by_cols(gate_slot(l, o, half, j), a["w_gate"][l], KD,
                                      br * D + 512 * half + 256 * j, 256)
                        k_by_cols(branch_slot(l, o, half), a["w_branch"][l, br], 4, 512 * half, 512)
                for j in range(4):
                    k_by_cols(out_slot(l, j), a["w_out"][l], KD, 256 * j, 256)
                if l == 0:
                    n0 = UNITS_AT[l]
                    with sp.Fori(0, N_HALF) as u:
                        w = [x.rearrange("(k p) c -> p k c", p=P) for x in (
                            a["w_ff_gate"][0][:, bass.ds(u * F_U, F_U)], a["w_ff_up"][0][:, bass.ds(u * F_U, F_U)],
                            a["w_ff_down"][0][bass.ds(u * F_U, F_U), :])]
                        for s in range(UNIT):
                            sp.wait_ge(lo_done, u * UNIT + (n0 + s - RING + 1))
                            unit_slot(w, s)
            n0 = UNITS_AT[1]

            def expert(e):
                return [a[f"w_ex_{x}"][0, e].rearrange("(k p) c -> p k c", p=P) if isinstance(e, int) else
                        a[f"w_ex_{x}"][0, bass.ds(e, 1)].rearrange("e (k p) c -> p (e k) c", p=P)
                        for x in ("gate", "up", "down")]

            for s in range(RING):
                sp.wait_ge(lo_done, n0 + s - RING + 1)
                unit_slot(expert(0), s)
            sp.wait_ge(pos_ready, 1)
            n_tasks = sp.value_load(tasks[0:1, NQ:NQ + 1], min_val=N_EXP, max_val=MAX_TASKS)
            with sp.Fori(0, n_tasks) as q:
                w, after = [expert(sp.value_load(tasks[0:1, bass.ds(i, 1)], min_val=0, max_val=N_EXP - 1))
                            for i in (q, q + 1)]
                for s in range(UNIT):
                    ahead = s == GU - RING - 1
                    if s != GU - RING:
                        sp.wait_ge(lo_done, q * UNIT + (n0 + s + ahead + 1))
                    unit_slot(w if s + RING < UNIT else after, (s + RING) % UNIT)
        @block.gpsimd
        def _(pool):
            pool.memset(epsc[:, :], EPS)
            pool.memset(ones[:, :], 1.0).then_inc(ones_set, 1)

            def layer_loads(l):
                if l == 0:
                    pool.wait_ge(v_ev, 2)
                    pool.wait_ge(lam_done, DEPTH)
                else:
                    pool.wait_ge(merge_done, 6 * l)
                ck = a["cache_win_k"][0, l].rearrange("t g d -> t (g d)")
                pool.dma_start(ctxk[:, 0:512], a["cache_diff_k"][0, l].rearrange("t h m d -> t (h m d)")).then_inc(layer_in[l], 16)
                for i in range(2):
                    for g in range(2):
                        pool.dma_start(ctxk[:, 512 + g * 128 + i * 64:512 + g * 128 + i * 64 + 64],
                                       ck[:, g * 64:(g + 1) * 64]).then_inc(layer_in[l], 16)
                pool.dma_start(ctxv[:, 0:512], a["cache_diff_v"][0, l].rearrange("t h e -> t (h e)")).then_inc(layer_in[l], 16)
                pool.dma_start(ctxv[:, 512:640], a["cache_win_v"][0, l].rearrange("t g d -> t (g d)")).then_inc(layer_in[l], 16)
                pool.dma_start(wpool[:, :, :], a["w_pool"][l].rearrange("g c e -> c g e")).then_inc(layer_in[l], 16)
                pool.wait_ge(h_ready, 4 * l + 2)
                pool.dma_start(poolm[:, :, :].rearrange("p g c -> p (g c)"), const[:, C_POOL:C_POOL + POOL_COLS]).then_inc(poolm_in, 16)

            layer_loads(0)
            pool.dma_start(wrout[:, :, :], a["w_router"][0].rearrange("(k p) e -> p k e", p=P)).then_inc(wrout_in, 16)
            pool.wait_ge(unit_done, 4 + 4 * N_HALF)
            layer_loads(1)
            pool.wait_ge(merge_done, 6 * DEPTH)
            pool.dma_start(slotc[:, :], const[:, C_SLOT:C_SLOT + SLOT_COLS]).then_inc(slotc_in, 16)

        @block.tensor
        def _(pe):
            def mm3(out, s, m, first, last, **kw):
                pe.matmul(out, s[0], m[0], start=first, stop=False, **kw)
                pe.matmul(out, s[0], m[1], start=False, stop=False, **kw)
                return pe.matmul(out, s[1], m[0], start=False, stop=last, **kw)

            def slot(n, k):
                return [w[:, n % RING, :].rearrange("p (k c) -> p k c", k=k) for w in (whi, wlo)]

            def ada_product(phase, i):
                n = ada_slot(phase, i)
                if i:
                    ada_transposes(phase, i - 1)
                pe.wait_ge(lo_done, n + 1)
                for j, w in enumerate(slot(n, KD)):
                    for k in range(KD):
                        mm = pe.matmul(ps[0:4, 7, 0:256], sil4[:, k, :], w[:, k, :], start=(j + k == 0), stop=(j + k == KD))
                mm.then_inc(mm_done, 1)

            def ada_transposes(phase, i):
                pe.wait_ge(ada_row, ADA_AT[phase] + i + 1)
                for c in range(2):
                    mm = pe.transpose(ps[:, 7, 256 + 4 * c:260 + 4 * c], adarow[0:4, c * P:(c + 1) * P], ident[0:4, 0:4])
                return mm

            def ada_end(phase):
                ada_transposes(phase, ADA_SLOTS[phase] - 1).then_inc(ada_turned, 1)

            def sum_squares(i):
                for half in range(2):
                    pe.wait_ge(sqs_done, 2 * i + half + 1)
                    mm = pe.matmul(ps[:, 6, 0:T], ones[:, :], ssum[:, half, :], start=(half == 0), stop=(half == 1))
                mm.then_inc(ssq_done, 1)

            def rot_transposes(l, ti):
                r = N_TR * l + ti
                pe.wait_ge(rope_done, len(STAGED) * l + ti + 1)
                if r >= 1:
                    pe.wait_ge(tr_evac, r)
                for c in range(2):
                    for b in range(BLK):
                        src = kcd[:, b, c * P:(c + 1) * P] if ti == 6 else stage[:, ti % 2, b, c * P:(c + 1) * P]
                        mm = pe.transpose(ps[:, 4 + c, b * P:(b + 1) * P], src, ident)
                mm.then_inc(tr_done, 1)

            def input_projection(l):
                pe.wait_ge(h_ready, 4 * l + 2)
                for s in range(N_WIN):
                    n = BASE[l] + s
                    pe.wait_ge(lo_done, n + 1)
                    g = s % 2
                    if s >= 2:
                        pe.wait_ge(win_evac, WIN_INC * l + s - 1)
                    w = slot(n, KD)
                    out = ps[:, 2 * g:2 * g + 2, :].rearrange("p a c -> p (a c)")
                    for b in range(BLK):
                        for k in range(KD):
                            mm = mm3(out[:, b * 256:(b + 1) * 256], [h[:, k, b * P:(b + 1) * P] for h in (hhi, hlo)],
                                     [x[:, k, :] for x in w], k == 0, k == KD - 1)
                    mm.then_inc(mm_done, 1)
                    if s - 1 in STAGED:
                        rot_transposes(l, STAGED.index(s - 1))
                rot_transposes(l, 6)
                pe.wait_ge(layer_in[l], 16 * 8)
                pe.wait_ge(tr_evac, N_TR * l + 7)
                for c in range(6):
                    mm = pe.transpose(ps[:, 4 + c // 4, (c % 4) * P:(c % 4 + 1) * P], ctxk[:, c * P:(c + 1) * P], ident)
                mm.then_inc(tr_done, 1)

            def pooling(l):
                pe.wait_ge(win_evac, WIN_INC * (l + 1))
                pe.wait_ge(poolm_in, 16 * (l + 1))
                for g in range(4):
                    u = [utok[:, b, g * P:(g + 1) * P] for b in range(BLK)]
                    pe.matmul(ps[:, g, 0:P], u[0], poolm[:, g, 0:P], start=True, stop=True)
                    pe.matmul(ps[:, g, P:T], u[1], poolm[:, g, P:P + 256], start=True, stop=False)
                    mm = pe.matmul(ps[:, g, P:T], u[2], poolm[:, g, P + 256:P + 512], start=False, stop=True)
                mm.then_inc(pool_mm, 1)
                pe.wait_ge(tr_evac, N_TR * (l + 1))
                pe.wait_ge(pool_ev, l + 1)
                for g in range(4):
                    mm = pe.matmul(ps[:, 4 + g, 0:T], wpool[:, g, :], pooled[:, g, :], start=True, stop=True)
                mm.then_inc(pooly_mm, 1)

            def attention(l, kind):
                st0 = 24 * l + 12 * kind
                it0 = 36 * l + 12 * kind
                per = 1 + kind
                phase = 1 + 2 * l + kind

                def scores(t):
                    h, qb = t // 3, t % 3
                    if t >= 2:
                        pe.wait_ge(e_done, st0 + t - 1)
                    nk, k0 = (P, 0) if qb == 0 else (T, P)
                    q, kk = (qTA, kTA[:, h, k0:k0 + nk]) if kind == 0 else (qTC, kTC[:, h // 2, k0:k0 + nk])
                    for m in range(2):
                        r = slice(64 * m, 64 * m + 64)
                        out, lhs = ps[:, 2 * (t % 2) + m, 0:nk], q[r, h, qb * P:(qb + 1) * P]
                        if kind == 0 or qb == 0:
                            mm = pe.matmul(out, lhs, kk[r], start=True, stop=True)
                            continue
                        o3, k3 = (x.rearrange("p (a c) -> p a c", c=P) for x in (out, kk[r]))
                        far = 2 - qb
                        near = slice(0, 3, 2) if far else slice(1, 3)
                        pe.matmul(o3[:, near, :], lhs, k3[:, near, :], start=True, stop=True)
                        pe.matmul(o3[:, far, :], lhs, k3[:, far, :], start=True, stop=False)
                        mm = pe.matmul(o3[:, far, :], ident, mask[:, qb - 1, :], start=False, stop=True)
                    mm.then_inc(s_done, 1)

                def transposes(i):
                    t, m = i // per, i % per
                    if m == 0:
                        pe.wait_ge(p_done, st0 + t + 1)
                    if it0 + i >= 2:
                        pe.wait_ge(pt_evac, it0 + i - 1)
                    for kb in range(1 if t % 3 == 0 else 3):
                        mm = pe.transpose(ps[:, 4 + (it0 + i) % 2, kb * P:(kb + 1) * P],
                                          ebuf[:, t % 2, m, kb * P:(kb + 1) * P], ident)
                    mm.then_inc(tp_done, 1)

                def values(i):
                    t, m = i // per, i % per
                    h, qb = t // 3, t % 3
                    pe.wait_ge(pt_evac, it0 + i + 1)
                    grp = 8 * l + 4 * kind + h
                    if qb == 0 and m == 0 and grp >= 1:
                        pe.wait_ge(o_evac, grp)
                    c = slice(h * P, (h + 1) * P) if kind == 0 else slice(512 + (h // 2) * 64, 576 + (h // 2) * 64)
                    keys = [vtok[:, 0, c]] if qb == 0 else [vtok[:, 1, c], vtok[:, 2, c], ctxv[:, c]]
                    rows = slice(0, P) if kind == 0 else slice(64 * m, 64 * m + 64)
                    for kb, v in enumerate(keys):
                        mm = pe.matmul(ps[rows, 6, qb * P:(qb + 1) * P], v,
                                       pt[:, (it0 + i) % 2, kb * P:(kb + 1) * P],
                                       start=(kb == 0), stop=(kb == len(keys) - 1))
                    mm.then_inc(pv_done, 1)

                pe.wait_ge(gate_evac, 12 * l + 4 * (kind + 1))
                scores(0)
                pe.wait_ge(merge_done, 6 * l + 2 * (kind + 1))
                n = 12 * per
                for i in range(n):
                    if i % per == 0 and i // per + 1 < 12:
                        scores(i // per + 1)
                    if i % per == 0 and i // per < ADA_SLOTS[phase]:
                        ada_product(phase, i // per)
                    transposes(i)
                    if i >= 1:
                        values(i - 1)
                values(n - 1)
                ada_end(phase)
                if kind == 0:
                    pe.wait_ge(osq_done, l + 1)
                    pe.wait_ge(ada_read, phase + 1)
                    for h in range(4):
                        mm = pe.matmul(ps[:, 4 + h, 0:T], ones[:, :], osq[:, h, :], start=True, stop=True)
                    mm.then_inc(oss_done, 1)

            def wide(l, n, w, x):
                for j in range(2):
                    for k in range(KD):
                        if n == out_slot(l, 0) and j == 0 and k == KD // 2:
                            pe.wait_ge(merged_ready, 2 * l + 2)
                        mm = mm3(ps[:, 2 * (n % 2) + j, 0:T], [y[:, k, j * P:(j + 1) * P] for y in w],
                                 [y[:, k, :] for y in x], k == 0, k == KD - 1)
                mm.then_inc(mm_done, 1)

            def branch(l, o):
                for half in range(2):
                    i = 6 * l + 2 * o + half
                    for j in range(2):
                        n = gate_slot(l, o, half, j)
                        pe.wait_ge(lo_done, n + 1)
                        if i and j == 0:
                            pe.wait_ge(gate_evac, 2 * i)
                        if o and half == 0 and j == 0:
                            pe.wait_ge(e_done, 24 * l + 12 * o)
                        wide(l, n, slot(n, KD), (hhi, hlo))
                    n = branch_slot(l, o, half)
                    pe.wait_ge(lo_done, n + 1)
                    pe.wait_ge(o_ready, 3 * l + o + 1)
                    if o:
                        pe.wait_ge(ada_read, 2 * l + o + 1)
                    if half:
                        pe.wait_ge(merge_done, i)
                    w = slot(n, 4)
                    for q in range(4):
                        for k in range(4):
                            mm = mm3(ps[:, 4 + q, 0:T], [y[:, k, q * P:(q + 1) * P] for y in w],
                                     [y[:, k, :] for y in (ohi, olo)], k == 0, k == 3)
                    mm.then_inc(mm_done, 1)

            def out_projection(l):
                pe.wait_ge(merged_ready, 2 * l + 1)
                pe.wait_ge(gate_evac, 12 * (l + 1))
                for j in range(4):
                    n = out_slot(l, j)
                    pe.wait_ge(lo_done, n + 1)
                    if j >= 2:
                        pe.wait_ge(out_evac, 4 * l + j - 1)
                    wide(l, n, slot(n, KD), (hhi, hlo))

            def router():
                pe.wait_ge(chain_m, 4 * 4)
                pe.wait_ge(mod_done, 2 * 4)
                pe.wait_ge(wrout_in, 16)
                for b in range(BLK):
                    for k in range(KD):
                        mm = pe.matmul(ps[:, 6, b * N_EXP:(b + 1) * N_EXP], macc[:, k, b * P:(b + 1) * P],
                                       wrout[:, k, :], start=(k == 0), stop=(k == KD - 1))
                mm.then_inc(rt_done, 1)
                for b in range(BLK):
                    for k in range(KD):
                        mm = pe.transpose(ps[:, 2 * b + k // 4, (k % 4) * P:(k % 4 + 1) * P],
                                          macc[:, k, b * P:(b + 1) * P], ident)
                mm.then_inc(h2_tr, 1)
                pe.wait_ge(sel_ready, 1)
                pe.wait_ge(slotc_in, 16)
                for b in range(BLK):
                    for c in range(b):
                        pe.matmul(ps[:, 6, b * N_EXP:(b + 1) * N_EXP], ones[:, :], rsm[:, c, 0:8],
                                  start=(c == 0), stop=False)
                    pe.matmul(ps[:, 6, b * N_EXP:(b + 1) * N_EXP], slotc[:, 0:P], rsm[:, b, 0:8], start=(b == 0), stop=True)
                for b in range(BLK):
                    mm = pe.matmul(ps[:, 6, 24:32], ones[:, :], rsm[:, b, 0:8], start=(b == 0), stop=(b == BLK - 1))
                mm.then_inc(pos_mm, 1)
                pe.wait_ge(h2_lo, 1)

            def gather():
                for m in range(KD):
                    for i, h in enumerate(htok):
                        for b in range(BLK):
                            mm = pe.matmul(ps[:, 2 + m // 4, (m % 4) * P:(m % 4 + 1) * P], h[:, b, m * P:(m + 1) * P],
                                           gat[:, b, :], start=(i + b == 0), stop=(i + b == BLK))
                mm.then_inc(gather_done, 1)

            def hidden_turned(s, q):
                pe.wait_ge(val_done, q * GU + (s + 1))
                if s >= 2:
                    pe.wait_ge(ehid_done, q * GU + (s - 1))
                pe.transpose(ps[:, 6 + s % 2, 0:P], evalu[:, s % 2, :], ident).then_inc(ht_done, 1)

            def scatter_turned(q):
                pe.wait_ge(sc_evac, 8 * q + 8)
                pe.wait_ge(gas_ready, q + 1)
                for b in range(BLK):
                    pe.transpose(ps[:, 2, b * P:(b + 1) * P], gas[:, b, :], ident)
                for b in range(BLK):
                    mm = pe.matmul(ps[:, 2, T:T + 1], gas[:, b, :], gwq[:, b, bass.ds(q, 1)], start=(b == 0),
                                   stop=(b == BLK - 1))
                mm.then_inc(st_done, 1)

            def scatter(s, q):
                if s == SCATTER[0]:
                    pe.wait_ge(yl_done, q + 1)
                    pe.wait_ge(sct_ready, q + 1)
                for m in range(8):
                    if SCATTER[m // 2] == s:
                        if m >= 2:
                            pe.wait_ge(sc_evac, 8 * q + (m - 1))
                        for i, y in enumerate((yhi, ylo)):
                            mm = pe.matmul(ps[:, 2 + m % 2, 0:T], y[:, m * P:(m + 1) * P], sct[:, :],
                                           start=(i == 0), stop=(i == 1))
                        mm.then_inc(sc_done, 1)

            def experts():
                n0 = UNITS_AT[1]
                pe.wait_ge(gat_ready, 1)
                pe.wait_ge(gates_ready, 1)
                n_tasks = pe.value_load(tasks[0:1, NQ:NQ + 1], min_val=N_EXP, max_val=MAX_TASKS)
                gather()
                with pe.Fori(0, n_tasks) as q:
                    pe.wait_ge(xg_ready, q + 1)
                    for s in range(GU):
                        pe.wait_ge(lo_done, q * UNIT + (n0 + s + 1))
                        if s >= 2:
                            pe.wait_ge(val_done, q * GU + (s - 1))
                        w = [x[:, s % RING, :].rearrange("p (w k c) -> p w k c", w=2, k=KD) for x in (whi, wlo)]
                        for k in range(KD):
                            mm = mm3(ps[:, s % 2, 0:2 * P].rearrange("p (w c) -> p w c", w=2), [y[:, k, :] for y in (xgh, xgl)],
                                     [y[:, :, k, :] for y in w], k == 0, k == KD - 1)
                        mm.then_inc(mm_done, 1)
                        if s:
                            hidden_turned(s - 1, q)
                        scatter(s, q)
                        if s == 8:
                            scatter_turned(q)
                    pe.wait_ge(sct_ready, q + 2)
                    pe.wait_ge(gat_ready, q + 2)
                    gather()
                    hidden_turned(GU - 1, q)
                    for i, f in enumerate(DOWN):
                        s = GU + i
                        pe.wait_ge(lo_done, q * UNIT + (n0 + s + 1))
                        pe.wait_ge(ehid_done, q * GU + (f[-1] + 1))
                        w = [x[:, s % RING, 0:len(f) * D].rearrange("p (k c) -> p k c", c=D) for x in (whi, wlo)]
                        for c, kf in enumerate(f):
                            for m in range(2):
                                mm = mm3(ps[:, 4 + m, :], [y[:, kf, :] for y in (ehh, ehl)],
                                         [y[:, c, m * 512:(m + 1) * 512] for y in w], kf == 0, kf == KF - 1)
                        mm.then_inc(mm_done, 1)
                for s in SCATTER:
                    scatter(s, n_tasks)

            def units():
                n0 = UNITS_AT[0]
                pe.wait_ge(h_ready, 4)
                pe.wait_ge(out_evac, 4)
                with pe.Fori(0, N_HALF) as u:
                    for s in range(GU):
                        pe.wait_ge(lo_done, u * UNIT + (n0 + s + 1))
                        if s < 2:
                            pe.wait_ge(unit_done, u * 4 + (s + 1))
                        else:
                            pe.wait_ge(hid_done, u * GU + (s - 1))
                        w = [x[:, s % RING, :].rearrange("p (w k c) -> p w k c", w=2, k=KD) for x in (whi, wlo)]
                        for j in range(2):
                            for k in range(KD):
                                mm = mm3(ps[:, 2 * (s % 2) + j, 0:T], [y[:, j, k, :] for y in w],
                                         [y[:, k, :] for y in (hhi, hlo)], k == 0, k == KD - 1)
                        mm.then_inc(mm_done, 1)
                    pe.wait_ge(unit_done, u * 4 + 4)
                    pe.wait_ge(hid_done, u * GU + GU)
                    for i, f in enumerate(DOWN):
                        s = GU + i
                        pe.wait_ge(lo_done, u * UNIT + (n0 + s + 1))
                        w = [x[:, s % RING, 0:len(f) * D].rearrange("p (k c) -> p k c", c=D) for x in (whi, wlo)]
                        for c, kf in enumerate(f):
                            for m in range(KD):
                                mm = mm3(ps[:, m, 0:T], [y[:, c, m * P:(m + 1) * P] for y in w],
                                         [y[:, kf, :] for y in (hidhi, hidlo)], kf == 0, kf == KF - 1)
                        mm.then_inc(mm_done, 1)

            pe.wait_ge(init_in, 16 * n_init)
            for l in range(DEPTH):
                mm = pe.transpose(ps[:, 6, l * P:l * P + R_END], vrows[0:R_END, l, :], ident[0:R_END, 0:R_END])
            mm.then_inc(v_tr, 1)
            for k in range(KD):
                for b in range(BLK):
                    mm = pe.transpose(ps[:, 2 * b + k // 4, k % 4 * P:(k % 4 + 1) * P], xtok[:, b, k * P:(k + 1) * P], ident)
            mm.then_inc(x_tr, 1)
            pe.wait_ge(silc_ready, 1)
            for i in range(ADA_SLOTS[0]):
                ada_product(0, i)
            ada_end(0)
            pe.wait_ge(ones_set, 1)
            for l in range(DEPTH):
                sum_squares(2 * l)
                input_projection(l)
                pooling(l)
                branch(l, 0)
                attention(l, 0)
                branch(l, 1)
                attention(l, 1)
                branch(l, 2)
                out_projection(l)
                sum_squares(2 * l + 1)
                if l == 0:
                    units()
                else:
                    router()
                    experts()
            sum_squares(2 * DEPTH)
            pe.wait_ge(chain_m, 4 * 2 * DEPTH + KD)
            for b in range(BLK):
                for k in range(KD):
                    mm = pe.transpose(ps[:, 2 * b + k // 4, (k % 4) * P:(k % 4 + 1) * P],
                                      macc[:, k, b * P:(b + 1) * P], ident)
                mm.then_inc(y_tr, 1)

        @block.scalar
        def _(act):
            copy = ACT.Copy

            def hi(n):
                raw_wait(act, n)
                if n >= RING:
                    act.wait_ge(mm_done, n - RING + 1)
                act.activation(whi[:, n % RING, :], raw[:, n % RING, :], copy).then_inc(hi_done, 1)

            def ada_turned_copy(a):
                l, c = divmod(a, N_ADA // 2)
                return act.activation(mods4[:, l, 2 * c:2 * c + 2, :].rearrange("p c v -> p (c v)"), ps[:, 7, 256:264], copy)

            def ada_evac(phase, i):
                act.wait_ge(mm_done, ada_slot(phase, i) + 1)
                if i:
                    ada_turned_copy(ADA_AT[phase] + i - 1)
                act.activation(adarow[0:4, :], ps[0:4, 7, 0:256], copy).then_inc(ada_row, 1)

            def ada_end(phase):
                act.wait_ge(ada_turned, phase + 1)
                ada_turned_copy(ADA_AT[phase + 1] - 1).then_inc(ada_read, 1)

            def square(i, halves=(0, 1)):
                for half in halves:
                    k = slice(4 * half, 4 * half + 4)
                    act.activation(macc[:, k, :], xT[:, k, :], ACT.Square).then_inc(sq_done, 1)

            def root(i):
                act.wait_ge(ssq_done, i + 1)
                act.activation(rstd[:, :], ps[:, 6, 0:T], ACT.Sqrt, scale=1.0 / D, bias=epsc[:, 0:1]).then_inc(rms_done, 1)

            def modulate(i):
                l, which = i // 2, i % 2
                sh = (SH1, SH2)[which]
                for half in range(2):
                    act.wait_ge(xn_done, 2 * i + half + 1)
                    k = 4 * half
                    for v, t in ((0, slice(P, T)), (1, slice(0, P))):
                        act.activation(macc[:, k, t], macc[:, k, t], ACT.Identity,
                                       scale=amul[:, l, which, k, v:v + 1],
                                       bias=mods[:, l, sh + k, v:v + 1]).then_inc(chain_m, 1)
                    act.wait_ge(chain_m, 4 * i + 2 * half + 2)
                    act.wait_ge(mod_done, 2 * i + half + 1)
                    if i < 3:
                        k = slice(4 * half, 4 * half + 4)
                        act.activation(hhi[:, k, :], macc[:, k, :], copy).then_inc(hf_done, 1)

            def input_evac(l, s):
                act.wait_ge(mm_done, BASE[l] + s + 1)
                g = s % 2
                src = ps[:, 2 * g:2 * g + 2, :].rearrange("p a c -> p (a c)")[:, 0:BLK * 256].rearrange(
                    "p (b c) -> p b c", b=BLK)
                kv = KV_SLOTS.index(s) if s in KV_SLOTS else None
                if s in STAGED:
                    ti = STAGED.index(s)
                    if ti >= 2:
                        act.wait_ge(tr_done, N_TR * l + ti - 1)
                    if ti == 4:
                        act.wait_ge(kv_out, 16 * (6 * l + 4))
                    if ti == 0 and l:
                        act.wait_ge(kv_out, 16 * 6 * l)
                    act.activation(stage[:, ti % 2], src, copy).then_inc(win_evac, 1)
                    if s == 10:
                        act.activation(vtok[:, :, 512:640], src[:, :, P:256], copy).then_inc(win_evac, 1)
                elif s < 6:
                    act.activation(vtok[:, :, (s - 4) * 256:(s - 3) * 256], src, copy).then_inc(win_evac, 1)
                else:
                    act.activation(utok[:, :, (s - 6) * 256:(s - 5) * 256], src, copy).then_inc(win_evac, 1)
                ev = WIN_INC * l + s + 1 + (s == 10)
                if kv is not None:
                    act.wait_ge(win_evac, ev)
                if s in (2, 3):
                    act.dma_start(new_dk[0, l].rearrange("t h m d -> t (h m d)")[:, (s - 2) * 256:(s - 1) * 256],
                                  stage[:, STAGED.index(s) % 2, 0, :]).then_inc(kv_out, 16)
                if s in (4, 5):
                    act.dma_start(new_dv[0, l].rearrange("t h e -> t (h e)")[:, (s - 4) * 256:(s - 3) * 256],
                                  vtok[:, 0, (s - 4) * 256:(s - 3) * 256]).then_inc(kv_out, 16)
                if s == 10:
                    act.dma_start(new_wk[0, l].rearrange("t g d -> t (g d)"), stage[:, 0, 0, 0:P]).then_inc(kv_out, 16)
                    act.dma_start(new_wv[0, l].rearrange("t g d -> t (g d)"), vtok[:, 0, 512:640]).then_inc(kv_out, 16)

            def turned_evac(l, ti):
                act.wait_ge(tr_done, N_TR * l + ti + 1)
                src = ps[:, 4:6, 0:T]
                if ti < 2:
                    act.activation(qTA[:, 2 * ti:2 * ti + 2, :], src, copy, scale=DHA ** -0.5).then_inc(tr_evac, 1)
                elif ti < 4:
                    act.activation(kTA[:, 2 * ti - 4:2 * ti - 2, 0:T], src, copy).then_inc(tr_evac, 1)
                elif ti < 6:
                    act.activation(qTC[:, 2 * ti - 8:2 * ti - 6, :], src, copy, scale=DHC ** -0.5).then_inc(tr_evac, 1)
                elif ti == 6:
                    act.activation(kTC[:, :, 0:T], src, copy).then_inc(tr_evac, 1)
                else:
                    act.activation(kTA[:, :, T:512], ps[:, 4, :].rearrange("p (h c) -> p h c", h=4), copy)
                    act.activation(kTC[:, :, T:512], ps[:, 5, 0:256].rearrange("p (h c) -> p h c", h=2),
                                   copy).then_inc(tr_evac, 1)

            def pooling(l):
                act.wait_ge(pool_mm, l + 1)
                act.activation(pooled[:, :, :], ps[:, 0:4, 0:T], copy).then_inc(pool_ev, 1)
                act.wait_ge(pooly_mm, l + 1)
                for g in range(4):
                    x = act.activation(oraw[:, g, :], ps[:, 4 + g, 0:T], copy, scale=cols[:, l, R_PS + g:R_PS + g + 1])
                    x.then_inc(chain_p, 1)
                act.wait_ge(chain_p, 4 * (l + 1))
                act.activation(ohi[:, :, :], oraw[:, :, :], copy).then_inc(oh_done, 1)

            def attention(l, kind):
                st0, it0, per, phase = 24 * l + 12 * kind, 36 * l + 12 * kind, 1 + kind, 1 + 2 * l + kind

                def exps(t):
                    p, nk = t % 2, (P if t % 3 == 0 else T)
                    act.wait_ge(nmax_done, st0 + t + 1)
                    if t >= 2:
                        act.wait_ge(tp_done, it0 + per * (t - 1))
                    for m in range(2):
                        x = act.activation(ebuf[:, p, m, 0:nk], ps[:, 2 * p + m, 0:nk], ACT.Exp,
                                           bias=small[:, p, m:m + 1], accum_out=small[:, p, 2 + m:3 + m])
                    if kind == 1:
                        x = act.activation(small[:, p, 6:8], small[:, p, 4:6], ACT.Exp)
                    x.then_inc(e_done, 1)

                def pt_copy(i):
                    act.wait_ge(tp_done, it0 + i + 1)
                    n = it0 + i
                    if n >= 2:
                        act.wait_ge(pv_done, n - 1)
                    nk = P if (i // per) % 3 == 0 else T
                    act.activation(pt[:, n % 2, 0:nk], ps[:, 4 + n % 2, 0:nk], copy).then_inc(pt_evac, 1)

                def o_copy(h):
                    act.wait_ge(pv_done, it0 + 3 * per * (h + 1))
                    act.activation(oraw[:, h, :], ps[:, 6, 0:T], copy).then_inc(o_evac, 1)

                if kind == 0:
                    act.wait_ge(kv_out, 16 * 6 * (l + 1))
                    act.wait_ge(o_ready, 3 * l + 1)
                else:
                    act.wait_ge(o_ready, 3 * l + 2)
                exps(0)
                for t in range(12):
                    if t + 1 < 12:
                        exps(t + 1)
                    if t < ADA_SLOTS[phase] and kind == 0:
                        hi(ada_slot(phase, t) + 2)
                    for m in range(per):
                        pt_copy(per * t + m)
                    if t < ADA_SLOTS[phase]:
                        ada_evac(phase, t)
                    if t % 3 == 0 and t >= 3:
                        o_copy(t // 3 - 1)
                    if t < ADA_SLOTS[phase] and kind == 1:
                        hi(ada_slot(phase, t) + 2)
                o_copy(3)
                ada_end(phase)
                act.wait_ge(o_evac, 8 * l + 4 * kind + 4)
                if kind == 0:
                    act.activation(osq[:, :, :], oraw[:, :, :], ACT.Square).then_inc(osq_done, 1)
                    act.wait_ge(oss_done, l + 1)
                    act.activation(osq[:, :, :], ps[:, 4:8, 0:T], ACT.Sqrt, scale=1.0 / P, bias=epsc[:, 0:1]).then_inc(orms_done, 1)
                    act.wait_ge(on_done, l + 1)
                act.wait_ge(mm_done, branch_slot(l, kind, 1) + 1)
                act.activation(ohi[:, :, :], oraw[:, :, :], copy).then_inc(oh_done, 1)

            def gate_out(l, o, half, j):
                n = gate_slot(l, o, half, j)
                act.wait_ge(mm_done, n + 1)
                i = 6 * l + 2 * o + half
                if i:
                    act.wait_ge(merge_done, i)
                act.activation(gbuf[:, 2 * j:2 * j + 2, :], pair(n % 2), ACT.Sigmoid).then_inc(gate_evac, 1)

            def units():
                n0 = UNITS_AT[0]
                with act.Fori(0, N_HALF) as u:
                    def unit_hi(s):
                        act.wait_ge(raw_in[s % RING], u * (32 * UNIT // RING) + 32 * ((n0 + s) // RING + 1))
                        act.wait_ge(mm_done, u * UNIT + (n0 + s - RING + 1))
                        used = len(DOWN[s - GU]) * D if GU <= s < UNIT else SLOT
                        act.activation(whi[:, s % RING, 0:used], raw[:, s % RING, 0:used], copy).then_inc(hi_done, 1)

                    for s in range(UNIT):
                        unit_hi(s + 2)
                        if s < GU:
                            act.wait_ge(mm_done, u * UNIT + (n0 + s + 1))
                            if s >= 2:
                                act.wait_ge(hid_done, u * GU + (s - 1))
                            act.activation(sil[:, s % 2, :], ps[:, 2 * (s % 2), 0:T], ACT.Silu).then_inc(sil_done, 1)

            def y_high(q):
                act.wait_ge(mm_done, q * UNIT + (UNITS_AT[1]))
                act.activation(yhi[:, :], ps[:, 4:6, :].rearrange("p a c -> p (a c)"), copy, scale=gws[:, 0:1]
                               ).then_inc(yh_done, 1)

            def gathered(n):
                act.wait_ge(gather_done, n)
                act.activation(xgh[:, :, :].rearrange("p k c -> p (k c)"), ps[:, 2:4, :].rearrange("p a c -> p (a c)"), copy
                               ).then_inc(xgh_done, 1)

            def hidden_high(s, q):
                act.wait_ge(ht_done, q * GU + (s + 1))
                act.activation(ehh[:, s, :], ps[:, 6 + s % 2, 0:P], copy).then_inc(ehh_done, 1)

            def experts():
                n0 = UNITS_AT[1]
                act.wait_ge(pos_ready, 1)
                n_tasks = act.value_load(tasks[0:1, NQ:NQ + 1], min_val=N_EXP, max_val=MAX_TASKS)
                act.wait_ge(exp_init, 1)
                gathered(1)
                with act.Fori(0, n_tasks) as q:
                    for s in range(UNIT):
                        n = s + 2
                        act.wait_ge(raw_in[n % RING], q * (32 * UNIT // RING) + 32 * ((n0 + n) // RING + 1))
                        act.wait_ge(mm_done, q * UNIT + (n0 + n - RING + 1))
                        used = len(DOWN[n - GU]) * D if GU <= n < UNIT else SLOT
                        act.activation(whi[:, n % RING, 0:used], raw[:, n % RING, 0:used], copy).then_inc(hi_done, 1)
                        if s < GU:
                            act.wait_ge(mm_done, q * UNIT + (n0 + s + 1))
                            if s >= 2:
                                act.wait_ge(val_done, q * GU + (s - 1))
                            act.activation(esil[:, s % 2, :], ps[:, s % 2, 0:P], ACT.Silu).then_inc(esil_done, 1)
                            if s:
                                hidden_high(s - 1, q)
                        if s == 1:
                            y_high(q)
                        if s == 9:
                            act.wait_ge(st_done, q + 1)
                            act.activation(gws[:, :], ps[:, 2, T:T + 1], copy)
                            act.activation(sct[:, :], ps[:, 2, 0:T], copy).then_inc(sct_ready, 1)
                        if s == GU:
                            gathered(q + 2)
                            hidden_high(GU - 1, q)
                y_high(n_tasks)
                act.wait_ge(raw_in[2], n_tasks * (UNIT // RING * 32) + 32 * (n0 // RING + 1))
                act.wait_ge(sc_evac, n_tasks * 8 + 8)

            act.wait_ge(v_tr, 1)
            act.activation(cols[:, :, :], ps[:, 6, 0:256].rearrange("p (l c) -> p l c", l=2)[:, :, 0:R_END],
                           copy).then_inc(v_ev, 1)
            act.wait_ge(v_ev, 1)
            act.activation(silc[:, :, :], cols[:, 0, R_C:R_FIN].rearrange("p (v k) -> p v k", v=2),
                           ACT.Silu).then_inc(silc_done, 1)
            act.wait_ge(silc_done, 1)
            act.activation(sil4[:, :, 0:2], silc[:, :, :].rearrange("p v k -> p k v"), copy).then_inc(silh_done, 1)
            act.wait_ge(lam_sums, 1)
            act.activation(lamp[:, :, :], lamp[:, :, :], ACT.Exp).then_inc(v_ev, 1)
            hi(0)
            hi(1)
            for i in range(ADA_SLOTS[0]):
                hi(i + 2)
                ada_evac(0, i)
                if i == 0:
                    act.wait_ge(x_tr, 1)
                    for b in range(BLK):
                        act.activation(xT[:, :, b * P:(b + 1) * P],
                                       ps[:, 2 * b:2 * b + 2, :].rearrange("p a (k t) -> p (a k) t", t=P), copy).then_inc(x_ev, 1)
            ada_end(0)
            act.wait_ge(x_ev, BLK)
            for l in range(DEPTH):
                b0 = BASE[l]
                if l:
                    act.wait_ge(unit_done, 4 + 4 * N_HALF)
                square(2 * l)
                root(2 * l)
                modulate(2 * l)
                for s in range(N_WIN):
                    hi(b0 + s + 2)
                    input_evac(l, s)
                    if s - 1 in STAGED:
                        turned_evac(l, STAGED.index(s - 1))
                turned_evac(l, 6)
                turned_evac(l, 7)
                pooling(l)
                for o in range(3):
                    if o:
                        attention(l, o - 1)
                    for half in range(2):
                        for j in range(2):
                            n = gate_slot(l, o, half, j)
                            hi(n + 2)
                            gate_out(l, o, half, j)
                        hi(branch_slot(l, o, half) + 2)
                for half in range(2):
                    k = slice(4 * half, 4 * half + 4)
                    act.wait_ge(mm_done, gate_slot(l, 2, 1, 1) + 1)
                    act.wait_ge(merge_done, 6 * l + 5 + half)
                    act.activation(hhi[:, k, :], macc[:, k, :], copy).then_inc(mh_done, 1)
                for j in range(4):
                    hi(out_slot(l, j + 2))
                for half in range(2):
                    act.wait_ge(out_evac, 4 * l + 2 * half + 2)
                    square(2 * l + 1, (half,))
                root(2 * l + 1)
                modulate(2 * l + 1)
                if l == 0:
                    units()
                else:
                    act.wait_ge(h2_tr, 1)
                    act.activation(htok[0].rearrange("p b d -> p (b d)"), ps[:, 0:6, :].rearrange("p a c -> p (a c)"), copy
                                   ).then_inc(h2_hi, 1)
                    act.wait_ge(rt_sub, 1)
                    act.activation(rsm[:, :, 8:16], rsm[:, :, 8:16], ACT.Exp).then_inc(rt_exp, 1)
                    experts()
            square(2 * DEPTH)
            root(2 * DEPTH)
            act.wait_ge(xn_done, 4 * DEPTH + 2)
            for k in range(KD):
                act.activation(macc[:, k, :], macc[:, k, :], copy, scale=cols[:, 0, R_FIN + k:R_FIN + k + 1]
                               ).then_inc(chain_m, 1)
            for b in range(BLK):
                act.wait_ge(y_tr, b + 1)
                act.activation(yout[:, b, :], ps[:, 2 * b:2 * b + 2, :].rearrange("p a c -> p (a c)"), copy
                               ).then_inc(y_ev, 1)
                act.wait_ge(y_ev, b + 1)
                dst = y_prompt[0] if b == 0 else y_sample[0, (b - 1) * P:b * P]
                act.dma_start(dst, yout[:, b, :]).then_inc(y_out, 16)
            act.wait_ge(y_out, 16 * BLK)
            act.wait_ge(kv_out, 16 * 6 * DEPTH)

        @block.vector
        def _(dve):
            count = [0]

            def link(ins):
                count[0] += 1
                ins.then_inc(chain_v, 1)
                dve.wait_ge(chain_v, count[0])

            def lo(n):
                dve.wait_ge(hi_done, n + 1)
                dve.tensor_tensor(wlo[:, n % RING, :], raw[:, n % RING, :], whi[:, n % RING, :].bitcast(F32),
                                  ALU.subtract).then_inc(lo_done, 1)

            def sum_half(i, half):
                dve.wait_ge(sq_done, 2 * i + half + 1)
                dve.tensor_reduce(ssum[:, half, :], macc[:, 4 * half:4 * half + 4, :].rearrange("p k t -> p t k"), X, ALU.add
                                  ).then_inc(sqs_done, 1)

            def normalise(i):
                dve.wait_ge(rms_done, i + 1)
                link(dve.reciprocal(rstd[:, :], rstd[:, :]))
                ks = [slice(4 * half, 4 * half + 4) for half in range(2)]
                l, which = i // 2, i % 2
                for half, ch in enumerate(ks):
                    dve.tensor_tensor(macc[:, ch, :], xT[:, ch, :], rstd[:, :].unsqueeze(1).to_broadcast([P, 4, T]),
                                      ALU.mult).then_inc(xn_done, 1)
                    if i == 2 * DEPTH:
                        continue
                    dve.wait_ge(xn_done, 2 * i + half + 1)
                    for k in range(4 * half + 1, 4 * half + 4):
                        for v, t in ((0, slice(P, T)), (1, slice(0, P))):
                            x = dve.tensor_scalar(macc[:, k, t], macc[:, k, t], amul[:, l, which, k, v:v + 1],
                                                  mods[:, l, (SH1, SH2)[which] + k, v:v + 1], ALU.mult, ALU.add)
                    x.then_inc(mod_done, 1)
                if i < 3:
                    for half, k in enumerate(ks):
                        dve.wait_ge(hf_done, 2 * i + half + 1)
                        dve.tensor_tensor(hlo[:, k, :], macc[:, k, :], hhi[:, k, :].bitcast(F32),
                                          ALU.subtract).then_inc(h_ready, 1)

            def modulations(l, c0, c1, norms, read):
                dve.wait_ge(ada_read, read)
                b = cols[:, l, R_BADA + c0:R_BADA + c1].unsqueeze(2).to_broadcast([P, c1 - c0, 2])
                m = mods[:, l, c0:c1]
                link(dve.tensor_tensor(m, mods4[:, l, c0:c1, 0:2], mods4[:, l, c0:c1, 2:4], ALU.add))
                link(dve.tensor_tensor(m, m, b, ALU.add))
                for which in norms:
                    sc, g = ((SC1, R_N1), (SC2, R_N2))[which]
                    link(dve.tensor_scalar(amul[:, l, which], mods[:, l, sc:sc + KD, :], 1.0, None, ALU.add))
                    link(dve.tensor_tensor(amul[:, l, which], amul[:, l, which],
                                           cols[:, l, g:g + KD].unsqueeze(2).to_broadcast([P, KD, 2]), ALU.mult))
                if 0 in norms:
                    lam_init = 0.8 - 0.6 * math.exp(-0.3 * l)
                    link(dve.tensor_scalar(subg[:, l:l + 1], cols[:, l, R_SUB:R_SUB + 1], 1.0 - lam_init, None, ALU.mult))

            def rotate(l, ti):
                s = STAGED[ti]
                dve.wait_ge(win_evac, WIN_INC * l + s + 1 + (s == 10))
                heads = 2 if s == 10 else 4
                for b in range(2):
                    x = stage[:, ti % 2, b + 1, 0:heads * 64].rearrange("p (h s f i) -> p h s f i", h=heads, s=2, f=2)
                    co, si = (rope[:, b, c, :].rearrange("p (s i) -> p s i", s=2).unsqueeze(1)
                              .to_broadcast([P, heads, 2, 16]) for c in range(2))
                    t1, t2 = (rope_t[:, i, 0:heads * 32].rearrange("p (h s i) -> p h s i", h=heads, s=2)
                              for i in range(2))
                    a1, a2 = x[:, :, :, 0, :], x[:, :, :, 1, :]
                    dve.tensor_tensor(t1, a2, si, ALU.mult)
                    link(dve.tensor_tensor(t2, a1, si, ALU.mult))
                    dve.tensor_tensor(a1, a1, co, ALU.mult)
                    link(dve.tensor_tensor(a2, a2, co, ALU.mult))
                    dve.tensor_tensor(a1, a1, t1, ALU.subtract)
                    x = dve.tensor_tensor(a2, a2, t2, ALU.add)
                    if b == 0 or ti == 6:
                        link(x)
                    else:
                        x.then_inc(rope_done, 1)
                        dve.wait_ge(rope_done, len(STAGED) * l + ti + 1)
                if ti == 6:
                    src = stage[:, ti % 2, :, 0:P]
                    for g in range(2):
                        for i in range(2):
                            x = dve.tensor_copy(kcd[:, :, g * P + i * 64:g * P + i * 64 + 64], src[:, :, g * 64:g * 64 + 64])
                            if g == 1 and i == 1:
                                x.then_inc(rope_done, 1)

            def attention(l, kind):
                st0, phase = 24 * l + 12 * kind, 1 + 2 * l + kind

                def maxima(t):
                    p, nk = t % 2, (P if t % 3 == 0 else T)
                    dve.wait_ge(s_done, st0 + t + 1)
                    x = dve.tensor_reduce(small[:, p, 0:2], ps[:, 2 * p:2 * p + 2, 0:nk], X, ALU.max, negate=True)
                    if kind == 1:
                        hp = t // 3
                        link(x)
                        link(dve.tensor_tensor(small[:, p, 0:2], small[:, p, 0:2], nsink[:, l, 2 * hp:2 * hp + 2], ALU.min))
                        x = dve.tensor_tensor(small[:, p, 4:6], small[:, p, 0:2], sinkr[:, l, 2 * hp:2 * hp + 2], ALU.add)
                    x.then_inc(nmax_done, 1)

                def normal(t):
                    p, nk = t % 2, (P if t % 3 == 0 else T)
                    dve.wait_ge(e_done, st0 + t + 1)
                    e = [ebuf[:, p, m, 0:nk] for m in range(2)]
                    if kind == 1:
                        link(dve.tensor_tensor(small[:, p, 2:4], small[:, p, 2:4], small[:, p, 6:8], ALU.add))
                    link(dve.reciprocal(small[:, p, 8:10], small[:, p, 2:4]))
                    if kind == 0:
                        link(dve.tensor_scalar(small[:, p, 9:10], small[:, p, 9:10], neglam[:, l:l + 1], None, ALU.mult))
                        link(dve.tensor_scalar(e[0], e[0], small[:, p, 8:9], None, ALU.mult))
                        dve.scalar_tensor_tensor(e[0], e[1], small[:, p, 9:10], e[0], ALU.mult, ALU.add).then_inc(p_done, 1)
                    else:
                        dve.tensor_scalar(e[0], e[0], small[:, p, 8:9], None, ALU.mult)
                        dve.tensor_scalar(e[1], e[1], small[:, p, 9:10], None, ALU.mult).then_inc(p_done, 1)

                maxima(0)
                for t in range(12):
                    normal(t)
                    if t + 1 < 12:
                        maxima(t + 1)
                    if 0 < t < ADA_SLOTS[phase]:
                        lo(ada_slot(phase, t) + 1)
                    if t == ADA_SLOTS[phase] - 1:
                        lo(ada_slot(phase, t) + 2)
                if kind == 0:
                    dve.wait_ge(orms_done, l + 1)
                    link(dve.reciprocal(osq[:, :, :], osq[:, :, :]))
                    dve.scalar_tensor_tensor(oraw[:, :, :].rearrange("p a b -> p (a b)"),
                                             oraw[:, :, :].rearrange("p a b -> p (a b)"), subg[:, l:l + 1],
                                             osq[:, :, :].rearrange("p a b -> p (a b)"), ALU.mult, ALU.mult
                                             ).then_inc(on_done, 1)

            def o_low(l, o):
                dve.wait_ge(oh_done, 3 * l + o + 1)
                dve.tensor_tensor(olo[:, :, :], oraw[:, :, :], ohi[:, :, :].bitcast(F32), ALU.subtract).then_inc(o_ready, 1)

            def merge(l, o, half):
                dve.wait_ge(mm_done, branch_slot(l, o, half) + 1)
                dve.wait_ge(gate_evac, 12 * l + 4 * o + 2 * half + 2)
                dst = macc[:, 4 * half:4 * half + 4, :]
                if o == 0:
                    dve.tensor_tensor(dst, gbuf[:, :, :], ps[:, 4:8, 0:T], ALU.mult).then_inc(merge_done, 1)
                else:
                    link(dve.tensor_tensor(gbuf[:, :, :], gbuf[:, :, :], ps[:, 4:8, 0:T], ALU.mult))
                    dve.tensor_tensor(dst, dst, gbuf[:, :, :], ALU.add).then_inc(merge_done, 1)

            def merged_low(l, half):
                k = slice(4 * half, 4 * half + 4)
                dve.wait_ge(mh_done, 2 * l + half + 1)
                dve.tensor_tensor(hlo[:, k, :], macc[:, k, :], hhi[:, k, :].bitcast(F32), ALU.subtract
                                  ).then_inc(merged_ready, 1)

            def residual(l, n, j):
                dve.wait_ge(mm_done, n + 1)
                for c in range(2):
                    m = 2 * j + c
                    for v, t in ((0, slice(P, T)), (1, slice(0, P))):
                        x = dve.scalar_tensor_tensor(xT[:, m, t], ps[:, 2 * (n % 2) + c, t], mods[:, l, G1 + m, v:v + 1],
                                                     xT[:, m, t], ALU.mult, ALU.add)
                x.then_inc(out_evac, 1)

            def router():
                dve.memset(gws[:, :], 0.0)
                dve.memset(sct[:, :].bitcast(F32), 0.0).then_inc(exp_init, 1)
                dve.wait_ge(rt_done, 1)
                lg, ex, sel = rsm[:, :, 8:16], rsm[:, :, 8:16], rsm[:, :, 0:8]
                link(dve.tensor_copy(lg, ps[:, 6, 0:BLK * 8].rearrange("p (b e) -> p b e", b=BLK)))
                mx = small[:, 0, 0:BLK]
                for b in range(BLK):
                    mine = lg[:, b, :].unsqueeze(2).to_broadcast([P, 8, 8])
                    other = lg[:, b, :].unsqueeze(1).to_broadcast([P, 8, 8])
                    gt = rcmp[:, 0, b, :].rearrange("p (e j) -> p e j", e=8)
                    eq = rcmp[:, 1, b, :].rearrange("p (e j) -> p e j", e=8)
                    dve.tensor_tensor(gt, other, mine, ALU.is_gt)
                    link(dve.tensor_tensor(eq, other, mine, ALU.is_equal))
                    link(dve.tensor_tensor(eq, eq, tri.rearrange("p (e j) -> p e j", e=8), ALU.mult))
                    link(dve.tensor_tensor(gt, gt, eq, ALU.add))
                    link(dve.tensor_reduce(sel[:, b, :], gt, X, ALU.add))
                dve.tensor_scalar(sel, sel, 1.5, None, ALU.is_lt).then_inc(sel_ready, 1)
                link(dve.tensor_reduce(mx, lg, X, ALU.max))
                dve.tensor_tensor(lg, lg, mx.unsqueeze(2).to_broadcast([P, BLK, 8]), ALU.subtract).then_inc(rt_sub, 1)
                dve.wait_ge(h2_hi, 1)
                dve.tensor_tensor(htok[1].rearrange("p b d -> p (b d)"), ps[:, 0:6, :].rearrange("p a c -> p (a c)"),
                                  htok[0].rearrange("p b d -> p (b d)").bitcast(F32), ALU.subtract).then_inc(h2_lo, 1)
                dve.wait_ge(rt_exp, 1)
                g8 = gwe[:, :, :]
                link(dve.tensor_tensor(g8, ex, sel, ALU.mult))
                link(dve.tensor_reduce(mx, g8, X, ALU.add))
                link(dve.reciprocal(mx, mx))
                link(dve.tensor_tensor(g8, g8, mx.unsqueeze(2).to_broadcast([P, BLK, 8]), ALU.mult))
                dve.wait_ge(pos_mm, 1)
                count, first, behind = tk[:, 0, 0:8], tk[:, 1, 0:8], tk[:, 2, 0:8]
                link(dve.tensor_scalar(tk[:, 3, 0:8], ps[:, 6, 24:32], P + 0.5, None, ALU.is_gt))
                link(dve.tensor_scalar(count, ps[:, 6, 24:32], 2 * P + 0.5, None, ALU.is_gt))
                link(dve.scalar_tensor_tensor(count, tk[:, 3, 0:8], 1.0, count, ALU.add, ALU.add))
                square8 = by_task[:, 0, 0:8, :]
                link(dve.tensor_tensor(square8, tri.rearrange("p (e j) -> p e j", e=8),
                                       count.unsqueeze(1).to_broadcast([P, 8, 8]), ALU.mult))
                link(dve.tensor_reduce(first, square8, X, ALU.add))
                link(dve.tensor_tensor(behind, first, count, ALU.add))
                index = slotc[:, P:P + NQ].unsqueeze(2).to_broadcast([P, NQ, 8])
                begun = by_task[:, 0]
                dve.tensor_tensor(begun, first.unsqueeze(1).to_broadcast([P, NQ, 8]), index, ALU.is_gt)
                link(dve.tensor_tensor(owner[:, :, :], behind.unsqueeze(1).to_broadcast([P, NQ, 8]), index, ALU.is_gt))
                link(dve.tensor_tensor(owner[:, :, :], owner[:, :, :], begun, ALU.subtract))
                base = tk[:, 4, :]
                dve.tensor_tensor(by_task[:, 0], owner[:, :, :], slotc[:, P:P + 8].unsqueeze(1).to_broadcast([P, NQ, 8]), ALU.mult)
                link(dve.tensor_tensor(by_task[:, 1], owner[:, :, :], first.unsqueeze(1).to_broadcast([P, NQ, 8]), ALU.mult))
                dve.tensor_reduce(tk[:, 5, :], by_task[:, 0], X, ALU.add)
                link(dve.tensor_reduce(base, by_task[:, 1], X, ALU.add))
                link(dve.tensor_tensor(base, slotc[:, P:P + NQ], base, ALU.subtract))
                link(dve.tensor_scalar(base, base, float(P), 1.0, ALU.mult, ALU.add))
                dve.tensor_copy(tasks[:, 0:NQ], tk[:, 5, :])
                dve.tensor_copy(tasks[:, NQ:NQ + 1], tk[:, 2, 7:8]).then_inc(pos_ready, 1)
                pos = ps[:, 6, 0:BLK * 8].rearrange("p (b e) -> p b e", b=BLK)
                link(dve.scalar_tensor_tensor(posx[:, :, :], pos, 1.0, sel, ALU.add, ALU.mult))
                for table, of_expert in ((posq, posx), (gwq, gwe)):
                    for b in range(BLK):
                        x = dve.tensor_tensor(by_task[:, b], owner[:, :, :], of_expert[:, b, :].unsqueeze(1).to_broadcast([P, NQ, 8]),
                                              ALU.mult)
                    link(x)
                    link(dve.tensor_reduce(table[:, :, :], by_task[:, :, :, :], X, ALU.add))
                    if table is posq:
                        link(dve.tensor_tensor(posq[:, :, :], posq[:, :, :], base.unsqueeze(1).to_broadcast([P, BLK, NQ]),
                                               ALU.subtract))
                        gather_matrix(lambda b: posq[:, b, 0:1])
                dve.wait_ge(gat_ready, 1)
                dve.memset(tk[:, 0, 0:1], 0.0).then_inc(gates_ready, 1)

            def gather_matrix(pos):
                for b in range(BLK):
                    x = dve.tensor_scalar(gat[:, b, :], slotc[:, P:2 * P], pos(b), None, ALU.is_equal)
                x.then_inc(gat_ready, 1)

            def y_low(q):
                dve.wait_ge(yh_done, q + 1)
                dve.scalar_tensor_tensor(ylo[:, :], ps[:, 4:6, :].rearrange("p a c -> p (a c)"), gws[:, 0:1],
                                         yhi[:, :].bitcast(F32), ALU.mult, ALU.subtract).then_inc(yl_done, 1)

            def scattered(s, q):
                for m in range(8):
                    if SCATTER[m // 2] == s:
                        dve.wait_ge(sc_done, 8 * q + (m + 1))
                        for v, t in ((0, slice(P, T)), (1, slice(0, P))):
                            x = dve.scalar_tensor_tensor(xT[:, m, t], ps[:, 2 + m % 2, t], mods[:, 1, G2 + m, v:v + 1],
                                                         xT[:, m, t], ALU.mult, ALU.add)
                        x.then_inc(sc_evac, 1)

            def gathered_low(n):
                dve.wait_ge(xgh_done, n)
                dve.tensor_tensor(xgl[:, :, :].rearrange("p k c -> p (k c)"), ps[:, 2:4, :].rearrange("p a c -> p (a c)"),
                                  xgh[:, :, :].rearrange("p k c -> p (k c)").bitcast(F32), ALU.subtract).then_inc(xg_ready, 1)

            def hidden_low(s, q):
                dve.wait_ge(ehh_done, q * GU + (s + 1))
                dve.tensor_tensor(ehl[:, s, :], ps[:, 6 + s % 2, 0:P], ehh[:, s, :].bitcast(F32), ALU.subtract
                                  ).then_inc(ehid_done, 1)

            def experts():
                n0 = UNITS_AT[1]
                n_tasks = dve.value_load(tasks[0:1, NQ:NQ + 1], min_val=N_EXP, max_val=MAX_TASKS)
                dve.memset(small[:, 0, 1:2], 0.0).then_inc(sct_ready, 1)
                gathered_low(1)
                with dve.Fori(0, n_tasks) as q:
                    for s in range(UNIT):
                        n = s + 2
                        used = len(DOWN[n - GU]) * D if GU <= n < UNIT else SLOT
                        dve.wait_ge(hi_done, q * UNIT + (n0 + n + 1))
                        dve.tensor_tensor(wlo[:, n % RING, 0:used], raw[:, n % RING, 0:used],
                                          whi[:, n % RING, 0:used].bitcast(F32), ALU.subtract).then_inc(lo_done, 1)
                        if s < GU:
                            dve.wait_ge(esil_done, q * GU + (s + 1))
                            if s >= 2:
                                dve.wait_ge(ht_done, q * GU + (s - 1))
                            dve.tensor_tensor(evalu[:, s % 2, :], esil[:, s % 2, :], ps[:, s % 2, P:2 * P],
                                              ALU.mult).then_inc(val_done, 1)
                            if s:
                                hidden_low(s - 1, q)
                        if s == 1:
                            y_low(q)
                        scattered(s, q)
                        if s == 8:
                            gather_matrix(lambda b: posq[:, b, bass.ds(q + 1, 1)])
                        if s == 7:
                            for b in range(BLK):
                                x = dve.tensor_scalar(gas[:, b, :], slotc[:, P:2 * P], posq[:, b, bass.ds(q, 1)], None,
                                                      ALU.is_equal)
                            x.then_inc(gas_ready, 1)
                        if s == GU:
                            gathered_low(q + 2)
                            hidden_low(GU - 1, q)
                y_low(n_tasks)
                for s in SCATTER:
                    scattered(s, n_tasks)

            def units():
                n0 = UNITS_AT[0]
                with dve.Fori(0, N_HALF) as u:
                    def unit_lo(s):
                        used = len(DOWN[s - GU]) * D if GU <= s < UNIT else SLOT
                        dve.wait_ge(hi_done, u * UNIT + (n0 + s + 1))
                        dve.tensor_tensor(wlo[:, s % RING, 0:used], raw[:, s % RING, 0:used],
                                          whi[:, s % RING, 0:used].bitcast(F32), ALU.subtract).then_inc(lo_done, 1)

                    for s in range(UNIT):
                        unit_lo(s + 2)
                        if s < GU:
                            dve.wait_ge(sil_done, u * GU + (s + 1))
                            dve.tensor_tensor(val[:, s % 2, :], sil[:, s % 2, :], ps[:, 2 * (s % 2) + 1, 0:T], ALU.mult
                                              ).then_inc(chain_u, 1)
                            dve.wait_ge(chain_u, u * (2 * GU) + (2 * s + 1))
                            dve.tensor_copy(hidhi[:, s, :], val[:, s % 2, :]).then_inc(chain_u, 1)
                            dve.wait_ge(chain_u, u * (2 * GU) + (2 * s + 2))
                            dve.tensor_tensor(hidlo[:, s, :], val[:, s % 2, :], hidhi[:, s, :].bitcast(F32),
                                              ALU.subtract).then_inc(hid_done, 1)
                    dve.wait_ge(mm_done, u * UNIT + (n0 + UNIT))
                    for m in range(KD):
                        for v, t in ((0, slice(P, T)), (1, slice(0, P))):
                            x = dve.scalar_tensor_tensor(xT[:, m, t], ps[:, m, t], mods[:, 0, G2 + m, v:v + 1], xT[:, m, t],
                                                         ALU.mult, ALU.add)
                        if m % 2:
                            x.then_inc(unit_done, 1)

            dve.memset(rope_t[:, :, :], 0.0).then_inc(unit_done, 4)
            dve.wait_ge(init_in, 16 * n_init)
            link(dve.tensor_tensor(lamprod[:, :, :], lamrow[:, :, 0, :], lamrow[:, :, 1, :], ALU.mult))
            link(dve.tensor_reduce(lamp[:, :, :].rearrange("p l i -> p (l i)"), lamprod[:, :, :], X, ALU.add))
            dve.tensor_scalar(nsink[:, :, :], sinkr[:, :, :], -1.0, None, ALU.mult).then_inc(lam_sums, 1)
            dve.wait_ge(v_ev, 2)
            link(dve.tensor_tensor(neglam[:, :], lamp[:, :, 1], lamp[:, :, 0], ALU.subtract))
            for l in range(DEPTH):
                dve.tensor_scalar(neglam[:, l:l + 1], neglam[:, l:l + 1], -(0.8 - 0.6 * math.exp(-0.3 * l)), None,
                                  ALU.add).then_inc(lam_done, 1)
            dve.wait_ge(lam_done, DEPTH)
            dve.wait_ge(silh_done, 1)
            dve.tensor_tensor(sil4[:, :, 2:4], silc[:, :, :].rearrange("p v k -> p k v"), sil4[:, :, 0:2].bitcast(F32),
                              ALU.subtract).then_inc(silc_ready, 1)
            for n in range(ADA_SLOTS[0] + 2):
                lo(n)
            modulations(0, 0, 2 * KD, (0,), 1)
            for l in range(DEPTH):
                b0 = BASE[l]
                for half in range(2):
                    sum_half(2 * l, half)
                normalise(2 * l)
                for s in range(N_WIN):
                    lo(b0 + s + 2)
                    if s in STAGED:
                        rotate(l, STAGED.index(s))
                o_low(l, 0)
                for o in range(3):
                    if o:
                        attention(l, o - 1)
                        o_low(l, o)
                    for half in range(2):
                        for j in range(2):
                            lo(gate_slot(l, o, half, j) + 2)
                        lo(branch_slot(l, o, half) + 2)
                        if o == 2 and half == 1:
                            modulations(l, 2 * KD, N_ADA, (1,), 3 + 2 * l)
                            merged_low(l, 0)
                        merge(l, o, half)
                merged_low(l, 1)
                for j in range(4):
                    lo(out_slot(l, j + 2))
                    if j == 3:
                        sum_half(2 * l + 1, 0)
                    residual(l, out_slot(l, j), j)
                sum_half(2 * l + 1, 1)
                if l == 0:
                    modulations(1, 0, 2 * KD, (0,), 3)
                normalise(2 * l + 1)
                if l == 0:
                    units()
                else:
                    router()
                    experts()
            for half in range(2):
                sum_half(2 * DEPTH, half)
            normalise(2 * DEPTH)


_INS = ["x_prompt", "x_sample", "cache_diff_k", "cache_diff_v", "cache_win_k", "cache_win_v", "c", "c_ctx",
        "w_ada", "b_ada", "norm1_g", "norm2_g", "w_in", "w_gate", "lam_p", "subln_g", "w_pool", "pool_scale",
        "sink", "w_branch", "w_out", "w_ff_gate", "w_ff_up", "w_ff_down", "w_router", "w_ex_gate", "w_ex_up",
        "w_ex_down", "final_g"]
_OUTS = [(1, 128, 1024), (1, 256, 1024), (1, 2, 128, 4, 2, 64), (1, 2, 128, 4, 128), (1, 2, 128, 2, 64),
         (1, 2, 128, 2, 64)]


def kernel(**inputs):
    import concourse.bacc as _bacc
    from concourse.bass_utils import run_bass_kernel_spmd as _run

    nc = _bacc.Bacc("TRN2", target_bir_lowering=False, num_devices=1)
    arrays, args = {}, {}
    for name in _INS:
        x = np.ascontiguousarray(inputs[name])
        arrays[f"in_{name}_dram"] = x
        args[name] = nc.dram_tensor(f"in_{name}_dram", x.shape, mybir.dt.from_np(x.dtype), kind="ExternalInput").ap()
    const = shape_constants()
    arrays["shape_constants_dram"] = const
    cap = nc.dram_tensor("shape_constants_dram", const.shape, F32, kind="ExternalInput").ap()
    outs = [nc.dram_tensor(f"out_{i}_dram", s, F32, kind="ExternalOutput").ap() for i, s in enumerate(_OUTS)]
    prefix_step_kernel(nc, args, outs, cap)
    r = _run(nc, [arrays], core_ids=[0])
    return tuple(r.results[0][f"out_{i}_dram"] for i in range(len(_OUTS)))
```
